# Optimizing a Trainium2 kernel written in Bass

```python
import math
import jax
import jax.numpy as jnp
from jax import lax
import numpy as np

D_MODEL = 1024
BATCH = 1
SEQ = 512
DEPTH = 2
DEC_BATCH = 8
DEC_SEQ = 1
PAST_LEN = 256
PAGE_SIZE = 128

HEAD_DIM = 64
NSA_HEADS = 8
NSA_KV = 2
NSA_GROUP = NSA_HEADS // NSA_KV
CMP_LEN = 32
CMP_STRIDE = 16
CMP_HIDDEN = 128
SLC_BLOCK = 64
N_SEL = 16
WINDOW = 512
Q_BLOCK = 128
DN_HEADS = 4
DN_DK = 128
DN_DV = 128
DN_CHUNK = 64
CONV_W = 4
HG_HEADS = 4
HG_DK = 128
HG_DV = 128
HG_CHUNK = 16
D_FF = 2816
NORM_EPS = 1e-6
L2_EPS = 1e-6
NEG_BIG = -1e30
SEL_BIG = 1e9

NSA_W = NSA_HEADS * HEAD_DIM
KV_W = NSA_KV * HEAD_DIM
DN_QK = DN_HEADS * DN_DK
DN_V = DN_HEADS * DN_DV
DN_QKV = 2 * DN_QK + DN_V
HG_WK = HG_HEADS * HG_DK
HG_WV = HG_HEADS * HG_DV
MIX_W = NSA_W + DN_V + HG_WV
IN_SPLITS = (NSA_W, 6 * KV_W, 3 * NSA_HEADS, DN_QKV, DN_HEADS, DN_HEADS, DN_V, HG_WK, HG_WV, HG_WK, HG_WV, 3 * D_MODEL)
IN_COLS = sum(IN_SPLITS)

kernel_name = 'nsa_deltanet_hgrn2_hybrid_step'

def rms_norm(x, g):
    xf = x.astype(jnp.float32)
    y = xf * lax.rsqrt(jnp.mean(xf * xf, axis=-1, keepdims=True) + NORM_EPS)
    return (y * g.astype(jnp.float32)).astype(x.dtype)

def l2_normalize(x):
    xf = x.astype(jnp.float32)
    return xf * lax.rsqrt(jnp.sum(xf * xf, axis=-1, keepdims=True) + L2_EPS)

def swiglu(x, w_gu, w_down):
    g, u = jnp.split(x @ w_gu, 2, axis=-1)
    return (jax.nn.silu(g) * u) @ w_down

def alibi_slopes(n):
    return 2.0 ** (-8.0 * (jnp.arange(n, dtype=jnp.float32) + 1.0) / n)

def masked_softmax(s, mask):
    s = jnp.where(mask, s, NEG_BIG)
    m = jnp.max(s, axis=-1, keepdims=True)
    e = jnp.where(mask, jnp.exp(s - m), 0.0)
    return e / jnp.maximum(jnp.sum(e, axis=-1, keepdims=True), 1e-30)

def masked_exp(diff, mask):
    return jnp.where(mask, jnp.exp(jnp.where(mask, diff, 0.0)), 0.0)

def split_in(z):
    offs = [int(o) for o in np.cumsum(IN_SPLITS)[:-1]]
    return jnp.split(z, offs, axis=-1)

def gather_pages(pool, page_table):
    rows = pool[page_table]
    return rows.reshape(rows.shape[0], rows.shape[1] * rows.shape[2], *rows.shape[3:])

def nsa_compress(rows, pe, w1, w2, k_gain):
    B, T = rows.shape[:2]
    pad = (-T) % CMP_STRIDE
    rows = jnp.pad(rows, ((0, 0), (0, pad), (0, 0), (0, 0), (0, 0)))
    n_chunk = (T + pad) // CMP_STRIDE
    ch = rows.reshape(B, n_chunk, CMP_STRIDE, 2, NSA_KV, HEAD_DIM)
    n_part = CMP_LEN // CMP_STRIDE
    n_blk = n_chunk - n_part + 1
    hid = 0.0
    for m in range(n_part):
        pe_m = pe[:, m * CMP_STRIDE:(m + 1) * CMP_STRIDE].transpose(1, 0, 2)[:, :, None, :]
        w1_m = w1[:, m * CMP_STRIDE:(m + 1) * CMP_STRIDE]
        hid = hid + jnp.einsum('bcrkgd,krdh->bckgh', ch + pe_m, w1_m)[:, m:m + n_blk]
    comp = jnp.einsum('bnkgh,khd->bnkgd', jax.nn.silu(hid), w2)
    ck = rms_norm(comp[:, :, 0], k_gain)
    cv = comp[:, :, 1]
    c_end = jnp.arange(n_blk) * CMP_STRIDE + CMP_LEN - 1
    return ck, cv, c_end

def nsa_attend(q, gates, q_pos, ck, cv, c_end, sk, sv, wk, wv, w_pos, slopes):
    B, Tq = q.shape[:2]
    f32 = jnp.float32
    qg = q.reshape(B, Tq, NSA_KV, NSA_GROUP, HEAD_DIM)
    m_h = slopes.reshape(NSA_KV, NSA_GROUP)[:, :, None]
    dist_c = q_pos[:, None] - c_end[None, :]
    s = jnp.einsum('btgjd,bngd->btgjn', qg, ck).astype(f32)
    s = s - m_h * jnp.abs(dist_c)[:, None, None, :].astype(f32)
    p_cmp = masked_softmax(s, (dist_c >= 0)[:, None, None, :])
    o_cmp = jnp.einsum('btgjn,bngd->btgjd', p_cmp.astype(cv.dtype), cv)
    NB = sk.shape[2]
    ci = jnp.arange(ck.shape[1])[:, None] * CMP_STRIDE
    bj = jnp.arange(NB)
    overlap = ((ci < (bj + 1) * SLC_BLOCK) & (ci + CMP_LEN > bj * SLC_BLOCK)).astype(f32)
    imp = jnp.einsum('btgjn,nm->btgm', p_cmp, overlap)
    cur = (q_pos // SLC_BLOCK)[:, None]
    causal_blk = (bj * SLC_BLOCK)[None, :] <= q_pos[:, None]
    forced = (bj == 0)[None, :] | (bj[None, :] == cur) | (bj[None, :] == cur - 1)
    imp = jnp.where(forced[:, None, :], SEL_BIG, jnp.where(causal_blk[:, None, :], imp, -SEL_BIG))
    _, sel = lax.top_k(imp, min(N_SEL, NB))
    bi = jnp.arange(B)[:, None, None, None]
    gi = jnp.arange(NSA_KV)[None, None, :, None]
    k_sel = sk[bi, gi, sel]
    v_sel = sv[bi, gi, sel]
    pos = sel[..., None] * SLC_BLOCK + jnp.arange(SLC_BLOCK)
    dist_s = (q_pos[None, :, None, None, None] - pos).reshape(B, Tq, NSA_KV, 1, -1)
    s = jnp.einsum('btgjd,btgkld->btgjkl', qg, k_sel).astype(f32).reshape(B, Tq, NSA_KV, NSA_GROUP, -1)
    s = s - m_h * jnp.abs(dist_s).astype(f32)
    p = masked_softmax(s, dist_s >= 0)
    o_slc = jnp.einsum('btgjn,btgnd->btgjd', p.astype(v_sel.dtype), v_sel.reshape(B, Tq, NSA_KV, -1, HEAD_DIM))
    dist_w = q_pos[:, None] - w_pos[None, :]
    mask_w = (dist_w >= 0) & (dist_w < WINDOW) & (w_pos >= 0)[None, :]
    s = jnp.einsum('btgjd,bsgd->btgjs', qg, wk).astype(f32) - m_h * jnp.abs(dist_w)[:, None, None, :].astype(f32)
    p = masked_softmax(s, mask_w[:, None, None, :])
    o_win = jnp.einsum('btgjs,bsgd->btgjd', p.astype(wv.dtype), wv)
    g = gates.reshape(B, Tq, NSA_KV, NSA_GROUP, 3)
    o = g[..., 0:1] * o_cmp + g[..., 1:2] * o_slc + g[..., 2:3] * o_win
    return o.reshape(B, Tq, NSA_W)

def nsa_mixer(q, gates, cmp_rows, slc_rows, win_rows, q_pos0, win_pos0, pe, w1, w2, k_gain_cmp, blocked):
    B, T = q.shape[:2]
    slopes = alibi_slopes(NSA_HEADS)
    ck, cv, c_end = nsa_compress(cmp_rows, pe, w1, w2, k_gain_cmp)
    Tk = slc_rows.shape[1]
    pad = (-Tk) % SLC_BLOCK
    nb = (Tk + pad) // SLC_BLOCK
    blk = jnp.pad(slc_rows, ((0, 0), (0, pad), (0, 0), (0, 0), (0, 0))).reshape(B, nb, SLC_BLOCK, 2, NSA_KV, HEAD_DIM)
    sk = blk[:, :, :, 0].transpose(0, 3, 1, 2, 4)
    sv = blk[:, :, :, 1].transpose(0, 3, 1, 2, 4)
    if not blocked:
        Tw = win_rows.shape[1]
        return nsa_attend(q, gates, q_pos0 + jnp.arange(T), ck, cv, c_end, sk, sv,
                          win_rows[:, :, 0], win_rows[:, :, 1], win_pos0 + jnp.arange(Tw), slopes)
    win_p = jnp.pad(win_rows, ((0, 0), (WINDOW, 0), (0, 0), (0, 0), (0, 0)))

    def one_block(b0):
        qb = lax.dynamic_slice_in_dim(q, b0, Q_BLOCK, 1)
        gb = lax.dynamic_slice_in_dim(gates, b0, Q_BLOCK, 1)
        wb = lax.dynamic_slice_in_dim(win_p, b0, WINDOW + Q_BLOCK, 1)
        return nsa_attend(qb, gb, q_pos0 + b0 + jnp.arange(Q_BLOCK), ck, cv, c_end, sk, sv,
                          wb[:, :, 0], wb[:, :, 1], win_pos0 - WINDOW + b0 + jnp.arange(WINDOW + Q_BLOCK), slopes)

    out = lax.map(one_block, jnp.arange(T // Q_BLOCK) * Q_BLOCK)
    return out.transpose(1, 0, 2, 3).reshape(B, T, NSA_W)

def to_chunks(a, C):
    B, T = a.shape[:2]
    pad = (-T) % C
    a = jnp.pad(a, [(0, 0), (0, pad)] + [(0, 0)] * (a.ndim - 2))
    a = a.reshape(B, (T + pad) // C, C, *a.shape[2:])
    return a.transpose((1, 0, 3, 2) + tuple(range(4, a.ndim)))

def from_chunks(o, T):
    n, B, H, C, d = o.shape
    return o.transpose(1, 0, 3, 2, 4).reshape(B, n * C, H, d)[:, :T]

def causal_conv(x_new, buf, w):
    T = x_new.shape[1]
    xx = jnp.concatenate([buf.astype(x_new.dtype), x_new], axis=1)
    y = sum(xx[:, j:j + T] * w[j] for j in range(CONV_W))
    return y, xx[:, -(CONV_W - 1):]

def gated_delta_rule(q, k, v, g, beta, S0):
    T = q.shape[1]
    C = DN_CHUNK
    f32 = jnp.float32
    xs = tuple(to_chunks(a.astype(f32), C) for a in (q, k, v, g, beta))
    incl = jnp.tril(jnp.ones((C, C), bool))
    strict = jnp.tril(jnp.ones((C, C), bool), -1)
    eye = jnp.eye(C, dtype=f32)

    def step(S, inp):
        qc, kc, vc, gc, bc = inp
        gcum = jnp.cumsum(gc, axis=-1)
        decay = masked_exp(gcum[..., :, None] - gcum[..., None, :], incl)
        L = jnp.where(strict, bc[..., :, None] * jnp.einsum('bhid,bhjd->bhij', kc, kc) * decay, 0.0)
        Tinv = lax.linalg.triangular_solve(eye + L, jnp.broadcast_to(eye, L.shape), left_side=True, lower=True, unit_diagonal=True)
        u = Tinv @ (vc * bc[..., None])
        w = Tinv @ (kc * (bc * jnp.exp(gcum))[..., None])
        v_new = u - w @ S
        attn = jnp.einsum('bhid,bhjd->bhij', qc, kc) * decay
        o = (qc * jnp.exp(gcum)[..., None]) @ S + attn @ v_new
        g_last = gcum[..., -1:]
        S = S * jnp.exp(g_last)[..., None] + jnp.einsum('bhcd,bhce->bhde', kc * jnp.exp(g_last - gcum)[..., None], v_new)
        return S, o

    S, o = lax.scan(step, S0.astype(f32), xs)
    return from_chunks(o, T), S

def hgrn2_recurrence(q, k, v, logf, S0):
    T = q.shape[1]
    C = HG_CHUNK
    f32 = jnp.float32
    xs = tuple(to_chunks(a.astype(f32), C) for a in (q, k, v, logf))
    incl = jnp.tril(jnp.ones((C, C), bool))[:, :, None]

    def step(S, inp):
        qc, kc, vc, lc = inp
        G = jnp.cumsum(lc, axis=2)
        dec = masked_exp(G[:, :, :, None, :] - G[:, :, None, :, :], incl)
        A = jnp.einsum('bhtc,bhsc,bhtsc->bhts', qc, kc, dec)
        o = jnp.einsum('bhtc,bhcd->bhtd', qc * jnp.exp(G), S) + A @ vc
        G_last = G[:, :, -1:]
        S = S * jnp.exp(G_last[:, :, 0])[..., None] + jnp.einsum('bhsc,bhsd->bhcd', kc * jnp.exp(G_last - G), vc)
        return S, o

    S, o = lax.scan(step, S0.astype(f32), xs)
    return from_chunks(o, T), S

def hgrn_lower_bounds(logits):
    p = jax.nn.softmax(logits.astype(jnp.float32), axis=0)
    return jnp.cumsum(p, axis=0) - p[0]

def decoder_layer(x, l, prm, past, pos0, blocked):
    B, T, _ = x.shape
    f32 = jnp.float32
    x = x + 0.5 * swiglu(rms_norm(x, prm['ffn1_norm'][l]), prm['ffn1_w_gu'][l], prm['ffn1_w_down'][l])
    h = rms_norm(x, prm['mix_norm'][l])
    (a_q, a_kv, a_g, d_qkv, d_b, d_a, d_z, r_f, r_i, r_q, r_og, m_g) = split_in(h @ prm['w_in'][l])

    q = rms_norm(a_q.reshape(B, T, NSA_HEADS, HEAD_DIM), prm['nsa_q_norm'][l]) * (HEAD_DIM ** -0.5)
    kv = a_kv.reshape(B, T, 3, 2, NSA_KV, HEAD_DIM)
    kg = prm['nsa_k_norm'][l]
    cmp_new = kv[:, :, 0]
    slc_new = jnp.stack([rms_norm(kv[:, :, 1, 0], kg[1]), kv[:, :, 1, 1]], axis=2)
    win_new = jnp.stack([rms_norm(kv[:, :, 2, 0], kg[2]), kv[:, :, 2, 1]], axis=2)
    gates = jax.nn.sigmoid(a_g.reshape(B, T, NSA_HEADS, 3))
    if past is None:
        cmp_rows, slc_rows, win_rows, win_pos0 = cmp_new, slc_new, win_new, pos0
        win_state = win_new[:, T - min(WINDOW, T):]
    else:
        cmp_rows = jnp.concatenate([past['cmp'], cmp_new], axis=1)
        slc_rows = jnp.concatenate([past['slc'], slc_new], axis=1)
        win_rows = jnp.concatenate([past['win'], win_new], axis=1)
        win_pos0 = pos0 - past['win'].shape[1]
        win_state = win_new
    o_a = nsa_mixer(q, gates, cmp_rows, slc_rows, win_rows, pos0, win_pos0, prm['nsa_cmp_pe'][l],
                    prm['nsa_cmp_w1'][l], prm['nsa_cmp_w2'][l], kg[0], blocked)

    conv_buf = jnp.zeros((B, CONV_W - 1, DN_QKV), x.dtype) if past is None else past['conv']
    qkv, conv_state = causal_conv(d_qkv, conv_buf, prm['dn_conv_w'][l])
    dq, dk, dv = jnp.split(jax.nn.silu(qkv), [DN_QK, 2 * DN_QK], axis=-1)
    dq = l2_normalize(dq.reshape(B, T, DN_HEADS, DN_DK)) * (DN_DK ** -0.5)
    dk = l2_normalize(dk.reshape(B, T, DN_HEADS, DN_DK))
    dv = dv.reshape(B, T, DN_HEADS, DN_DV)
    beta = jax.nn.sigmoid(d_b.astype(f32))
    g = -jnp.exp(prm['dn_A_log'][l].astype(f32)) * jax.nn.softplus(d_a.astype(f32) + prm['dn_dt_bias'][l].astype(f32))
    S0 = jnp.zeros((B, DN_HEADS, DN_DK, DN_DV), f32) if past is None else past['dn_S']
    o_d, dn_state = gated_delta_rule(dq, dk, dv, g, beta, S0)
    o_d = rms_norm(o_d.astype(x.dtype), prm['dn_out_norm'][l]) * jax.nn.silu(d_z.reshape(B, T, DN_HEADS, DN_DV))

    lb = hgrn_lower_bounds(prm['hg_lb_logits'])[l]
    zf = r_f.astype(f32)
    logf = jnp.log(lb + (1.0 - lb) * jax.nn.sigmoid(zf))
    k_in = (1.0 - lb) * jax.nn.sigmoid(-zf)
    hq = jax.nn.silu(r_q.reshape(B, T, HG_HEADS, HG_DK)) * (HG_DK ** -0.5)
    H0 = jnp.zeros((B, HG_HEADS, HG_DK, HG_DV), f32) if past is None else past['hg_S']
    o_h, hg_state = hgrn2_recurrence(hq, k_in.reshape(B, T, HG_HEADS, HG_DK), r_i.reshape(B, T, HG_HEADS, HG_DV),
                                     logf.reshape(B, T, HG_HEADS, HG_DK), H0)
    o_h = rms_norm(o_h.astype(x.dtype), prm['hg_out_norm'][l]) * jax.nn.sigmoid(r_og.reshape(B, T, HG_HEADS, HG_DV))

    wb = prm['w_branch'][l]
    mg = jax.nn.sigmoid(m_g.reshape(B, T, 3, D_MODEL))
    branches = (o_a, o_d.reshape(B, T, DN_V), o_h.reshape(B, T, HG_WV))
    offs = (0, NSA_W, NSA_W + DN_V, MIX_W)
    merged = sum(mg[:, :, i] * (branches[i] @ wb[offs[i]:offs[i + 1]]) for i in range(3))
    x = x + merged @ prm['w_out'][l]
    x = x + 0.5 * swiglu(rms_norm(x, prm['ffn2_norm'][l]), prm['ffn2_w_gu'][l], prm['ffn2_w_down'][l])
    return x, (cmp_new, slc_new, win_state, conv_state, dn_state.astype(x.dtype), hg_state.astype(x.dtype))

def run_trunk(x, prm, caches, page_table, pos0, blocked):
    new = []
    for l in range(DEPTH):
        if caches is None:
            past = None
        else:
            c_cmp, c_slc, c_win, s_conv, s_dn, s_hg = caches
            past = {'cmp': gather_pages(c_cmp[l], page_table), 'slc': gather_pages(c_slc[l], page_table),
                    'win': c_win[l], 'conv': s_conv[l], 'dn_S': s_dn[l], 'hg_S': s_hg[l]}
        x, st = decoder_layer(x, l, prm, past, pos0, blocked)
        new.append(st)
    stacked = [jnp.stack([s[i] for s in new], axis=0) for i in range(6)]
    return x, stacked

def setup_inputs(seed: int = 0) -> dict:
    key = jax.random.key(seed)
    keys = iter(jax.random.split(key, 48))

    def nrm(shape, scale=1.0):
        return jax.random.normal(next(keys), shape, jnp.float32) * scale

    def gain(shape):
        return 1.0 + 0.05 * jax.random.normal(next(keys), shape, jnp.float32)

    n_pages = PAST_LEN // PAGE_SIZE
    n_used = DEC_BATCH * n_pages
    n_pool = n_used + n_used // 4
    win_buf = min(WINDOW, PAST_LEN)
    x_prompt = nrm((BATCH, SEQ, D_MODEL))
    x_sample = nrm((DEC_BATCH, DEC_SEQ, D_MODEL))
    cache_cmp_kv = nrm((DEPTH, n_pool, PAGE_SIZE, 2, NSA_KV, HEAD_DIM))
    cache_slc_kv = nrm((DEPTH, n_pool, PAGE_SIZE, 2, NSA_KV, HEAD_DIM))
    cache_win_kv = nrm((DEPTH, DEC_BATCH, win_buf, 2, NSA_KV, HEAD_DIM))
    state_dn_conv = nrm((DEPTH, DEC_BATCH, CONV_W - 1, DN_QKV))
    state_dn_S = nrm((DEPTH, DEC_BATCH, DN_HEADS, DN_DK, DN_DV), 0.1)
    state_hg_S = nrm((DEPTH, DEC_BATCH, HG_HEADS, HG_DK, HG_DV), 0.3)
    page_table = jax.random.permutation(next(keys), n_pool)[:n_used].reshape(DEC_BATCH, n_pages).astype(jnp.int32)
    ffn1_norm = gain((DEPTH, D_MODEL))
    ffn1_w_gu = nrm((DEPTH, D_MODEL, 2 * D_FF), D_MODEL ** -0.5)
    ffn1_w_down = nrm((DEPTH, D_FF, D_MODEL), D_FF ** -0.5)
    mix_norm = gain((DEPTH, D_MODEL))
    w_in = nrm((DEPTH, D_MODEL, IN_COLS), D_MODEL ** -0.5)
    nsa_q_norm = gain((DEPTH, HEAD_DIM))
    nsa_k_norm = gain((DEPTH, 3, HEAD_DIM))
    nsa_cmp_pe = nrm((DEPTH, 2, CMP_LEN, HEAD_DIM), 0.1)
    nsa_cmp_w1 = nrm((DEPTH, 2, CMP_LEN, HEAD_DIM, CMP_HIDDEN), (CMP_LEN * HEAD_DIM) ** -0.5)
    nsa_cmp_w2 = nrm((DEPTH, 2, CMP_HIDDEN, HEAD_DIM), CMP_HIDDEN ** -0.5)
    dn_conv_w = nrm((DEPTH, CONV_W, DN_QKV), CONV_W ** -0.5)
    dn_A_log = jnp.log(jax.random.uniform(next(keys), (DEPTH, DN_HEADS), jnp.float32, 1.0, 16.0))
    dt = jnp.exp(jax.random.uniform(next(keys), (DEPTH, DN_HEADS), jnp.float32, math.log(1e-3), math.log(1e-1)))
    dn_dt_bias = dt + jnp.log(-jnp.expm1(-dt))
    dn_out_norm = gain((DEPTH, DN_DV))
    hg_lb_logits = nrm((DEPTH, HG_WK))
    hg_out_norm = gain((DEPTH, HG_DV))
    w_branch = nrm((DEPTH, MIX_W, D_MODEL), NSA_W ** -0.5)
    w_out = nrm((DEPTH, D_MODEL, D_MODEL), D_MODEL ** -0.5)
    ffn2_norm = gain((DEPTH, D_MODEL))
    ffn2_w_gu = nrm((DEPTH, D_MODEL, 2 * D_FF), D_MODEL ** -0.5)
    ffn2_w_down = nrm((DEPTH, D_FF, D_MODEL), D_FF ** -0.5)
    return {'x_prompt': x_prompt, 'x_sample': x_sample, 'cache_cmp_kv': cache_cmp_kv, 'cache_slc_kv': cache_slc_kv,
            'cache_win_kv': cache_win_kv, 'state_dn_conv': state_dn_conv, 'state_dn_S': state_dn_S,
            'state_hg_S': state_hg_S, 'page_table': page_table, 'ffn1_norm': ffn1_norm, 'ffn1_w_gu': ffn1_w_gu,
            'ffn1_w_down': ffn1_w_down, 'mix_norm': mix_norm, 'w_in': w_in, 'nsa_q_norm': nsa_q_norm,
            'nsa_k_norm': nsa_k_norm, 'nsa_cmp_pe': nsa_cmp_pe, 'nsa_cmp_w1': nsa_cmp_w1, 'nsa_cmp_w2': nsa_cmp_w2,
            'dn_conv_w': dn_conv_w, 'dn_A_log': dn_A_log, 'dn_dt_bias': dn_dt_bias, 'dn_out_norm': dn_out_norm,
            'hg_lb_logits': hg_lb_logits, 'hg_out_norm': hg_out_norm, 'w_branch': w_branch, 'w_out': w_out,
            'ffn2_norm': ffn2_norm, 'ffn2_w_gu': ffn2_w_gu, 'ffn2_w_down': ffn2_w_down}

def reference(x_prompt, x_sample, cache_cmp_kv, cache_slc_kv, cache_win_kv, state_dn_conv, state_dn_S, state_hg_S,
              page_table, ffn1_norm, ffn1_w_gu, ffn1_w_down, mix_norm, w_in, nsa_q_norm, nsa_k_norm, nsa_cmp_pe,
              nsa_cmp_w1, nsa_cmp_w2, dn_conv_w, dn_A_log, dn_dt_bias, dn_out_norm, hg_lb_logits, hg_out_norm,
              w_branch, w_out, ffn2_norm, ffn2_w_gu, ffn2_w_down):
    prm = {'ffn1_norm': ffn1_norm, 'ffn1_w_gu': ffn1_w_gu, 'ffn1_w_down': ffn1_w_down, 'mix_norm': mix_norm,
           'w_in': w_in, 'nsa_q_norm': nsa_q_norm, 'nsa_k_norm': nsa_k_norm, 'nsa_cmp_pe': nsa_cmp_pe,
           'nsa_cmp_w1': nsa_cmp_w1, 'nsa_cmp_w2': nsa_cmp_w2, 'dn_conv_w': dn_conv_w, 'dn_A_log': dn_A_log,
           'dn_dt_bias': dn_dt_bias, 'dn_out_norm': dn_out_norm, 'hg_lb_logits': hg_lb_logits,
           'hg_out_norm': hg_out_norm, 'w_branch': w_branch, 'w_out': w_out, 'ffn2_norm': ffn2_norm,
           'ffn2_w_gu': ffn2_w_gu, 'ffn2_w_down': ffn2_w_down}
    y_prompt, (p_cmp, p_slc, p_win, p_conv, p_dn, p_hg) = run_trunk(x_prompt, prm, None, None, 0, True)
    caches = (cache_cmp_kv, cache_slc_kv, cache_win_kv, state_dn_conv, state_dn_S, state_hg_S)
    y_sample, (s_cmp, s_slc, s_win, s_conv, s_dn, s_hg) = run_trunk(x_sample, prm, caches, page_table, PAST_LEN, False)
    return (y_prompt, y_sample, p_cmp, s_cmp, p_slc, s_slc, p_win, s_win, p_conv, s_conv, p_dn, s_dn, p_hg, s_hg)


_drawn_inputs = setup_inputs


def setup_inputs(seed=0):
    import zlib

    import numpy as np

    out = dict(_drawn_inputs(seed))
    spreads = {}
    factors = {'nsa_q_norm': 8.0, 'dn_out_norm': 2.996, 'hg_out_norm': 2.79, 'ffn2_norm': 2.911}
    for name, (base, spread) in spreads.items():
        noise = np.random.default_rng([zlib.crc32(name.encode()), seed]).standard_normal(out[name].shape)
        drawn = base * np.exp(spread * noise) if base else spread * noise
        out[name] = jnp.asarray(drawn.astype(out[name].dtype))
    for name, factor in factors.items():
        out[name] = (out[name] * factor).astype(out[name].dtype)
    return out
```

```python
from contextlib import ExitStack

import concourse.bass as bass
from concourse import mybir

F32 = mybir.dt.float32
I32 = mybir.dt.int32
ALU = mybir.AluOpType
ACT = mybir.ActivationFunctionType
AX_X = mybir.AxisListType.X

P = 128
L = 2
T = 512
B = 8
N = T + B
HALF = N // 2
KD = 8
FC = 22
KF = FC // 2
SLOT = 12
PAST = 256
NPOOL = 20
PAGES = 2
HD = 64
NBLK = 160
CMPW = T + B * PAST + 16
NPB = 31
QT = T // P
EPS = 1e-6
ZT = 42
SLOT_USES = (49, 49, 49, 48)

CONST = {}
_at = 0
for _name, _w in (("ident", 128), ("ones", 128), ("bones", 128), ("upper", 128), ("level", 7 * 128),
                  ("dist", 512), ("dcmp", 4 * 8 * NPB), ("dsm", PAST + B), ("dcs", 128),
                  ("sel8", 64), ("pos8", 8), ("scanmask", 512), ("slope64", 1)):
    CONST[_name] = (_at, _w)
    _at += _w
NCONST = _at

VEC = {}
_at = 0
for _name, _w in (("ffn1", 8), ("mix", 8), ("ffn2", 8), ("conv", 48), ("qg", 1), ("kg", 3), ("dng", 1),
                  ("hgg", 1), ("alog", 4), ("dtb", 4), ("pe", 64), ("w2", 128)):
    VEC[_name] = (_at, _w)
    _at += _w
NVEC = _at


def slope(pos):
    return 2.0 ** -(4 * (pos % 2) + pos // 2 + 1)


class Steps:

    def __init__(self, sem, names, reps=1):
        self.sem, self.names, self.reps, self.made = sem, names, reps, 0
        self.index = {n: i + 1 for i, n in enumerate(names)}

    def at(self, name, l, r=0):
        return (l * self.reps + r) * len(self.names) + self.index[name]

    def step(self, name):
        assert self.names[self.made % len(self.names)] == name, (name, self.names[self.made % len(self.names)])
        self.made += 1
        return self.sem, 1


def blocks_of(ap, n):
    return ap.rearrange("p (k n) -> p k n", k=n)


def gate_tile(gate, t):
    return gate[:, 28 * t:28 * t + 28]


def attention_plan(m):
    part, sem, bank, pair, both, halves = m["part"], m["sem"], m["bank"], m["pair"], m["both"], m["halves"]
    const_of, scalar_of, gate, ident, o_a = m["const_of"], m["scalar_of"], m["gate"], m["ident"], m["o_a"]

    qT = part(0, 4 * N, 4)
    kvT = part(4 * N, 6 * N, 6)
    cmpT = part(5200, 2 * CMPW, 2)
    w1 = [part(10352, 32 * P, 32), blocks_of(m["mixed"][:, 4 * N:4 * N + 32 * P], 32)]
    hs = part(14448, 4 * NBLK).rearrange("p (k g n) -> p k g n", k=2, g=2)
    sqr = part(15088, 2 * N, 2)
    ckT = part(16128, NBLK)
    peb = part(16288, 2)
    nm = part(16290, 64)
    rs = part(16354, 64)
    fac = part(16418, 64)
    winK = part(16640, B * PAST, B)
    winV = part(18688, B * PAST, 2 * B)
    slcP = part(20736, 2 * B * PAST, 2 * B)
    ssb = part(5200, 3 * 512, 3)
    prb = part(6736, 3 * 512, 3)
    ptb = part(8272, 3 * 512, 3)
    oacc = part(9808, 4 * 512, 4)
    tmp = part(11856, 512)
    vrow = part(12368, 10 * P).rearrange("p (b t n) -> p b t n", b=2, t=5)
    scb = part(13648, 248)
    pcb = part(13896, 248)
    cvp = part(14144, P)
    cvs = part(14272, P)
    ptc = part(24832, 1024)
    qm = part(25856, 64)
    g64 = part(25920, 3)
    g64w = part(25923, 24)
    snm = part(25947, 9, 3)
    stb = part(25956, P)
    ssm = part(15088, PAST + B)
    spm = part(15352, PAST + B)
    spt = part(15616, 512)

    dsm, dcs, sel8, pos8 = const_of("dsm", 64), const_of("dcs", 64), const_of("sel8", 8), const_of("pos8", 64)
    dcmp = const_of("dcmp").rearrange("p (t n) -> p t n", t=QT)
    cached = sem("kv_cache_loaded")
    cmp_in = sem("cmp_rows_loaded")
    padded = sem("cmp_rows_padded")
    kv_saved = sem("kv_rows_saved")
    norm6 = [qT[:, 0, :], qT[:, 1, :], qT[:, 2, :], qT[:, 3, :], kvT[:, 2, :], kvT[:, 4, :]]
    gains = [("qg", 0)] * 4 + [("kg", 1), ("kg", 2)]
    UNITS = QT * 2 * 8

    T_ = Steps(sem("attn_tensor_step"),
               [f"ss{i}" for i in range(6)] + ["peb", "hs0", "hs1", "ckraw", "ckss", "cv", "vt", "g64"]
               + ["st0", "srow0", "spt0", "st1", "srow1", "spt1", "srow2", "spt2", "spv"]
               + [n + str(t) for t in range(QT) for n in ("cs", "cpt", "cpv")])
    S_ = Steps(sem("attn_scalar_step"),
               ["kv", "sq0", "sq1", "std0", "sq2", "std1", "sq3", "std2", "sq4", "std3", "sq5", "std4", "std5"]
               + ["gates", "peb", "hs00", "hs01", "hs10", "hs11", "cksq", "ckstd", "cv", "vrow"]
               + ["st0", "sexp0", "spt0", "st1", "sexp1", "spt1", "sexp2", "spt2"]
               + [n + str(t) for t in range(QT) for n in ("ce", "cpt")])
    V_ = Steps(sem("attn_vector_step"),
               [f"nrm{i}" for i in range(6)] + ["ck", "qm", "g64", "sb0", "sn0", "sb1", "sn1", "sb2", "sn2", "so"]
               + [n + str(t) for t in range(QT) for n in ("cb", "cn", "co")])
    s_ready, biased, negmax, probs, pt_ready, pt_copied, pv_done, comb, ot_ready, ot_copied = (
        sem(n) for n in ("scores_ready", "scores_biased", "row_max_ready", "probs_ready", "probs_transposed",
                         "probs_copied", "values_summed", "branch_added", "o_transposed", "o_copied"))

    def unit(a):
        return a // 16, a // 8 % 2, a % 8

    class Plan:
        def pool(self, e, l):
            e.wait_ge(m["x_done"], 24 * l + 8)
            e.sem_inc(m["turns"], 1)
            e.dma_start(winK, m["ins"]["win_k"][l].rearrange("p (b n) -> p b n", b=B)).then_inc(cached, 16)
            e.dma_start(winV, m["ins"]["win_v"][l].rearrange("p (b n) -> p b n", b=2 * B)).then_inc(cached, 16)
            e.dma_start(w1[1], m["ins"]["w1"][l, 1].rearrange("p (r n) -> p r n", r=32)).then_inc(cmp_in, 16)
            with e.Fori(0, B * PAGES) as i:
                page = e.value_load(m["pages"][0:1, bass.DynSlice(i, 1)], min_val=0, max_val=NPOOL - 1)
                e.dma_start(slcP[:, bass.DynSlice(i, 1), :], m["ins"]["slc_pages"][bass.DynSlice(l * NPOOL + page, 1)]
                            .rearrange("a p n -> p a n")).then_inc(cached, 16)
            e.wait_ge(m["h_done"], 8 * (3 * l + 2))
            e.sem_inc(m["turns"], 1)
            e.dma_start(w1[0], m["ins"]["w1"][l, 0].rearrange("p (r n) -> p r n", r=32)).then_inc(cmp_in, 16)
            e.memset(cmpT[:, :, T + B * PAST:CMPW], 0.0).then_inc(padded, 1)
            with e.Fori(0, B * PAGES) as i:
                page = e.value_load(m["pages"][0:1, bass.DynSlice(i, 1)], min_val=0, max_val=NPOOL - 1)
                e.dma_start(cmpT[:, :, bass.DynSlice(T + P * i, P)],
                            m["ins"]["cmp_pages"][bass.DynSlice(l * NPOOL + page, 1)]
                            .rearrange("a p (k n) -> p (a k) n", k=2)).then_inc(cmp_in, 16)
            e.wait_ge(S_.sem, S_.at("kv", l))
            e.wait_ge(V_.sem, V_.at("nrm5", l))
            e.sem_inc(m["turns"], 1)
            e.dma_start(m["outs"]["kv"][l].rearrange("p (k n) -> p k n", k=6), kvT).then_inc(kv_saved, 16)

        def tensor(self, pe, l):
            def s_(n):
                pe.wait_ge(S_.sem, S_.at(n, l))

            def v_(n):
                pe.wait_ge(V_.sem, V_.at(n, l))

            for i in range(6):
                s_(f"sq{i}")
                if i >= 2:
                    s_(f"std{i - 2}")
                for a in range(2):
                    mm = pe.matmul(pair[2 + i % 2][:, a, 0:HALF], m["bones"], sqr[:, i % 2, a * HALF:(a + 1) * HALF],
                                   start=True, stop=True)
                mm.then_inc(*T_.step(f"ss{i}"))
            pe.wait_ge(cmp_in, 16 * 18 * (l + 1))
            pe.wait_ge(padded, l + 1)
            s_("gates")
            for k in range(2):
                for r in range(32):
                    pe_col = m["vec"][0:HD, VEC["pe"][0] + 32 * k + r:VEC["pe"][0] + 32 * k + r + 1]
                    mm = pe.matmul(bank(2)[:, k:k + 1], w1[k][0:HD, r, :], pe_col, start=(r == 0), stop=(r == 31))
            mm.then_inc(*T_.step("peb"))
            s_("std5")
            for k in range(2):
                for g in range(2):
                    for r in range(32):
                        o = slice(HD * g, HD * g + HD)
                        mm = pe.matmul(pair[2 + k][:, g, 0:NBLK], w1[k][o, r, :],
                                       cmpT[o, k, r:r + 16 * (NBLK - 1) + 1:16], start=(r == 0), stop=(r == 31))
                mm.then_inc(*T_.step(f"hs{k}"))
            w2 = [m["vec"][:, VEC["w2"][0] + HD * k:VEC["w2"][0] + HD * k + HD] for k in range(2)]
            s_("hs01")
            for g in range(2):
                mm = pe.matmul(bank(0)[HD * g:HD * g + HD, 0:NBLK], w2[0], hs[:, 0, g, :], start=True, stop=True)
            mm.then_inc(*T_.step("ckraw"))
            s_("cksq")
            pe.matmul(bank(1)[:, 0:NBLK], m["bones"], sqr[:, 0, 0:NBLK], start=True, stop=True).then_inc(*T_.step("ckss"))
            s_("hs11")
            for g in range(2):
                pe.matmul(bank(2)[0:NPB, 128 + HD * g:128 + HD * g + HD], hs[:, 1, g, 0:NPB], w2[1], start=True, stop=True)
                mm = pe.matmul(bank(3)[:, HD * g:HD * g + HD], hs[:, 1, g, 32:NBLK], w2[1], start=True, stop=True)
            mm.then_inc(*T_.step("cv"))
            v_("nrm5")
            for b in range(2):
                for t in range(4):
                    pe.transpose(bank(4 + b)[:, P * t:P * t + P], kvT[:, 3 + 2 * b, P * t:P * t + P], ident)
                mm = pe.transpose(bank(6)[0:B, P * b:P * b + P], kvT[:, 3 + 2 * b, T:N], ident)
            mm.then_inc(*T_.step("vt"))
            s_("gates")
            s_("hs11")
            pe.matmul(bank(7)[0:64, 0:24], sel8, gate_tile(gate, 4)[0:B, 0:24], start=True, stop=True).then_inc(*T_.step("g64"))

            v_("qm")
            s_("vrow")
            pe.wait_ge(cached, 16 * 18 * (l + 1))
            for b in range(3):
                if b < 2:
                    if b:
                        s_("st0")
                    for k in range(2):
                        for s in range(B):
                            kk = slcP[:, 2 * s + k, 0:P] if b == 0 else winK[:, s, P * k:P * k + P]
                            mm = pe.matmul(bank(0)[:, 64 * k + 8 * s:64 * k + 8 * s + 8], kk, qm[:, 8 * s:8 * s + 8],
                                           start=True, stop=True)
                    mm.then_inc(*T_.step(f"st{b}"))
                    s_(f"st{b}")
                    if b:
                        v_("sb0")
                    pe.matmul(bank(1)[0:64, PAST:PAST + B], qm, kvT[:, 2 + 2 * b, T:N], start=True, stop=True)
                    for k in range(2):
                        mm = pe.transpose(bank(1)[0:64, P * k:P * k + P], stb[:, 64 * k:64 * k + 64], ident)
                    mm.then_inc(*T_.step(f"srow{b}"))
                else:
                    v_("ck")
                    v_("sb1")
                    pe.matmul(bank(1)[0:64, 0:P], qm, ckT[:, 32:NBLK], start=True, stop=True).then_inc(*T_.step("srow2"))
                v_(f"sn{b}")
                if b:
                    s_(f"spt{b - 1}")
                for k in range(2 if b < 2 else 1):
                    mm = pe.matmul(bank(2)[:, 64 * k:64 * k + 64], spm[0:64, P * k:P * k + P], ident[0:64, 0:64],
                                   start=True, stop=True)
                if b < 2:
                    mm = pe.matmul(bank(2)[0:B, 128:192], spm[0:64, PAST:PAST + B], ident[0:64, 0:64],
                                   start=True, stop=True)
                mm.then_inc(*T_.step(f"spt{b}"))
            s_("spt2")
            pe.matmul(bank(3)[:, 0:64], cvs, spt[:, 384:448], start=True, stop=False, skip_group_check=True)
            for b in range(2):
                pe.matmul(bank(3)[:, 0:64], vrow[0:B, b, 4, :], spt[0:B, 192 * b + 128:192 * b + 192],
                          start=False, stop=False, skip_group_check=True)
                for k in range(2):
                    for s in range(B):
                        vv = slcP[:, 2 * s + k, P:2 * P] if b == 0 else winV[:, 2 * s + k, :]
                        mm = pe.matmul(bank(3)[:, 8 * s:8 * s + 8], vv, spt[:, 192 * b + 64 * k + 8 * s:192 * b + 64 * k + 8 * s + 8],
                                       start=False, stop=(b == 1 and k == 1), skip_group_check=True)
            mm.then_inc(*T_.step("spv"))

            v_("so")
            for t in range(QT):
                if t:
                    v_(f"cb{t - 1}")
                for p in range(8):
                    c, g = p // 2, p % 2
                    o = slice(HD * g, HD * g + HD)
                    mm = pe.matmul(bank(g)[:, NPB * c:NPB * c + NPB], qT[o, c, P * t:P * t + P], ckT[o, 0:NPB],
                                   start=True, stop=True)
                mm.then_inc(*T_.step(f"cs{t}"))
                v_(f"cn{t}")
                for p in range(8):
                    mm = pe.transpose(pair[1][0:NPB, p // 4, P * (p % 4):P * (p % 4) + P], pcb[:, NPB * p:NPB * p + NPB], ident)
                mm.then_inc(*T_.step(f"cpt{t}"))
                s_(f"cpt{t}")
                if t:
                    v_(f"co{t - 1}")
                for p in range(8):
                    mm = pe.matmul(bank(4)[:, HD * p:HD * p + HD], ptc[0:NPB, P * p:P * p + P],
                                   cvp[0:NPB, HD * (p % 2):HD * (p % 2) + HD], start=True, stop=True)
                mm.then_inc(*T_.step(f"cpv{t}"))

            v_(f"co{QT - 1}")

            def scores(a):
                t, b, p = unit(a)
                if a >= 3:
                    pe.wait_ge(biased, UNITS * l + a - 2)
                w = P * (t + 1)
                o = slice(HD * (p % 2), HD * (p % 2) + HD)
                pe.matmul(bank(a % 3)[:, 0:w], qT[o, p // 2, P * t:P * t + P], kvT[o, 2 + 2 * b, 0:w],
                          start=True, stop=True).then_inc(s_ready, 1)

            def turn(a):
                t, _, _ = unit(a)
                pe.wait_ge(probs, UNITS * l + a + 1)
                if a >= 2:
                    pe.wait_ge(pt_copied, UNITS * l + a - 1)
                for k in range(t + 1):
                    mm = pe.transpose(bank(3 + a % 2)[:, P * k:P * k + P], prb[:, a % 3, P * k:P * k + P], ident)
                mm.then_inc(pt_ready, 1)

            def values(a):
                t, b, p = unit(a)
                c = a // 8
                pe.wait_ge(pt_copied, UNITS * l + a + 1)
                if p == 0 and c >= 2:
                    pe.wait_ge(comb, 8 * l + c - 1)
                for k in range(t + 1):
                    mm = pe.matmul(bank(5 + c % 2)[:, HD * p:HD * p + HD], ptb[:, a % 3, P * k:P * k + P],
                                   vrow[:, b, k, HD * (p % 2):HD * (p % 2) + HD], start=(k == 0), stop=(k == t))
                mm.then_inc(pv_done, 1)

            def o_turn(t):
                pe.wait_ge(comb, 8 * l + 2 * t + 2)
                if t:
                    pe.wait_ge(ot_copied, QT * l + t)
                for c in range(4):
                    mm = pe.transpose(bank(7)[:, P * c:P * c + P], oacc[:, t, P * c:P * c + P], ident)
                mm.then_inc(ot_ready, 1)

            for i in range(UNITS + 4):
                if i < UNITS:
                    scores(i)
                if 2 <= i < UNITS + 2:
                    turn(i - 2)
                if i >= 4:
                    values(i - 4)
                if i >= 28 and (i - 28) % 16 == 0:
                    o_turn((i - 28) // 16)
            o_turn(QT - 1)

        def scalar(self, e, l):
            def t_(n):
                e.wait_ge(T_.sem, T_.at(n, l))

            def v_(n):
                e.wait_ge(V_.sem, V_.at(n, l))

            for zi in range(10):
                e.wait_ge(m["z_ready"], ZT * l + zi + 1)
                if zi in (4, 5):
                    e.activation(cmpT[:, zi - 4, 0:HALF], pair[zi % 2][:, 0, 0:HALF], ACT.Copy)
                    e.activation(cmpT[:, zi - 4, HALF:T], pair[zi % 2][:, 1, 0:T - HALF], ACT.Copy)
                dst = qT[:, zi, :] if zi < 4 else kvT[:, zi - 4, :]
                e.activation(halves(dst), both(zi % 2), ACT.Copy).then_inc(m["z_used"], 1)
            e.drain().then_inc(*S_.step("kv"))

            def square(i):
                if i >= 2:
                    t_(f"ss{i - 2}")
                e.activation(sqr[:, i % 2, :], norm6[i], ACT.Square).then_inc(*S_.step(f"sq{i}"))

            def std(i):
                t_(f"ss{i}")
                if i >= 2:
                    v_(f"nrm{i - 2}")
                e.activation(halves(m["rstd"][:, N * (i % 2):N * (i % 2) + N]), both(2 + i % 2), ACT.Sqrt,
                             bias=m["eps"][:, :], scale=1.0 / HD).then_inc(*S_.step(f"std{i}"))

            square(0)
            square(1)
            for i in range(6):
                std(i)
                if i + 2 < 6:
                    square(i + 2)
            e.wait_ge(m["small_ready"], l + 1)
            e.activation(m["small"][:, 0:128], bank(0)[:, 0:128], ACT.Copy)
            e.activation(m["small"][0:B, 128:160], bank(0)[0:B, 128:160], ACT.Copy)
            e.drain()
            e.activation(m["gate"][:, :].rearrange("p (t n) -> p t n", t=5),
                         m["small"][:, :].rearrange("p (t n) -> p t n", t=5)[:, :, 0:28], ACT.Sigmoid).then_inc(*S_.step("gates"))
            t_("peb")
            e.activation(peb, bank(2)[:, 0:2], ACT.Copy).then_inc(*S_.step("peb"))
            e.drain()
            for k in range(2):
                t_(f"hs{k}")
                for g in range(2):
                    e.activation(hs[:, k, g, :], pair[2 + k][:, g, 0:NBLK], ACT.Silu,
                                 bias=peb[:, k:k + 1]).then_inc(*S_.step(f"hs{k}{g}"))
            t_("ckraw")
            e.activation(sqr[:, 0, 0:NBLK], bank(0)[:, 0:NBLK], ACT.Square).then_inc(*S_.step("cksq"))
            t_("ckss")
            v_("nrm5")
            e.activation(m["rstd"][:, 0:NBLK], bank(1)[:, 0:NBLK], ACT.Sqrt, bias=m["eps"][:, :],
                         scale=1.0 / HD).then_inc(*S_.step("ckstd"))
            t_("cv")
            e.activation(cvp[0:NPB, :], bank(2)[0:NPB, 128:256], ACT.Copy)
            e.activation(cvs, bank(3)[:, 0:P], ACT.Copy).then_inc(*S_.step("cv"))
            t_("vt")
            for b in range(2):
                e.activation(vrow[:, b, 0:4, :], bank(4 + b).rearrange("p (t n) -> p t n", t=4), ACT.Copy)
            e.activation(vrow[0:B, :, 4, :], bank(6)[0:B, 0:2 * P].rearrange("p (b n) -> p b n", b=2),
                         ACT.Copy).then_inc(*S_.step("vrow"))
            for b in range(3):
                if b < 2:
                    t_(f"st{b}")
                    if b:
                        t_("srow0")
                    e.activation(stb, bank(0)[:, 0:P], ACT.Copy).then_inc(*S_.step(f"st{b}"))
                v_(f"sb{b}")
                w = PAST + B if b < 2 else P
                e.activation(spm[0:64, 0:w], ssm[0:64, 0:w], ACT.Exp, bias=snm[0:64, b, 0:1],
                             accum_out=snm[0:64, b, 1:2]).then_inc(*S_.step(f"sexp{b}"))
                t_(f"spt{b}")
                e.activation(spt[:, 192 * b:192 * b + (128 if b < 2 else 64)], bank(2)[:, 0:(128 if b < 2 else 64)], ACT.Copy) \
                    .then_inc(*(S_.step("spt2") if b == 2 else (spare, 1)))
                if b < 2:
                    e.activation(spt[0:B, 192 * b + 128:192 * b + 192], bank(2)[0:B, 128:192],
                                 ACT.Copy).then_inc(*S_.step(f"spt{b}"))
            for t in range(QT):
                v_(f"cb{t}")
                if t:
                    t_(f"cpt{t - 1}")
                e.activation(pcb, scb, ACT.Exp).then_inc(*S_.step(f"ce{t}"))
                t_(f"cpt{t}")
                if t:
                    t_(f"cpv{t - 1}")
                e.activation(ptc[0:NPB, :].rearrange("p (a n) -> p a n", a=2), pair[1][0:NPB, :, :],
                             ACT.Copy).then_inc(*S_.step(f"cpt{t}"))

            def exp(a):
                w = P * (unit(a)[0] + 1)
                e.wait_ge(negmax, UNITS * l + a + 1)
                if a >= 3:
                    e.wait_ge(pt_ready, UNITS * l + a - 2)
                e.activation(prb[:, a % 3, 0:w], ssb[:, a % 3, 0:w], ACT.Exp, bias=nm[:, a:a + 1],
                             accum_out=rs[:, a:a + 1]).then_inc(probs, 1)

            def copy_pt(a):
                w = P * (unit(a)[0] + 1)
                e.wait_ge(pt_ready, UNITS * l + a + 1)
                if a >= 3:
                    e.wait_ge(pv_done, UNITS * l + a - 2)
                e.activation(ptb[:, a % 3, 0:w], bank(3 + a % 2)[:, 0:w], ACT.Copy).then_inc(pt_copied, 1)

            def o_copy(t):
                e.wait_ge(ot_ready, QT * l + t + 1)
                e.activation(o_a[:, :, P * t:P * t + P], bank(7).rearrange("p (c n) -> p c n", c=4),
                             ACT.Copy).then_inc(ot_copied, 1)

            for i in range(UNITS + 2):
                if i < UNITS:
                    exp(i)
                if i >= 2:
                    copy_pt(i - 2)
                if i >= 30 and (i - 30) % 16 == 0:
                    o_copy((i - 30) // 16)
            o_copy(QT - 1)

        def vector(self, e, l):
            def t_(n):
                e.wait_ge(T_.sem, T_.at(n, l))

            def s_(n):
                e.wait_ge(S_.sem, S_.at(n, l))

            for i in range(6):
                s_(f"std{i}")
                r = m["rstd"][:, N * (i % 2):N * (i % 2) + N]
                e.reciprocal(r, r)
                e.drain()
                e.scalar_tensor_tensor(norm6[i], norm6[i], scalar_of(*gains[i]), r, ALU.mult, ALU.mult)
                if i < 4:
                    e.drain()
                    e.tensor_scalar(norm6[i], norm6[i], HD ** -0.5, None, ALU.mult).then_inc(*V_.step(f"nrm{i}"))
                else:
                    e.drain().then_inc(*V_.step(f"nrm{i}"))
            s_("ckstd")
            e.reciprocal(m["rstd"][:, 0:NBLK], m["rstd"][:, 0:NBLK])
            e.drain()
            e.scalar_tensor_tensor(ckT, bank(0)[:, 0:NBLK], scalar_of("kg", 0), m["rstd"][:, 0:NBLK],
                                   ALU.mult, ALU.mult).then_inc(*V_.step("ck"))
            q4 = qm.rearrange("p (b c g) -> p b c g", c=4, g=2)
            e.memset(qm, 0.0)
            e.drain()
            for g in range(2):
                o = slice(HD * g, HD * g + HD)
                mm = e.tensor_copy(q4[o, :, :, g], qT[o, :, T:N].rearrange("p c b -> p b c"))
            e.drain().then_inc(*V_.step("qm"))
            t_("g64")
            gw = g64w[0:64, :].rearrange("p (b n) -> p b n", b=3)
            e.tensor_tensor(gw, bank(7)[0:64, 0:24].rearrange("p (b n) -> p b n", b=3),
                            pos8.unsqueeze(1).to_broadcast([64, 3, 8]), ALU.mult)
            e.drain()
            e.tensor_reduce(g64[0:64, :], gw, AX_X, ALU.add).then_inc(*V_.step("g64"))
            for b in range(3):
                w = PAST + B if b < 2 else P
                t_(f"srow{b}")
                e.tensor_tensor(ssm[0:64, 0:w], bank(1)[0:64, 0:w], dsm if b < 2 else dcs, ALU.add)
                e.drain()
                e.tensor_reduce(snm[0:64, b, 0:1], ssm[0:64, 0:w], AX_X, ALU.max, negate=True).then_inc(*V_.step(f"sb{b}"))
                s_(f"sexp{b}")
                e.reciprocal(snm[0:64, b, 2:3], snm[0:64, b, 1:2])
                e.drain()
                gi = (1, 2, 0)[b]
                e.tensor_scalar(spm[0:64, 0:w], spm[0:64, 0:w], snm[0:64, b, 2:3], g64[0:64, gi:gi + 1],
                                ALU.mult, ALU.mult).then_inc(*V_.step(f"sn{b}"))
            t_("spv")
            for g in range(2):
                o = slice(HD * g, HD * g + HD)
                e.tensor_copy(o_a[o, :, T:N].rearrange("p c b -> p b c"),
                              bank(3)[o, 0:64].rearrange("p (b c g) -> p b c g", c=4, g=2)[:, :, :, g])
            e.drain().then_inc(*V_.step("so"))
            for t in range(QT):
                s8 = scb.rearrange("p (h n) -> p h n", h=8)
                p8 = pcb.rearrange("p (h n) -> p h n", h=8)
                t_(f"cs{t}")
                for g in range(2):
                    e.tensor_tensor(scb.rearrange("p (c g n) -> p g c n", c=4, g=2)[:, g],
                                    bank(g)[:, 0:4 * NPB].rearrange("p (c n) -> p c n", c=4),
                                    dcmp[:, t, :].rearrange("p (c g n) -> p g c n", c=4, g=2)[:, g], ALU.add)
                e.drain()
                e.tensor_reduce(nm[:, 0:8], s8, AX_X, ALU.max, negate=True)
                e.drain()
                e.tensor_scalar(nm[:, 8:16], nm[:, 0:8], 1e20, None, ALU.min)
                e.drain()
                e.tensor_tensor(s8, s8, nm[:, 8:16].unsqueeze(2).to_broadcast([P, 8, NPB]),
                                ALU.add).then_inc(*V_.step(f"cb{t}"))
                s_(f"ce{t}")
                e.tensor_reduce(rs[:, 0:8], p8, AX_X, ALU.add)
                e.drain()
                e.tensor_scalar(rs[:, 8:16], rs[:, 0:8], 1e-30, None, ALU.max)
                e.drain()
                e.reciprocal(rs[:, 16:24], rs[:, 8:16])
                e.drain()
                e.tensor_tensor(fac[:, 0:8], rs[:, 16:24], gate_tile(gate, t)[:, 0:8], ALU.mult)
                e.drain()
                e.tensor_tensor(p8, p8, fac[:, 0:8].unsqueeze(2).to_broadcast([P, 8, NPB]),
                                ALU.mult).then_inc(*V_.step(f"cn{t}"))
                t_(f"cpv{t}")
                e.tensor_copy(oacc[:, t, :], bank(4)).then_inc(*V_.step(f"co{t}"))
            e.drain()

            def bias(a):
                t, b, p = unit(a)
                w = P * (t + 1)
                e.wait_ge(s_ready, UNITS * l + a + 1)
                if a >= 3:
                    e.wait_ge(probs, UNITS * l + a - 2)
                e.scalar_tensor_tensor(ssb[:, a % 3, 0:w], m["dist"][:, T - w:T], slope(p), bank(a % 3)[:, 0:w],
                                       ALU.mult, ALU.add).then_inc(biased, 1)

            def rowmax(a):
                w = P * (unit(a)[0] + 1)
                e.wait_ge(biased, UNITS * l + a + 1)
                e.tensor_reduce(nm[:, a:a + 1], ssb[:, a % 3, 0:w], AX_X, ALU.max, negate=True).then_inc(negmax, 1)

            def combine(c):
                t, b = c // 2, c % 2
                e.wait_ge(pv_done, UNITS * l + 8 * c + 8)
                e.reciprocal(fac[:, 0:8], rs[:, 8 * c:8 * c + 8])
                e.drain()
                e.tensor_tensor(fac[:, 8:16], fac[:, 0:8], gate_tile(gate, t)[:, 8 + 8 * b:16 + 8 * b], ALU.mult)
                e.drain()
                e.tensor_tensor(tmp.rearrange("p (h n) -> p h n", h=8), bank(5 + c % 2).rearrange("p (h n) -> p h n", h=8),
                                fac[:, 8:16].unsqueeze(2).to_broadcast([P, 8, HD]), ALU.mult)
                e.drain()
                e.tensor_tensor(oacc[:, t, :], oacc[:, t, :], tmp, ALU.add).then_inc(comb, 1)

            for i in range(UNITS + 6):
                if i < UNITS:
                    bias(i)
                if 1 <= i <= UNITS:
                    rowmax(i - 1)
                if i >= 13 and (i - 13) % 8 == 0:
                    combine((i - 13) // 8)
            e.drain()

    spare = sem("sample_probs_copied")
    p = Plan()
    p.kv_saved = kv_saved
    p.ot_copied = ot_copied
    return p


def state_steps(kind):
    vb = [f"vb{i}" for i in range(8)]
    return vb + ["so"], ["so"], ["sdec"] + [f"sa{i}" for i in range(8)]


def state_tensor(pe, l, m, T_, V_, S_, ss, vcol, q, banks):
    for i in range(8):
        pe.wait_ge(V_.sem, V_.at("sdec" if i < 2 else f"sa{i - 2}", l))
        for j in range(4):
            mm = pe.matmul(m["bank"](banks[i % 2])[:, P * j:P * j + P], vcol(4 * i + j).to_broadcast([P, P]), m["ident"],
                           start=True, stop=True)
        mm.then_inc(*T_.step(f"vb{i}"))
    pe.wait_ge(V_.sem, V_.at("sa7", l))
    for i in range(32):
        mm = pe.matmul(m["bank"](banks[2])[:, i:i + 1], ss[:, i, :], q[:, i // 8, T + i % 8:T + i % 8 + 1],
                       start=True, stop=True)
    mm.then_inc(*T_.step("so"))


def state_vector(e, l, m, T_, V_, ss, decay, k, tmp, banks):
    e.tensor_tensor(ss, ss, decay.unsqueeze(2).to_broadcast([P, 32, P]), ALU.mult).then_inc(*V_.step("sdec"))
    for i in range(8):
        e.wait_ge(T_.sem, T_.at(f"vb{i}", l))
        kc = k[:, i // 2, T + 4 * (i % 2):T + 4 * (i % 2) + 4]
        e.tensor_tensor(tmp[:, i % 2, :].rearrange("p (i n) -> p i n", i=4),
                        m["bank"](banks[i % 2]).rearrange("p (i n) -> p i n", i=4),
                        kc.unsqueeze(2).to_broadcast([P, 4, P]), ALU.mult)
        e.drain()
        e.tensor_tensor(ss[:, 4 * i:4 * i + 4, :], ss[:, 4 * i:4 * i + 4, :],
                        tmp[:, i % 2, :].rearrange("p (i n) -> p i n", i=4), ALU.add).then_inc(*V_.step(f"sa{i}"))


def state_scalar(e, l, m, T_, S_, o, banks):
    e.wait_ge(T_.sem, T_.at("so", l))
    e.activation(o[:, :, T:N], m["bank"](banks[2])[:, 0:32].rearrange("p (h b) -> p h b", h=4),
                 ACT.Copy).then_inc(*S_.step("so"))


def norm_steps(name, n):
    s = [f"{name}q0", f"{name}q1"]
    for i in range(n):
        s.append(f"{name}d{i}")
        if i + 2 < n:
            s.append(f"{name}q{i + 2}")
    return [f"{name}s{i}" for i in range(n)], s, [f"{name}n{i}" for i in range(n)]


def norm_tensor(pe, l, m, T_, S_, name, n, sqr):
    for i in range(n):
        pe.wait_ge(S_.sem, S_.at(f"{name}q{i}", l))
        if i >= 2:
            pe.wait_ge(S_.sem, S_.at(f"{name}d{i - 2}", l))
        for a in range(2):
            mm = pe.matmul(m["pair"][2 + i % 2][:, a, 0:HALF], m["ones"], sqr[:, i % 2, a * HALF:(a + 1) * HALF],
                           start=True, stop=True)
        mm.then_inc(*T_.step(f"{name}s{i}"))


def norm_scalar(e, l, m, T_, S_, V_, name, bufs, sqr, scale, ready=None):
    n = len(bufs)

    def square(i):
        if ready is not None:
            ready(i)
        if i >= 2:
            e.wait_ge(T_.sem, T_.at(f"{name}s{i - 2}", l))
        e.activation(sqr[:, i % 2, :], bufs[i], ACT.Square).then_inc(*S_.step(f"{name}q{i}"))

    square(0)
    square(1)
    for i in range(n):
        e.wait_ge(T_.sem, T_.at(f"{name}s{i}", l))
        if i >= 2:
            e.wait_ge(V_.sem, V_.at(f"{name}n{i - 2}", l))
        e.activation(m["halves"](m["rstd"][:, N * (i % 2):N * (i % 2) + N]), m["both"](2 + i % 2), ACT.Sqrt,
                     bias=m["eps"][:, :], scale=scale).then_inc(*S_.step(f"{name}d{i}"))
        if i + 2 < n:
            square(i + 2)


def norm_vector(e, l, m, S_, V_, name, bufs, gain, after):
    for i, b in enumerate(bufs):
        e.wait_ge(S_.sem, S_.at(f"{name}d{i}", l))
        r = m["rstd"][:, N * (i % 2):N * (i % 2) + N]
        e.reciprocal(r, r)
        e.drain()
        e.scalar_tensor_tensor(b, b, gain(i), r, ALU.mult, ALU.mult)
        if after(i) is None:
            e.drain().then_inc(*V_.step(f"{name}n{i}"))
        else:
            e.drain()
            e.tensor_tensor(b, b, after(i), ALU.mult).then_inc(*V_.step(f"{name}n{i}"))


def delta_plan(m):
    part, sem, bank, pair, both, halves = m["part"], m["sem"], m["bank"], m["pair"], m["both"], m["halves"]
    scalar_of, vec_of, gate, ident, ones, upper, level, o_d = (
        m["scalar_of"], m["vec_of"], m["gate"], m["ident"], m["ones"], m["upper"], m["level"], m["o_d"])

    cx = part(0, 12 * 515, 12)
    xs = part(6180, 12 * B * 4).rearrange("p (c b j) -> p c b j", c=12, b=B)
    cy = part(6564, 12 * N, 12)
    dz = part(12804, 4 * N, 4)
    ss = part(14884, 32 * P, 32)
    sqr = part(18980, 2 * N, 2)

    def four(at):
        return part(at, 512, 4)

    S, dec, at_, lt, ta, tb, yb, ls0, ls1, rb, vn, eg = (four(20020 + 512 * i) for i in range(12))
    ls = (ls0, ls1)
    ktl, vr, qt = four(0), four(512), four(1024)
    tmp = part(1536, 1024, 2)
    cin = part(21044, 288)
    cout = part(2700, 36 + 288)
    xw = part(21400, 128).rearrange("p (c b j) -> p c b j", c=4, b=B)
    gx, ga, gl, gd = (part(26164 + 20 * i, 20) for i in range(4))
    gc, egc, ktf, neg, ea = (part(26244 + 4 * i, 4) for i in range(5))
    egs = part(26264, 32)
    vns = part(26296, 32)

    n_t, n_s, n_v = norm_steps("l", 8)
    o_t, o_s, o_v = norm_steps("o", 4)
    st_t, st_s, st_v = state_steps("d")
    lv = range(1, 7)
    tile_t = ["gb", "kk", "rows", "y0"] + [n for i in lv for n in (f"y{i}", f"ty{i}")] + ["ks", "vn", "o", "s"]
    tile_s = ["exp", "vr"] + [f"y{i}" for i in lv] + ["vn", "o"]
    tile_v = ["dec", "lt", "qt", "kt"] + [f"t{i}" for i in range(7)] + ["r", "s"]
    T_ = Steps(sem("delta_tensor_step"), n_t + [f"{n}.{t}" for t in range(QT) for n in tile_t] + ["sk"] + st_t + o_t)
    S_ = Steps(sem("delta_scalar_step"), ["ge", "gl"] + ["silu0", "silu1", "silu2"] + n_s
               + [f"{n}.{t}" for t in range(QT) for n in tile_s] + ["seg"] + st_s + o_s)
    V_ = Steps(sem("delta_vector_step"), ["ga", "cin", "conv0", "conv1", "conv2", "g"] + n_v
               + [f"{n}.{t}" for t in range(QT) for n in tile_v] + ["svn"] + st_v + o_v)
    P_ = Steps(sem("delta_pool_step"), ["pad"] + [f"ls{i}.{t}" for t in range(QT) for i in range(7)])
    conv_in, states_in, saved = sem("conv_state_loaded"), sem("delta_states_loaded"), sem("delta_outputs_saved")

    def each_head(ap):
        return ap.unsqueeze(1).to_broadcast([P, 4, P])

    def cols(ap):
        return ap.unsqueeze(2).to_broadcast([P, 4, P])

    def heads(i):
        return bank(i).rearrange("p (h n) -> p h n", h=4)

    class Plan:
        def pool(self, e, l):
            e.wait_ge(m["A"].ot_copied, QT * (l + 1))
            e.wait_ge(m["A"].kv_saved, 16 * (l + 1))
            e.sem_inc(m["turns"], 1)
            e.dma_start(cin, m["ins"]["conv_in"][l]).then_inc(conv_in, 16)
            e.dma_start(ss, m["ins"]["dn_in"][l].rearrange("p (i n) -> p i n", i=32)).then_inc(states_in, 16)
            e.memset(cx[:, :, 0:3], 0.0).then_inc(*P_.step("pad"))
            for t in range(QT):
                e.wait_ge(V_.sem, V_.at(f"lt.{t}", l))
                for i in range(7):
                    if i >= 2:
                        e.wait_ge(T_.sem, T_.at(f"y{i - 2}.{t}", l))
                    elif t:
                        e.wait_ge(T_.sem, T_.at(f"y{5 + i}.{t - 1}", l))
                    if i == 2:
                        e.wait_ge(V_.sem, V_.at(f"t0.{t}", l))
                    e.tensor_tensor(ls[i % 2], lt, each_head(level[:, i, :]), ALU.mult).then_inc(*P_.step(f"ls{i}.{t}"))
            e.wait_ge(V_.sem, V_.at("sa7", l))
            e.sem_inc(m["turns"], 1)
            e.dma_start(m["outs"]["conv_p"][l], cout[:, 0:36]).then_inc(saved, 16)
            e.dma_start(m["outs"]["conv_s"][l], cout[:, 36:324]).then_inc(saved, 16)
            e.dma_start(m["outs"]["dn_p"][l].rearrange("p (h n) -> p h n", h=4), S).then_inc(saved, 16)
            e.dma_start(m["outs"]["dn_s"][l].rearrange("p (i n) -> p i n", i=32), ss).then_inc(saved, 16)

        def tensor(self, pe, l):
            def w(steps, n):
                pe.wait_ge(steps.sem, steps.at(n, l))

            norm_tensor(pe, l, m, T_, S_, "l", 8, sqr)
            w(V_, "g")
            w(V_, "ln7")
            for t in range(QT):
                k = [cy[:, 4 + h, P * t:P * t + P] for h in range(4)]
                q = [cy[:, h, P * t:P * t + P] for h in range(4)]
                v = [cy[:, 8 + h, P * t:P * t + P] for h in range(4)]
                if t:
                    w(V_, f"t6.{t - 1}")
                    w(S_, f"o.{t - 1}")
                pe.matmul(bank(7)[:, 0:4], upper, gd[:, 4 * t:4 * t + 4], start=True, stop=True)
                for h in range(4):
                    pe.matmul(heads(6)[:, h, :], gd[:, 4 * t + h:4 * t + h + 1].to_broadcast([P, P]), upper,
                              start=True, stop=True)
                    b = gate_tile(gate, t)[:, 24 + h:25 + h]
                    mm = pe.matmul(heads(5)[:, h, :], b.to_broadcast([P, P]), ident, start=True, stop=True)
                mm.then_inc(*T_.step(f"gb.{t}"))
                if t:
                    w(V_, f"s.{t - 1}")
                for h in range(4):
                    pe.matmul(heads(4)[:, h, :], k[h], k[h], start=True, stop=True)
                    mm = pe.matmul(heads(3)[:, h, :], k[h], q[h], start=True, stop=True)
                mm.then_inc(*T_.step(f"kk.{t}"))
                for h in range(4):
                    pe.transpose(heads(2)[:, h, :], k[h], ident)
                    mm = pe.transpose(heads(1)[:, h, :], v[h], ident)
                mm.then_inc(*T_.step(f"rows.{t}"))
                w(P_, f"ls0.{t}")
                for h in range(4):
                    mm = pe.matmul(heads(0)[:, h, :], ls[0][:, h, :], ident, start=True, stop=True)
                mm.then_inc(*T_.step(f"y0.{t}"))
                for i in lv:
                    w(V_, f"t{i - 1}.{t}")
                    w(P_, f"ls{i}.{t}")
                    for h in range(4):
                        mm = pe.matmul(heads(0)[:, h, :], ls[i % 2][:, h, :], ta[:, h, :], start=True, stop=True)
                    mm.then_inc(*T_.step(f"y{i}.{t}"))
                    w(S_, f"y{i}.{t}")
                    for h in range(4):
                        if i < 6:
                            pe.matmul(heads(6)[:, h, :], tb[:, h, :], yb[:, h, :], start=True, stop=True)
                        mm = pe.matmul(heads(7)[:, h, :], yb[:, h, :], tb[:, h, :], start=True, stop=True)
                    mm.then_inc(*T_.step(f"ty{i}.{t}"))
                for h in range(4):
                    mm = pe.matmul(heads(4)[:, h, :], k[h], S[:, h, :], start=True, stop=True)
                mm.then_inc(*T_.step(f"ks.{t}"))
                w(V_, f"r.{t}")
                for h in range(4):
                    mm = pe.matmul(heads(3)[:, h, :], tb[:, h, :], rb[:, h, :], start=True, stop=True)
                mm.then_inc(*T_.step(f"vn.{t}"))
                w(S_, f"vn.{t}")
                for h in range(4):
                    pe.matmul(heads(5)[:, h, :], S[:, h, :], qt[:, h, :], start=True, stop=False)
                    mm = pe.matmul(heads(5)[:, h, :], vn[:, h, :], at_[:, h, :], start=False, stop=True)
                mm.then_inc(*T_.step(f"o.{t}"))
                for h in range(4):
                    mm = pe.matmul(heads(4)[:, h, :], ktl[:, h, :], vn[:, h, :], start=True, stop=True)
                mm.then_inc(*T_.step(f"s.{t}"))
            w(V_, "t6.3")
            pe.wait_ge(states_in, 16 * (l + 1))
            for h in range(4):
                pe.matmul(bank(7)[:, 8 * h:8 * h + 8], gd[0:B, 16 + h:17 + h].to_broadcast([B, P]), ident[0:B, 0:B],
                          start=True, stop=True)
                pe.matmul(bank(7)[:, 32 + 8 * h:40 + 8 * h], gate_tile(gate, 4)[0:B, 24 + h:25 + h].to_broadcast([B, P]),
                          ident[0:B, 0:B], start=True, stop=True)
            for i in range(32):
                mm = pe.matmul(bank(7)[:, 64 + i:65 + i], ss[:, i, :], cy[:, 4 + i // 8, T + i % 8:T + i % 8 + 1],
                               start=True, stop=True)
            mm.then_inc(*T_.step("sk"))
            w(S_, "o.3")
            state_tensor(pe, l, m, T_, V_, S_, ss, lambda i: vns[:, i:i + 1], cy, (5, 6, 0))
            norm_tensor(pe, l, m, T_, S_, "o", 4, sqr)

        def scalar(self, e, l):
            def w(steps, n):
                e.wait_ge(steps.sem, steps.at(n, l))

            w(V_, "ga")
            e.activation(ga, ga, ACT.Exp, scale=-1.0)
            e.activation(ea, vec_of("alog"), ACT.Exp).then_inc(*S_.step("ge"))
            e.drain()
            e.activation(gl, ga, ACT.Ln, bias=ones[:, 0:1]).then_inc(*S_.step("gl"))
            for zi in range(10, 26):
                e.wait_ge(m["z_ready"], ZT * l + zi + 1)
                c = zi - 10
                if c == 0:
                    w(P_, "pad")
                if c < 12:
                    e.activation(cx[:, c, 3:3 + HALF], pair[zi % 2][:, 0, 0:HALF], ACT.Copy)
                    e.activation(cx[:, c, 3 + HALF:3 + T], pair[zi % 2][:, 1, 0:T - HALF], ACT.Copy)
                    e.activation(xs[:, c, :, 3], pair[zi % 2][:, 1, T - HALF:HALF], ACT.Copy).then_inc(m["z_used"], 1)
                else:
                    e.activation(halves(dz[:, c - 12, :]), both(zi % 2), ACT.Silu).then_inc(m["z_used"], 1)
            for g in range(3):
                w(V_, f"conv{g}")
                e.activation(cy[:, 4 * g:4 * g + 4, :], cy[:, 4 * g:4 * g + 4, :], ACT.Silu).then_inc(*S_.step(f"silu{g}"))
            e.drain()
            norm_scalar(e, l, m, T_, S_, V_, "l", [cy[:, i, :] for i in range(8)], sqr, 1.0)
            for t in range(QT):
                w(V_, f"dec.{t}")
                if t:
                    w(T_, f"o.{t - 1}")
                e.activation(dec, dec, ACT.Exp)
                e.activation(eg, heads(6), ACT.Exp)
                e.activation(egc, gc, ACT.Exp)
                e.activation(ktf, ktf, ACT.Exp).then_inc(*S_.step(f"exp.{t}"))
                w(T_, f"rows.{t}")
                e.activation(vr, heads(1), ACT.Copy).then_inc(*S_.step(f"vr.{t}"))
                for i in lv:
                    w(T_, f"y{i}.{t}")
                    e.activation(yb, heads(0), ACT.Copy).then_inc(*S_.step(f"y{i}.{t}"))
                w(T_, f"vn.{t}")
                e.activation(vn, heads(3), ACT.Copy).then_inc(*S_.step(f"vn.{t}"))
                w(T_, f"o.{t}")
                e.activation(o_d[:, :, P * t:P * t + P], heads(5), ACT.Copy).then_inc(*S_.step(f"o.{t}"))
            w(T_, "sk")
            e.activation(egs, bank(7)[:, 0:32], ACT.Exp).then_inc(*S_.step("seg"))
            state_scalar(e, l, m, T_, S_, o_d, (5, 6, 0))
            e.drain()
            norm_scalar(e, l, m, T_, S_, V_, "o", [o_d[:, i, :] for i in range(4)], sqr, 1.0 / P)

        def vector(self, e, l):
            def w(steps, n):
                e.wait_ge(steps.sem, steps.at(n, l))

            def v3(ap, n=5):
                return ap.rearrange("p (t h) -> p t h", t=n)

            w(P_, "pad")
            e.tensor_tensor(v3(gx), m["small"][:, :].rearrange("p (t n) -> p t n", t=5)[:, :, 28:32],
                            vec_of("dtb").unsqueeze(1).to_broadcast([P, 5, 4]), ALU.add)
            e.drain()
            e.scalar_tensor_tensor(ga, gx, -1.0, gx, ALU.mult, ALU.max).then_inc(*V_.step("ga"))
            e.wait_ge(conv_in, 16 * (l + 1))
            e.tensor_copy(xs[:, :, :, 0:3], cin.rearrange("p (c b j) -> p c b j", c=12, b=B)).then_inc(*V_.step("cin"))
            e.drain()
            cw = vec_of("conv").rearrange("p (c j) -> p c j", j=4)
            for g in range(3):
                e.wait_ge(m["z_used"], ZT * l + 10 + 4 * g + 4)
                for j in range(4):
                    for c in range(4 * g, 4 * g + 4):
                        if j == 0:
                            e.tensor_scalar(cy[:, c, 0:T], cx[:, c, 0:T], cw[:, c, 0:1], None, ALU.mult)
                        else:
                            e.scalar_tensor_tensor(cy[:, c, 0:T], cx[:, c, j:j + T], cw[:, c, j:j + 1], cy[:, c, 0:T],
                                                   ALU.mult, ALU.add)
                    if j == 0:
                        e.tensor_tensor(xw, xs[:, 4 * g:4 * g + 4], cw[:, 4 * g:4 * g + 4, :].unsqueeze(2)
                                        .to_broadcast([P, 4, B, 4]), ALU.mult)
                    if j == 2:
                        e.tensor_reduce(cy[:, 4 * g:4 * g + 4, T:N], xw, AX_X, ALU.add)
                    e.drain() if j < 3 else e.drain().then_inc(*V_.step(f"conv{g}"))
            e.tensor_copy(cout[:, 36:324].rearrange("p (c b j) -> p c b j", c=12, b=B), xs[:, :, :, 1:4])
            e.tensor_copy(cout[:, 0:36].rearrange("p (c j) -> p c j", c=12), cx[:, :, T:T + 3])
            w(S_, "gl")
            e.tensor_scalar(gx, gx, 0.0, None, ALU.max)
            e.drain()
            e.tensor_tensor(gx, gx, gl, ALU.add)
            e.drain()
            e.scalar_tensor_tensor(v3(gd), v3(gx), -1.0, ea.unsqueeze(1).to_broadcast([P, 5, 4]),
                                   ALU.mult, ALU.mult).then_inc(*V_.step("g"))
            e.memset(S, 0.0)
            norm_vector(e, l, m, S_, V_, "l", [cy[:, i, :] for i in range(8)],
                        lambda i: P ** -0.5 if i < 4 else 1.0, lambda i: None)
            for t in range(QT):
                k4 = slice(P * t, P * t + P)
                w(T_, f"gb.{t}")
                e.tensor_copy(gc, bank(7)[:, 0:4])
                e.drain()
                for h in range(4):
                    e.tensor_scalar(dec[:, h, :], heads(6)[:, h, :], gc[:, h:h + 1], 0.0, ALU.subtract, ALU.min)
                e.tensor_tensor(ktf, heads(6)[:, :, P - 1], gc, ALU.subtract)
                e.drain().then_inc(*V_.step(f"dec.{t}"))
                w(S_, f"exp.{t}")
                e.tensor_tensor(dec, dec, each_head(upper), ALU.mult)
                e.tensor_scalar(neg, egc, -1.0, None, ALU.mult)
                e.drain()
                w(T_, f"kk.{t}")
                e.tensor_tensor(lt, heads(4), dec, ALU.mult)
                e.tensor_tensor(at_, heads(3), dec, ALU.mult)
                e.drain()
                e.tensor_tensor(lt, lt, heads(5), ALU.mult).then_inc(*V_.step(f"lt.{t}"))
                e.tensor_tensor(qt, cy[:, 0:4, k4], eg, ALU.mult).then_inc(*V_.step(f"qt.{t}"))
                w(T_, f"rows.{t}")
                e.tensor_tensor(ktl, heads(2), cols(ktf), ALU.mult).then_inc(*V_.step(f"kt.{t}"))
                w(T_, f"y0.{t}")
                e.tensor_tensor(ta, each_head(ident), heads(0), ALU.subtract)
                e.tensor_tensor(tb, each_head(ident), ls[0], ALU.subtract)
                e.drain().then_inc(*V_.step(f"t0.{t}"))
                for i in lv:
                    w(T_, f"ty{i}.{t}")
                    if i < 6:
                        e.tensor_tensor(ta, ta, heads(6), ALU.subtract)
                    e.tensor_tensor(tb, tb, heads(7), ALU.subtract)
                    e.drain().then_inc(*V_.step(f"t{i}.{t}"))
                w(T_, f"ks.{t}")
                w(S_, f"vr.{t}")
                for h in range(4):
                    e.scalar_tensor_tensor(rb[:, h, :], heads(4)[:, h, :], neg[:, h:h + 1], vr[:, h, :],
                                           ALU.mult, ALU.add)
                e.drain()
                e.tensor_tensor(rb, rb, cols(gate_tile(gate, t)[:, 24:28]), ALU.mult).then_inc(*V_.step(f"r.{t}"))
                w(T_, f"s.{t}")
                for h in range(4):
                    e.scalar_tensor_tensor(S[:, h, :], S[:, h, :], eg[:, h, P - 1:P], heads(4)[:, h, :],
                                           ALU.mult, ALU.add)
                e.drain().then_inc(*V_.step(f"s.{t}"))
            w(S_, "seg")
            v32 = vns.rearrange("p (h b) -> p h b", h=4)
            e.tensor_tensor(vns, bank(7)[:, 64:96], egs, ALU.mult)
            e.drain()
            e.tensor_tensor(v32, cy[:, 8:12, T:N], v32, ALU.subtract)
            e.drain()
            e.tensor_tensor(vns, vns, bank(7)[:, 32:64], ALU.mult).then_inc(*V_.step("svn"))
            state_vector(e, l, m, T_, V_, ss, egs, cy[:, 4:8], tmp, (5, 6, 0))
            norm_vector(e, l, m, S_, V_, "o", [o_d[:, i, :] for i in range(4)],
                        lambda i: scalar_of("dng"), lambda i: dz[:, i, :])

    p = Plan()
    p.saved, p.T_, p.S_, p.V_ = saved, T_, S_, V_
    return p


def hgrn_plan(m):
    part, sem, bank, pair, both, halves = m["part"], m["sem"], m["bank"], m["pair"], m["both"], m["halves"]
    scalar_of, ident, ones, level, o_h = m["scalar_of"], m["ident"], m["ones"], m["level"], m["o_h"]

    lf, kin, q, vT, og, gc, ex, qk = (part(4 * N * i, 4 * N, 4) for i in range(8))
    am = part(0, 2048).rearrange("p (t h n) -> p t h n", t=QT, h=4)
    qt = vT
    ktr = part(16640, 2048).rearrange("p (t h n) -> p t h n", t=QT, h=4)
    vr = part(18688, 2048).rearrange("p (t h n) -> p t h n", t=QT, h=4)
    ss = part(20736, 32 * P, 32)
    S = part(24832, 512, 4)
    fs = part(25344, 32)
    egl = part(25376, 16, 4)
    lbc = part(25392, 4)
    oml = part(25396, 4)
    tmp = part(4 * N * 5, 1024, 2)
    sqr = part(4 * N * 6, 2 * N, 2)
    scan = m["const_of"]("scanmask")
    i32 = [level[:, i, :].bitcast(I32).unsqueeze(1).to_broadcast([P, 4, P]) for i in range(7)]

    st_t, st_s, st_v = state_steps("h")
    o_t, o_s, o_v = norm_steps("o", 4)
    T_ = Steps(sem("hgrn_tensor_step"), ["vrows", "ktr", "ad"] + [f"a{i}" for i in range(7)]
               + [n + str(t) for t in range(QT) for n in ("o", "s")] + st_t + o_t)
    S_ = Steps(sem("hgrn_scalar_step"), ["z", "ln", "e0", "vr", "ke", "ktr"] + [f"e{i}" for i in range(1, 8)]
               + [f"o{t}" for t in range(QT)] + st_s + o_s)
    V_ = Steps(sem("hgrn_vector_step"), ["f", "scan", "ka", "kt", "ad"]
               + ["arg0"] + [n for i in range(7) for n in ([f"qk{i}"] + [f"arg{i + 1}"] * (i < 6) + [f"a{i}"])]
               + [f"s{t}" for t in range(QT)] + st_v + o_v)
    states_in, saved = sem("hgrn_states_loaded"), sem("hgrn_outputs_saved")

    def halves_of(ap, n):
        return ap[:, :, 0:T].rearrange("p h (b s n) -> p h b s n", s=2, n=n)

    class Plan:
        def pool(self, e, l):
            e.wait_ge(D_saved, 64 * (l + 1))
            e.wait_ge(m["D"].V_.sem, m["D"].V_.at("on3", l))
            e.sem_inc(m["turns"], 1)
            e.dma_start(ss, m["ins"]["hg_in"][l].rearrange("p (i n) -> p i n", i=32)).then_inc(states_in, 16)
            e.wait_ge(V_.sem, V_.at("sa7", l))
            e.sem_inc(m["turns"], 1)
            e.dma_start(m["outs"]["hg_p"][l].rearrange("p (h n) -> p h n", h=4), S).then_inc(saved, 16)
            e.dma_start(m["outs"]["hg_s"][l].rearrange("p (i n) -> p i n", i=32), ss).then_inc(saved, 16)

        def tensor(self, pe, l):
            def w(steps, n):
                pe.wait_ge(steps.sem, steps.at(n, l))

            def tile(ap, t, h):
                return ap[:, h, P * t:P * t + P]

            w(S_, "z")
            for t in range(QT):
                for h in range(4):
                    mm = pe.transpose(bank(t)[:, P * h:P * h + P], tile(vT, t, h), ident)
            mm.then_inc(*T_.step("vrows"))
            w(V_, "kt")
            for t in range(QT):
                for h in range(4):
                    mm = pe.transpose(bank(4 + t)[:, P * h:P * h + P], tile(qk, t, h), ident)
            mm.then_inc(*T_.step("ktr"))
            w(S_, "vr")
            for t in range(QT):
                for h in range(4):
                    mm = pe.matmul(bank(t)[:, P * h:P * h + P], tile(kin, t, h), tile(q, t, h), start=True, stop=True)
            mm.then_inc(*T_.step("ad"))
            w(S_, "ktr")
            for i in range(7):
                w(V_, f"qk{i}")
                if i:
                    w(V_, f"a{i - 2}" if i >= 2 else "ad")
                for t in range(QT):
                    for h in range(4):
                        mm = pe.matmul(bank(4 * (1 - i % 2) + t)[:, P * h:P * h + P], tile(qk, t, h), tile(qk, t, h),
                                       start=True, stop=True)
                mm.then_inc(*T_.step(f"a{i}"))
            w(V_, "a6")
            for t in range(QT):
                if t:
                    w(V_, f"s{t - 1}")
                    w(S_, f"o{t - 1}")
                for h in range(4):
                    pe.matmul(bank(4)[:, P * h:P * h + P], S[:, h, :], tile(qt, t, h), start=True, stop=False)
                    mm = pe.matmul(bank(4)[:, P * h:P * h + P], vr[:, t, h, :], am[:, t, h, :], start=False, stop=True)
                mm.then_inc(*T_.step(f"o{t}"))
                for h in range(4):
                    mm = pe.matmul(bank(5)[:, P * h:P * h + P], ktr[:, t, h, :], vr[:, t, h, :], start=True, stop=True)
                mm.then_inc(*T_.step(f"s{t}"))
            w(S_, "o3")
            state_tensor(pe, l, m, T_, V_, S_, ss, lambda i: vT[:, i // 8, T + i % 8:T + i % 8 + 1], q, (1, 2, 0))
            norm_tensor(pe, l, m, T_, S_, "o", 4, sqr)

        def wait_mixed(self, pe, l):
            pe.wait_ge(V_.sem, V_.at("on3", l))

        def scalar(self, e, l):
            def w(steps, n):
                e.wait_ge(steps.sem, steps.at(n, l))

            for zi in range(26, 42):
                e.wait_ge(m["z_ready"], ZT * l + zi + 1)
                c, src = (zi - 26) % 4, both(zi % 2)
                if zi == 26:
                    e.wait_ge(D_saved, 64 * (l + 1))
                    w(m["D"].V_, "on3")
                if zi < 30:
                    e.activation(halves(lf[:, c, :]), src, ACT.Sigmoid)
                    e.activation(halves(kin[:, c, :]), src, ACT.Sigmoid, scale=-1.0).then_inc(m["z_used"], 1)
                else:
                    dst, f = ((vT, ACT.Copy), (q, ACT.Silu), (og, ACT.Sigmoid))[(zi - 30) // 4]
                    e.activation(halves(dst[:, c, :]), src, f).then_inc(m["z_used"], 1)
            e.drain().then_inc(*S_.step("z"))
            w(V_, "f")
            e.activation(lf, lf, ACT.Ln).then_inc(*S_.step("ln"))
            w(V_, "scan")
            e.activation(ex[:, :, 0:T], gc[:, :, 0:T], ACT.Exp).then_inc(*S_.step("e0"))
            w(T_, "vrows")
            for t in range(QT):
                a = e.activation(vr[:, t, :, :], bank(t).rearrange("p (h n) -> p h n", h=4), ACT.Copy)
            a.then_inc(*S_.step("vr"))
            w(V_, "ka")
            e.activation(qk[:, :, 0:T], qk[:, :, 0:T], ACT.Exp).then_inc(*S_.step("ke"))
            w(T_, "ktr")
            for t in range(QT):
                a = e.activation(ktr[:, t, :, :], bank(4 + t).rearrange("p (h n) -> p h n", h=4), ACT.Copy)
            a.then_inc(*S_.step("ktr"))
            for i in range(7):
                w(V_, f"arg{i}")
                e.activation(ex[:, :, 0:T], ex[:, :, 0:T], ACT.Exp).then_inc(*S_.step(f"e{i + 1}"))
            for t in range(QT):
                w(T_, f"o{t}")
                e.activation(o_h[:, :, P * t:P * t + P], bank(4).rearrange("p (h n) -> p h n", h=4),
                             ACT.Copy).then_inc(*S_.step(f"o{t}"))
            state_scalar(e, l, m, T_, S_, o_h, (1, 2, 0))
            e.drain()
            norm_scalar(e, l, m, T_, S_, V_, "o", [o_h[:, i, :] for i in range(4)], sqr, 1.0 / P)

        def vector(self, e, l):
            def w(steps, n):
                e.wait_ge(steps.sem, steps.at(n, l))

            e.wait_ge(D_saved, 64 * (l + 1))
            e.tensor_copy(lbc, m["lb"][:, bass.DynSlice(4 * l, 4)])
            e.drain()
            e.tensor_scalar(oml, lbc, -1.0, 1.0, ALU.mult, ALU.add)
            e.drain()
            w(S_, "z")
            for c in range(4):
                e.tensor_scalar(lf[:, c, :], lf[:, c, :], oml[:, c:c + 1], lbc[:, c:c + 1], ALU.mult, ALU.add)
                e.tensor_scalar(kin[:, c, :], kin[:, c, :], oml[:, c:c + 1], None, ALU.mult)
            e.drain()
            e.tensor_scalar(lf, lf, 1e-18, None, ALU.max)
            e.tensor_scalar(q, q, P ** -0.5, None, ALU.mult)
            e.drain()
            e.tensor_copy(fs.rearrange("p (h b) -> p h b", h=4), lf[:, :, T:N]).then_inc(*V_.step("f"))
            w(S_, "ln")
            for c in range(4):
                e.tensor_tensor_scan(gc[:, c, 0:T], scan, lf[:, c, 0:T], 0.0, ALU.mult, ALU.add)
            e.memset(S, 0.0)
            e.drain().then_inc(*V_.step("scan"))
            ends = gc[:, :, 0:T].rearrange("p h (t n) -> p h t n", t=QT)
            e.tensor_tensor(qk[:, :, 0:T].rearrange("p h (t n) -> p h t n", t=QT),
                            ends[:, :, :, P - 1:P].to_broadcast([P, 4, QT, P]), ends, ALU.subtract).then_inc(*V_.step("ka"))
            w(S_, "e0")
            e.tensor_copy(egl, ex[:, :, P - 1:T:P])
            w(S_, "vr")
            e.tensor_tensor(qt[:, :, 0:T], q[:, :, 0:T], ex[:, :, 0:T], ALU.mult)
            w(S_, "ke")
            e.tensor_tensor(qk[:, :, 0:T], qk[:, :, 0:T], kin[:, :, 0:T], ALU.mult).then_inc(*V_.step("kt"))
            w(T_, "ad")
            for t in range(QT):
                d = e.tensor_tensor(am[:, t, :, :], bank(t).rearrange("p (h n) -> p h n", h=4),
                                    ident.unsqueeze(1).to_broadcast([P, 4, P]), ALU.mult)
            d.then_inc(*V_.step("ad"))

            def argument(i):
                n = 1 << i
                g5, e5 = halves_of(gc, n), halves_of(ex, n)
                for h in range(4):
                    r = g5[:, h, :, 0, n - 1:n].to_broadcast([P, T // (2 * n), n])
                    e.tensor_tensor(e5[:, h, :, 1, :], g5[:, h, :, 1, :], r, ALU.subtract)
                    d = e.tensor_tensor(e5[:, h, :, 0, :], r, g5[:, h, :, 0, :], ALU.subtract)
                return d

            argument(0).then_inc(*V_.step("arg0"))
            for i in range(7):
                n = 1 << i
                w(S_, f"e{i + 1}")
                w(T_, f"a{i - 1}" if i else "ktr")
                e5, k5, q5, o5 = (halves_of(a, n) for a in (ex, kin, q, qk))
                e.tensor_tensor(o5[:, :, :, 1, :], q5[:, :, :, 1, :], e5[:, :, :, 1, :], ALU.mult)
                e.tensor_tensor(o5[:, :, :, 0, :], k5[:, :, :, 0, :], e5[:, :, :, 0, :],
                                ALU.mult)
                e.drain().then_inc(*V_.step(f"qk{i}"))
                if i < 6:
                    argument(i + 1).then_inc(*V_.step(f"arg{i + 1}"))
                w(T_, f"a{i}")
                e.sem_inc(m["turns"], 1)
                for t in range(QT):
                    d = e.copy_predicated(am[:, t, :, :], i32[i],
                                          bank(4 * (1 - i % 2) + t).rearrange("p (h n) -> p h n", h=4))
                d.then_inc(*V_.step(f"a{i}"))
            for t in range(QT):
                w(T_, f"s{t}")
                for h in range(4):
                    e.scalar_tensor_tensor(S[:, h, :], S[:, h, :], egl[:, h, t:t + 1], bank(5)[:, P * h:P * h + P],
                                           ALU.mult, ALU.add)
                e.drain().then_inc(*V_.step(f"s{t}"))
            e.wait_ge(states_in, 16 * (l + 1))
            state_vector(e, l, m, T_, V_, ss, fs, kin, tmp, (1, 2, 0))
            norm_vector(e, l, m, S_, V_, "o", [o_h[:, i, :] for i in range(4)],
                        lambda i: scalar_of("hgg"), lambda i: og[:, i, :])
            e.wait_ge(saved, 32 * (l + 1))
            e.sem_inc(m["turns"], 1)

    D_saved = m["D"].saved
    return Plan()


def hybrid_step_kernel(nc, ins, outs):
    ctx = ExitStack()
    with ctx:
        def sb(name, width, parts=P):
            return ctx.enter_context(nc.sbuf_tensor(name, [parts, width], F32))

        def sem(name):
            return ctx.enter_context(nc.semaphore(name))

        def blocks(ap, n):
            return ap.rearrange("p (k n) -> p k n", k=n)

        def halves(ap):
            return ap.rearrange("p (a n) -> p a n", a=2)

        x = blocks(sb("x", KD * N)[:, :], KD)
        h = blocks(sb("h", KD * N)[:, :], KD)
        ring = [blocks(sb(f"slot{i}", SLOT * P)[:, :], SLOT) for i in range(4)]
        const = sb("const", NCONST)
        vecs = sb("vecs", L * NVEC)
        vec = sb("vec", NVEC)
        lbl = sb("lbl", 8)
        lbw = sb("lbw", 24)
        lb = sb("lb", 8)
        eps = sb("eps", 1)
        rstd = sb("rstd", 2 * N)
        mixed = sb("mixed", 12 * N)
        o_a, o_d, o_h = (blocks(mixed[:, i * 4 * N:(i + 1) * 4 * N], 4) for i in range(3))
        small = sb("small", 5 * 32)
        gate = sb("gate", 5 * 28)
        pages = ctx.enter_context(nc.sbuf_tensor("page_ids", [1, B * PAGES], I32))
        ARENA = 26340
        arena = sb("arena", ARENA)

        def part(at, width, n=None, parts=P):
            assert at + width <= ARENA
            ap = arena[0:parts, at:at + width]
            return ap if n is None else blocks(ap, n)

        def const_of(name, parts=P):
            o, w = CONST[name]
            return const[0:parts, o:o + w]

        ident, ones, bones, upper = (const_of(n) for n in ("ident", "ones", "bones", "upper"))
        level = blocks(const_of("level"), 7)
        dist = const_of("dist")

        def vec_of(name):
            o, w = VEC[name]
            return vec[:, o:o + w]

        def scalar_of(name, i=0, parts=P):
            o, _ = VEC[name]
            return vec[0:parts, o + i:o + i + 1]

        pair = [ctx.enter_context(nc.psum_tensor(f"pair{i}", [P, 2, 512], F32)) for i in range(4)]

        def bank(i):
            return pair[i // 2][:, i % 2, :]

        def both(i):
            return pair[i][:, :, 0:HALF]

        act = part(0, FC * N, FC)
        sq = part(FC * N, KD * N, KD)
        sg = part(FC * N + KD * N, 4 * HALF, 4)
        merged = part(0, KD * N, KD)
        mgate = part(KD * N, 2 * N, 2)
        mprod = part((KD + 2) * N, 2 * N, 2)

        loaded = sem("constants_loaded")
        x_loaded = sem("x_loaded")
        setup = sem("setup_done")
        landed = [sem(f"slot{i}_landed") for i in range(4)]
        slot_free = [sem(f"slot{i}_free") for i in range(4)]
        vec_ready = sem("layer_vectors_ready")
        x_done = sem("x_block_done")
        sq_done = sem("x_block_squared")
        ss_done = sem("norm_sum_done")
        std_done = sem("norm_std_done")
        h_done = sem("h_block_done")
        gu_ready = sem("gate_up_ready")
        silu_done = sem("silu_done")
        gu_free = sem("gate_up_used")
        proj_ready = sem("projection_ready")
        z_ready = sem("z_block_ready")
        z_used = sem("z_block_used")
        small_ready = sem("small_ready")
        mg_ready = sem("merge_product_ready")
        mg_gate = sem("merge_gate_done")
        mg_used = sem("merge_product_used")
        y_stored = sem("y_stored")
        turns = sem("waits_passed")
        lbx = sem("lower_bound_step")

        env = dict(bank=bank, bones=bones, both=both, const_of=const_of, dist=dist, eps=eps, gate=gate,
                   h_done=h_done, halves=halves, ident=ident, ins=ins, lb=lb, level=level, mixed=mixed,
                   o_a=o_a, o_d=o_d, o_h=o_h, ones=ones, outs=outs, pages=pages, pair=pair, part=part,
                   rstd=rstd, scalar_of=scalar_of, sem=sem, small=small, small_ready=small_ready, turns=turns,
                   upper=upper, vec=vec, vec_of=vec_of, x_done=x_done, z_ready=z_ready, z_used=z_used)
        A = env["A"] = attention_plan(env)
        D = env["D"] = delta_plan(env)
        G = hgrn_plan(env)
        block = ctx.enter_context(nc.Block())

        @block.sync
        def _(sp):
            sp.dma_start(x, ins["x"]).then_inc(x_loaded, 16)
            sp.dma_start(const[:, :], ins["const"]).then_inc(loaded, 16)
            sp.dma_start(vecs[:, :].rearrange("p (l n) -> p l n", l=L),
                         ins["vec"].rearrange("l p n -> p l n")).then_inc(loaded, 16)
            sp.dma_start(lbl[:, :], ins["lb"]).then_inc(loaded, 16)
            sp.dma_start(pages[:, :], ins["pages"]).then_inc(loaded, 16)

            def tile(s, use, src, k):
                sp.wait_ge(slot_free[s], use + 1)
                sp.dma_start(ring[s][:, 0:k, :], src.rearrange("a p (k n) -> p (a k) n", k=k)).then_inc(landed[s], 16)

            with sp.Fori(0, L) as l:
                def ffn(f, at):
                    with sp.Fori(0, FC // 2) as r:
                        for s in range(4):
                            tile(s, l * SLOT_USES[s] + at + r,
                                 ins["w_up"][2 * l + f, bass.DynSlice(4 * r + s, 1)], KD)
                    with sp.Fori(0, KD // 2) as r:
                        for s in range(4):
                            tile(s, l * SLOT_USES[s] + at + FC // 2 + r,
                                 ins["w_dn"][2 * l + f, bass.DynSlice(4 * r + s, 1)], KF)

                ffn(0, 0)
                for z in range(43):
                    i = z if z < 11 else z + 1
                    s, use = i % 4, l * SLOT_USES[i % 4] + 15 + i // 4 - (1 if i % 4 == 3 and i > 11 else 0)
                    if z == 10:
                        sp.wait_ge(slot_free[s], use + 1)
                        sp.dma_start(ring[s][:, 0:KD, 0:32], ins["w_sm"][bass.DynSlice(l, 1)].rearrange(
                            "a p (k n) -> p (a k) n", k=KD)).then_inc(landed[s], 16)
                    else:
                        zi = z if z < 10 else z - 1
                        tile(s, use, ins["w_z"][l, zi:zi + 1], KD)
                with sp.Fori(0, 6) as r:
                    for s in range(4):
                        tile(s, l * SLOT_USES[s] + (26 if s < 3 else 25) + r,
                             ins["w_mg"][l, bass.DynSlice(4 * r + s, 1)], SLOT)
                with sp.Fori(0, 2) as r:
                    for s in range(4):
                        tile(s, l * SLOT_USES[s] + (32 if s < 3 else 31) + r,
                             ins["w_out"][l, bass.DynSlice(4 * r + s, 1)], KD)
                for s in range(4):
                    assert SLOT_USES[s] == (34 if s < 3 else 33) + 15
                with sp.Fori(0, FC // 2) as r:
                    for s in range(4):
                        tile(s, l * SLOT_USES[s] + (34 if s < 3 else 33) + r,
                             ins["w_up"][2 * l + 1, bass.DynSlice(4 * r + s, 1)], KD)
                with sp.Fori(0, KD // 2) as r:
                    for s in range(4):
                        tile(s, l * SLOT_USES[s] + (45 if s < 3 else 44) + r,
                             ins["w_dn"][2 * l + 1, bass.DynSlice(4 * r + s, 1)], KF)
            sp.wait_ge(x_done, 8 * (3 * L + 1))
            sp.dma_start(outs["y"].rearrange("p (k n) -> p k n", k=KD), x).then_inc(y_stored, 16)
            sp.wait_ge(y_stored, 16)

        @block.tensor
        def _(pe):
            for s in range(4):
                pe.sem_inc(slot_free[s], 1)
            pe.wait_ge(loaded, 64)

            def use_of(l, s, at):
                return 16 * (l * SLOT_USES[s] + at + 1)

            def norm(l, s):
                for k in range(KD):
                    pe.wait_ge(sq_done, 8 * (3 * l + s) + k + 1)
                    for a in range(2):
                        mm = pe.matmul(pair[3][:, a, 0:HALF], ones, sq[:, k, a * HALF:(a + 1) * HALF],
                                       start=(k == 0), stop=(k == KD - 1), skip_group_check=True)
                mm.then_inc(ss_done, 1)

            def ffn(l, f, at):
                with pe.Fori(0, FC // 2) as r:
                    pe.wait_ge(h_done, 8 * (3 * l + 2 * f + 1))
                    for j in range(2):
                        pe.wait_ge(landed[2 * j], use_of(l, 2 * j, at[2 * j] + r))
                        pe.wait_ge(landed[2 * j + 1], use_of(l, 2 * j + 1, at[2 * j + 1] + r))
                        for a in range(2):
                            q = 2 * j + a
                            pe.wait_ge(gu_free, 44 * (2 * l + f) + 4 * r + q + 1)
                            for gu in range(2):
                                for k in range(KD):
                                    mm = pe.matmul(pair[q][:, gu, 0:HALF], ring[2 * j + gu][:, k, :],
                                                   h[:, k, a * HALF:(a + 1) * HALF],
                                                   start=(k == 0), stop=(k == KD - 1))
                                if a == 1 and gu == 0:
                                    mm.then_inc(slot_free[2 * j], 1)
                            mm.then_inc(gu_ready, 1)
                        pe.drain().then_inc(slot_free[2 * j + 1], 1)
                with pe.Fori(0, KD // 2) as r:
                    pe.wait_ge(gu_free, 44 * (2 * l + f + 1) + 4)
                    for j in range(2):
                        for q in (2 * j, 2 * j + 1):
                            pe.wait_ge(landed[q], use_of(l, q, at[q] + FC // 2 + r))
                        pe.wait_ge(x_done, 8 * (3 * l + 2 * f) + 2 * r + j + 7)
                        for a in range(2):
                            for k in range(FC):
                                mm = pe.matmul(pair[j][:, a, 0:HALF], ring[2 * j + k // KF][:, k % KF, :],
                                               act[:, k, a * HALF:(a + 1) * HALF],
                                               start=(k == 0), stop=(k == FC - 1))
                                if a == 1 and k == KF - 1:
                                    mm.then_inc(slot_free[2 * j], 1)
                        mm.then_inc(proj_ready, 1)
                        pe.drain().then_inc(slot_free[2 * j + 1], 1)

            def z_block(l, zi):
                z = zi if zi < 10 else zi + 1
                i = z if z < 11 else z + 1
                s, use = i % 4, 15 + i // 4 - (1 if i % 4 == 3 and i > 11 else 0)
                pe.wait_ge(landed[s], use_of(l, s, use))
                if zi >= 2:
                    pe.wait_ge(z_used, ZT * l + zi - 1)
                for a in range(2):
                    for k in range(KD):
                        mm = pe.matmul(pair[zi % 2][:, a, 0:HALF], ring[s][:, k, :], h[:, k, a * HALF:(a + 1) * HALF],
                                       start=(k == 0), stop=(k == KD - 1))
                mm.then_inc(z_ready, 1)
                pe.drain().then_inc(slot_free[s], 1)

            def z_small(l):
                pe.wait_ge(landed[2], use_of(l, 2, 17))
                pe.wait_ge(z_used, ZT * l + 9)
                for t in range(5):
                    w = P if t < 4 else B
                    for k in range(KD):
                        mm = pe.matmul(bank(0)[0:w, 32 * t:32 * t + 32], h[:, k, P * t:P * t + w], ring[2][:, k, 0:32],
                                       start=(k == 0), stop=(k == KD - 1))
                mm.then_inc(small_ready, 1)
                pe.drain().then_inc(slot_free[2], 1)

            def merge(l):
                for i, o in enumerate((o_a, o_d, o_h)):
                    with pe.Fori(0, 2) as r:
                        G.wait_mixed(pe, l)
                        for s in range(4):
                            at = (26 if s < 3 else 25) + 2 * i
                            pe.wait_ge(landed[s], use_of(l, s, at + r))
                            p = s % 2
                            pe.wait_ge(mg_used, 24 * l + 8 * i + 4 * r + s + 1)
                            for a in range(2):
                                for k in range(KD):
                                    pe.matmul(pair[2 * p][:, a, 0:HALF], ring[s][:, k, :],
                                              h[:, k, a * HALF:(a + 1) * HALF], start=(k == 0), stop=(k == KD - 1))
                                for k in range(4):
                                    mm = pe.matmul(pair[2 * p + 1][:, a, 0:HALF], ring[s][:, KD + k, :],
                                                   o[:, k, a * HALF:(a + 1) * HALF], start=(k == 0), stop=(k == 3))
                            mm.then_inc(mg_ready, 1)
                            pe.drain().then_inc(slot_free[s], 1)
                with pe.Fori(0, 2) as r:
                    pe.wait_ge(mg_used, 24 * (l + 1) + 2)
                    for s in range(4):
                        at = 32 if s < 3 else 31
                        pe.wait_ge(landed[s], use_of(l, s, at + r))
                        pe.wait_ge(x_done, 8 * (3 * l + 1) + 4 * r + s + 7)
                        for a in range(2):
                            for k in range(KD):
                                mm = pe.matmul(pair[s % 2][:, a, 0:HALF], ring[s][:, k, :],
                                               merged[:, k, a * HALF:(a + 1) * HALF],
                                               start=(k == 0), stop=(k == KD - 1))
                        mm.then_inc(proj_ready, 1)
                        pe.drain().then_inc(slot_free[s], 1)

            with pe.Fori(0, L) as l:
                norm(l, 0)
                ffn(l, 0, (0, 0, 0, 0))
                norm(l, 1)
                pe.wait_ge(h_done, 8 * (3 * l + 2))
                for zi in range(10):
                    z_block(l, zi)
                z_small(l)
                A.tensor(pe, l)
                for zi in range(10, 26):
                    z_block(l, zi)
                D.tensor(pe, l)
                for zi in range(26, 42):
                    z_block(l, zi)
                G.tensor(pe, l)
                merge(l)
                norm(l, 2)
                ffn(l, 1, (34, 34, 34, 33))

        @block.scalar
        def _(act_e):
            act_e.wait_ge(setup, 1)
            act_e.wait_ge(lbx, 1)
            act_e.activation(lbw[:, 4:12], lbw[:, 4:12], ACT.Exp).then_inc(lbx, 1)

            def norm(l, s):
                for k in range(KD):
                    act_e.wait_ge(x_done, 8 * (3 * l + s) + k + 1)
                    act_e.activation(sq[:, k, :], x[:, k, :], ACT.Square).then_inc(sq_done, 1)
                act_e.wait_ge(ss_done, 3 * l + s + 1)
                act_e.activation(halves(rstd[:, 0:N]), both(3), ACT.Sqrt, bias=eps[:, :],
                                 scale=1.0 / (KD * P)).then_inc(std_done, 1)

            def ffn(l, f):
                with act_e.Fori(0, FC // 2) as r:
                    for q in range(4):
                        act_e.wait_ge(gu_ready, 44 * (2 * l + f) + 4 * r + q + 1)
                        act_e.wait_ge(gu_free, 44 * (2 * l + f) + 4 * r + q + 1)
                        act_e.activation(sg[:, q, :], pair[q][:, 0, 0:HALF], ACT.Silu).then_inc(silu_done, 1)

            def merge(l):
                with act_e.Fori(0, 12) as r:
                    for j in range(2):
                        act_e.wait_ge(mg_ready, 24 * l + 2 * r + j + 1)
                        act_e.wait_ge(mg_used, 24 * l + 2 * r + j + 1)
                        act_e.activation(halves(mgate[:, j, :]), both(2 * j), ACT.Sigmoid).then_inc(mg_gate, 1)

            with act_e.Fori(0, L) as l:
                norm(l, 0)
                ffn(l, 0)
                norm(l, 1)
                A.scalar(act_e, l)
                D.scalar(act_e, l)
                G.scalar(act_e, l)
                merge(l)
                norm(l, 2)
                ffn(l, 1)

        @block.vector
        def _(dve):
            dve.memset(eps[:, :], EPS)
            dve.memset(small[:, :], 0.0).then_inc(setup, 1)
            dve.sem_inc(gu_free, 4)
            dve.sem_inc(mg_used, 2)
            dve.wait_ge(loaded, 64)
            a0, a1 = lbl[:, 0:4], lbl[:, 4:8]
            mx, e0, e1, r0 = (lbw[:, 4 * i:4 * i + 4] for i in range(4))
            dve.tensor_tensor(mx, a0, a1, ALU.max)
            dve.drain()
            dve.tensor_tensor(e0, a0, mx, ALU.subtract)
            dve.tensor_tensor(e1, a1, mx, ALU.subtract)
            dve.drain().then_inc(lbx, 1)
            dve.wait_ge(lbx, 2)
            dve.tensor_tensor(r0, e0, e1, ALU.add)
            dve.drain()
            dve.reciprocal(mx, r0)
            dve.drain()
            dve.tensor_tensor(e0, e0, mx, ALU.mult)
            dve.tensor_tensor(e1, e1, mx, ALU.mult)
            dve.drain()
            dve.tensor_tensor(lb[:, 0:4], e0, e0, ALU.subtract)
            dve.tensor_tensor(r0, e0, e1, ALU.add)
            dve.drain()
            dve.tensor_tensor(lb[:, 4:8], r0, e0, ALU.subtract)
            dve.wait_ge(x_loaded, 16)
            dve.sem_inc(x_done, 8)

            def norm(l, s, gain):
                dve.wait_ge(std_done, 3 * l + s + 1)
                dve.reciprocal(rstd[:, 0:N], rstd[:, 0:N])
                dve.drain()
                for k in range(KD):
                    dve.scalar_tensor_tensor(h[:, k, :], x[:, k, :], scalar_of(gain, k), rstd[:, 0:N],
                                             ALU.mult, ALU.mult).then_inc(h_done, 1)

            def ffn(l, f):
                with dve.Fori(0, FC // 2) as r:
                    for q in range(4):
                        dve.wait_ge(silu_done, 44 * (2 * l + f) + 4 * r + q + 1)
                        dve.tensor_tensor(act[:, bass.DynSlice(2 * r + q // 2, 1), (q % 2) * HALF:(q % 2 + 1) * HALF],
                                          sg[:, q:q + 1, :], pair[q][:, 1:2, 0:HALF], ALU.mult).then_inc(gu_free, 1)
                residual(l, 2 * f, 0.5)

            def residual(l, s, scale):
                with dve.Fori(0, KD // 2) as r:
                    for j in range(2):
                        dve.wait_ge(proj_ready, 8 * (3 * l + s) + 2 * r + j + 1)
                        xk = x[:, bass.DynSlice(2 * r + j, 1), :].rearrange("p k (a n) -> p (k a) n", a=2)
                        dve.scalar_tensor_tensor(xk, both(j), scale, xk, ALU.mult, ALU.add).then_inc(x_done, 1)

            def merge(l):
                for i in range(3):
                    with dve.Fori(0, KD // 2) as r:
                        for j in range(2):
                            dve.wait_ge(mg_gate, 24 * l + 8 * i + 2 * r + j + 1)
                            out = merged[:, bass.DynSlice(2 * r + j, 1), :].rearrange("p k (a n) -> p (k a) n", a=2)
                            g = halves(mgate[:, j, :])
                            if i == 0:
                                dve.tensor_tensor(out, g, both(2 * j + 1), ALU.mult).then_inc(mg_used, 1)
                            else:
                                t = halves(mprod[:, j, :])
                                dve.tensor_tensor(t, g, both(2 * j + 1), ALU.mult)
                                dve.drain()
                                dve.tensor_tensor(out, out, t, ALU.add).then_inc(mg_used, 1)

            with dve.Fori(0, L) as l:
                dve.tensor_copy(vec[:, :], vecs[:, bass.DynSlice(l * NVEC, NVEC)])
                dve.drain()
                norm(l, 0, "ffn1")
                ffn(l, 0)
                norm(l, 1, "mix")
                A.vector(dve, l)
                D.vector(dve, l)
                G.vector(dve, l)
                merge(l)
                residual(l, 1, 1.0)
                norm(l, 2, "ffn2")
                ffn(l, 1)

        @block.gpsimd
        def _(pool):
            pool.wait_ge(loaded, 64)
            with pool.Fori(0, L) as l:
                A.pool(pool, l)
                D.pool(pool, l)
                G.pool(pool, l)


def _constants():
    import numpy as np
    big = np.float32(-1e30)
    c = np.zeros((P, NCONST), np.float32)

    def put(name, a):
        o, w = CONST[name]
        a = np.asarray(a, np.float32).reshape(a.shape[0], -1)
        assert a.shape[1] == w, name
        c[:a.shape[0], o:o + w] = a

    p = np.arange(P)
    put("ident", np.eye(P))
    put("ones", np.ones((P, P)))
    put("bones", (p[:, None] // HD == p[None] // HD))
    put("upper", (p[:, None] <= p[None]))
    lev = []
    for s in (1, 2, 4, 8, 16, 32, 64):
        j, i = p[:, None], p[None]
        lev.append((j // (2 * s) == i // (2 * s)) & (j % (2 * s) < s) & (i % (2 * s) >= s))
    put("level", np.stack(lev, 1))
    d = np.arange(T)[None] - (T - P) - p[:, None]
    put("dist", np.where(d <= 0, d, big))
    t, pos, n = np.arange(QT), np.arange(8), np.arange(NPB)
    d = 16 * n + 31 - P * t[None, :, None, None] - p[:, None, None, None] + 0 * pos[None, None, :, None]
    sl = np.array([slope(x) for x in range(8)])
    put("dcmp", np.where(d <= 0, d * sl[None, None, :, None], big))
    m = np.arange(64)
    d = np.concatenate([np.broadcast_to(np.arange(PAST) - PAST, (64, PAST)),
                        np.where(np.arange(B)[None] == m[:, None] // 8, 0.0, big)], 1)
    put("dsm", d * sl[m % 8][:, None])
    k = np.arange(128)
    d = np.where((k[None] // 16 == m[:, None] // 8) & (k[None] % 16 <= 14), 16 * (k[None] % 16) + 31 - PAST, big)
    put("dcs", d * sl[m % 8][:, None])
    put("sel8", (np.arange(8)[:, None] == m[None] // 8))
    put("pos8", (m[:, None] % 8 == np.arange(8)[None]))
    put("scanmask", np.broadcast_to(np.arange(T) % P != 0, (P, T)))
    put("slope64", sl[m % 8][:, None])
    return c


def _layout(v):
    import numpy as np
    v = {k: np.asarray(a) for k, a in v.items()}
    f = np.ascontiguousarray
    out = {}
    x = np.concatenate([v["x_prompt"][0], v["x_sample"][:, 0]], 0)
    out["x"] = f(x.T.reshape(KD, P, N).transpose(1, 0, 2))
    out["const"] = _constants()
    ups, downs = [], []
    for l in range(L):
        for s in ("ffn1", "ffn2"):
            w = v[s + "_w_gu"][l].reshape(KD, P, 2, FC, P)
            ups.append(w.transpose(3, 2, 1, 0, 4).reshape(2 * FC, P, KD * P))
            w = v[s + "_w_down"][l].reshape(2, KF, P, KD, P)
            downs.append(w.transpose(3, 0, 2, 1, 4).reshape(2 * KD, P, KF * P))
    out["w_up"], out["w_dn"] = f(np.stack(ups)), f(np.stack(downs))
    w = v["w_in"]
    q = w[:, :, 0:512].reshape(L, 1024, 2, 4, HD).transpose(0, 1, 3, 2, 4).reshape(L, 1024, 512)
    z = np.concatenate([q, w[:, :, 512:1280], w[:, :, 1304:2840], w[:, :, 2848:5408]], 2)
    out["w_z"] = f(z.reshape(L, KD, P, ZT, P).transpose(0, 3, 2, 1, 4).reshape(L, ZT, P, KD * P))
    g = w[:, :, 1280:1304].reshape(L, 1024, 2, 4, 3).transpose(0, 1, 4, 3, 2).reshape(L, 1024, 24)
    sm = np.concatenate([g, w[:, :, 2840:2848]], 2)
    out["w_sm"] = f(sm.reshape(L, KD, P, 32).transpose(0, 2, 1, 3).reshape(L, P, KD * 32))
    mg = w[:, :, 5408:].reshape(L, KD, P, 24, P).transpose(0, 3, 2, 1, 4)
    wb = v["w_branch"].reshape(L, 3, 512, 1024)
    wa = wb[:, 0].reshape(L, 2, 4, HD, 1024).transpose(0, 2, 1, 3, 4).reshape(L, 1, 512, 1024)
    wb = np.concatenate([wa, wb[:, 1:]], 1).reshape(L, 3, 4, P, KD, P).transpose(0, 1, 4, 3, 2, 5).reshape(L, 24, P, 4, P)
    out["w_mg"] = f(np.concatenate([mg, wb], 3).reshape(L, 24, P, SLOT * P))
    out["w_out"] = f(v["w_out"].reshape(L, KD, P, KD, P).transpose(0, 3, 2, 1, 4).reshape(L, KD, P, KD * P))
    w1 = v["nsa_cmp_w1"].transpose(0, 1, 3, 2, 4).reshape(L, 2, HD, 32 * P)
    out["w1"] = f(np.concatenate([w1, w1], 2))
    vec = np.zeros((L, P, NVEC), np.float32)

    def put(name, a):
        o, n = VEC[name]
        vec[:, :, o:o + n] = a.reshape(L, P, n)

    for s, k in (("ffn1", "ffn1_norm"), ("mix", "mix_norm"), ("ffn2", "ffn2_norm")):
        put(s, v[k].reshape(L, KD, P).transpose(0, 2, 1))
    put("conv", v["dn_conv_w"].reshape(L, 4, 12, P).transpose(0, 3, 2, 1))
    put("qg", np.concatenate([v["nsa_q_norm"]] * 2, 1))
    put("kg", np.concatenate([v["nsa_k_norm"].transpose(0, 2, 1)] * 2, 1))
    put("dng", v["dn_out_norm"])
    put("hgg", v["hg_out_norm"])
    put("alog", np.broadcast_to(v["dn_A_log"][:, None], (L, P, 4)))
    put("dtb", np.broadcast_to(v["dn_dt_bias"][:, None], (L, P, 4)))
    pe = v["nsa_cmp_pe"].transpose(0, 3, 1, 2).reshape(L, HD, 64)
    put("pe", np.concatenate([pe, pe], 1))
    put("w2", v["nsa_cmp_w2"].transpose(0, 2, 1, 3))
    out["vec"] = vec
    out["lb"] = f(v["hg_lb_logits"].reshape(L, 4, P).transpose(2, 0, 1).reshape(P, 8))
    out["pages"] = f(v["page_table"].reshape(1, B * PAGES))
    c = v["cache_cmp_kv"]
    out["cmp_pages"] = f(c.transpose(0, 1, 4, 5, 3, 2).reshape(L * NPOOL, P, 2 * P))
    c = v["cache_slc_kv"]
    sk = c[:, :, :, 0].transpose(0, 1, 3, 4, 2).reshape(L * NPOOL, P, P)
    sv = c[:, :, :, 1].reshape(L * NPOOL, P, P)
    out["slc_pages"] = f(np.stack([sk, sv], 2).reshape(L * NPOOL, P, 2 * P))
    c = v["cache_win_kv"]
    out["win_k"] = f(c[:, :, :, 0].transpose(0, 3, 4, 1, 2).reshape(L, P, B * PAST))
    out["win_v"] = f(c[:, :, :, 1].reshape(L, B, PAGES, P, P).transpose(0, 3, 1, 2, 4).reshape(L, P, B * PAST))
    out["conv_in"] = f(v["state_dn_conv"].reshape(L, B, 3, 12, P).transpose(0, 4, 3, 1, 2).reshape(L, P, 12 * B * 3))
    for k in ("dn", "hg"):
        out[k + "_in"] = f(v[f"state_{k}_S"].transpose(0, 3, 2, 1, 4).reshape(L, P, 32 * P))
    return out


_OUTS = [("y", (P, KD * N)), ("kv", (L, P, 6 * N)), ("conv_p", (L, P, 12 * 3)), ("conv_s", (L, P, 12 * B * 3)),
         ("dn_p", (L, P, 4 * P)), ("dn_s", (L, P, 32 * P)), ("hg_p", (L, P, 4 * P)), ("hg_s", (L, P, 32 * P))]


def kernel(**inputs):
    import numpy as np
    import concourse.bacc as _bacc
    from concourse.bass_utils import run_bass_kernel_spmd as _run

    nc = _bacc.Bacc("TRN2", target_bir_lowering=False, num_devices=1)
    arrays, ins, outs = {}, {}, {}
    for name, a in _layout(inputs).items():
        arrays["in_" + name] = a
        ins[name] = nc.dram_tensor("in_" + name, a.shape, mybir.dt.from_np(a.dtype), kind="ExternalInput").ap()
    for name, shape in _OUTS:
        outs[name] = nc.dram_tensor("out_" + name, shape, F32, kind="ExternalOutput").ap()
    hybrid_step_kernel(nc, ins, outs)
    r = _run(nc, [arrays], core_ids=[0]).results[0]
    g = {name: np.asarray(r["out_" + name]) for name, _ in _OUTS}

    y = g["y"].reshape(P, KD, N).transpose(2, 1, 0).reshape(N, KD * P)
    kv = g["kv"].reshape(L, 2, HD, 3, 2, N).transpose(0, 3, 5, 4, 1, 2)
    kvp = [kv[:, i, :T].reshape(L, 1, T, 2, 2, HD) for i in range(3)]
    kvs = [kv[:, i, T:].reshape(L, B, 1, 2, 2, HD) for i in range(3)]
    conv_p = g["conv_p"].reshape(L, P, 12, 3).transpose(0, 3, 2, 1).reshape(L, 1, 3, 12 * P)
    conv_s = g["conv_s"].reshape(L, P, 12, B, 3).transpose(0, 3, 4, 2, 1).reshape(L, B, 3, 12 * P)
    res = [y[:T].reshape(1, T, KD * P), y[T:].reshape(B, 1, KD * P)]
    for i in range(3):
        res += [kvp[i], kvs[i]]
    res += [conv_p, conv_s]
    for k in ("dn", "hg"):
        res.append(g[k + "_p"].reshape(L, P, 4, P).transpose(0, 2, 1, 3).reshape(L, 1, 4, P, P))
        res.append(g[k + "_s"].reshape(L, P, 4, B, P).transpose(0, 3, 2, 1, 4).reshape(L, B, 4, P, P))
    return tuple(np.ascontiguousarray(a) for a in res)
```

```python
from contextlib import ExitStack

import concourse.bass as bass
from concourse import mybir

F32 = mybir.dt.float32
F16 = mybir.dt.float16
I32 = mybir.dt.int32
ALU = mybir.AluOpType
ACT = mybir.ActivationFunctionType
AX_X = mybir.AxisListType.X

P = 128
L = 2
T = 512
B = 8
N = T + B
HALF = N // 2
KD = 8
FC = 22
DOWN = (8, 8, 6)
TILES = 224
PAST = 256
NPOOL = 20
PAGES = 2
HD = 64
NBLK = 160
CMPW = T + B * PAST + 16
NPB = 31
QT = T // P
EPS = 1e-6
ZT = 42

CONST = {}
_at = 0
for _name, _w in (("ident", 128), ("ones", 128), ("bones", 128), ("upper", 128), ("level", 7 * 128),
                  ("dist", 512), ("dcmp", 4 * 8 * NPB), ("dsm", PAST + B), ("dcs", 128),
                  ("sel8", 64), ("pos8", 8), ("scanmask", 512), ("slope64", 1)):
    CONST[_name] = (_at, _w)
    _at += _w
NCONST = _at

VEC = {}
_at = 0
for _name, _w in (("ffn1", 8), ("mix", 8), ("ffn2", 8), ("conv", 48), ("qg", 1), ("kg", 3), ("dng", 1),
                  ("hgg", 1), ("alog", 4), ("dtb", 4), ("pe", 64), ("w2", 128)):
    VEC[_name] = (_at, _w)
    _at += _w
NVEC = _at


def slope(pos):
    return 2.0 ** -(4 * (pos % 2) + pos // 2 + 1)


class Steps:

    def __init__(self, sem, names, reps=1):
        self.sem, self.names, self.reps, self.made = sem, names, reps, 0
        self.index = {n: i + 1 for i, n in enumerate(names)}

    def at(self, name, l, r=0):
        return (l * self.reps + r) * len(self.names) + self.index[name]

    def step(self, name):
        assert self.names[self.made % len(self.names)] == name, (name, self.names[self.made % len(self.names)])
        self.made += 1
        return self.sem, 1


def blocks_of(ap, n):
    return ap.rearrange("p (k n) -> p k n", k=n)


def gate_tile(gate, t):
    return gate[:, 28 * t:28 * t + 28]


def attention_plan(m):
    part, sem, bank, pair, both, halves = m["part"], m["sem"], m["bank"], m["pair"], m["both"], m["halves"]
    const_of, scalar_of, gate, ident, o_a = m["const_of"], m["scalar_of"], m["gate"], m["ident"], m["o_a"]

    qT = part(0, 4 * N, 4)
    kvT = part(4 * N, 6 * N, 6)
    cmpT = part(5200, 2 * CMPW, 2)
    w1 = [part(10352, 32 * P, 32), blocks_of(m["mixed"][:, 4 * N:4 * N + 32 * P], 32)]
    hs = part(14448, 4 * NBLK).rearrange("p (k g n) -> p k g n", k=2, g=2)
    sqr = part(15088, 2 * N, 2)
    ckT = part(16128, NBLK)
    peb = part(16288, 2)
    nm = part(16290, 64)
    rs = part(16354, 64)
    fac = part(16418, 64)
    winK = part(16640, B * PAST, B)
    winV = part(18688, B * PAST, 2 * B)
    slcP = part(20736, 2 * B * PAST, 2 * B)
    ssb = part(5200, 3 * 512, 3)
    prb = part(6736, 3 * 512, 3)
    ptb = part(8272, 3 * 512, 3)
    oacc = part(9808, 4 * 512, 4)
    tmp = part(11856, 512)
    vrow = part(12368, 10 * P).rearrange("p (b t n) -> p b t n", b=2, t=5)
    scb = part(13648, 248)
    pcb = part(13896, 248)
    cvp = part(14144, P)
    cvs = part(14272, P)
    ptc = part(24832, 1024)
    qm = part(25856, 64)
    g64 = part(25920, 3)
    g64w = part(25923, 24)
    snm = part(25947, 9, 3)
    stb = part(25956, P)
    ssm = part(15088, PAST + B)
    spm = part(15352, PAST + B)
    spt = part(15616, 512)

    dsm, dcs, sel8, pos8 = const_of("dsm", 64), const_of("dcs", 64), const_of("sel8", 8), const_of("pos8", 64)
    dcmp = const_of("dcmp").rearrange("p (t n) -> p t n", t=QT)
    cached = sem("kv_cache_loaded")
    cmp_in = sem("cmp_rows_loaded")
    padded = sem("cmp_rows_padded")
    kv_saved = sem("kv_rows_saved")
    norm6 = [qT[:, 0, :], qT[:, 1, :], qT[:, 2, :], qT[:, 3, :], kvT[:, 2, :], kvT[:, 4, :]]
    gains = [("qg", 0)] * 4 + [("kg", 1), ("kg", 2)]
    UNITS = QT * 2 * 8

    T_ = Steps(sem("attn_tensor_step"),
               [f"ss{i}" for i in range(6)] + ["peb", "hs0", "hs1", "ckraw", "ckss", "cv", "vt", "g64"]
               + ["st0", "srow0", "spt0", "st1", "srow1", "spt1", "srow2", "spt2", "spv"]
               + [n + str(t) for t in range(QT) for n in ("cs", "cpt", "cpv")])
    S_ = Steps(sem("attn_scalar_step"),
               ["kv", "sq0", "sq1", "std0", "sq2", "std1", "sq3", "std2", "sq4", "std3", "sq5", "std4", "std5"]
               + ["gates", "peb", "hs00", "hs01", "hs10", "hs11", "cksq", "ckstd", "cv", "vrow"]
               + ["st0", "sexp0", "spt0", "st1", "sexp1", "spt1", "sexp2", "spt2"]
               + [n + str(t) for t in range(QT) for n in ("ce", "cpt")])
    V_ = Steps(sem("attn_vector_step"),
               [f"nrm{i}" for i in range(6)] + ["ck", "qm", "g64", "sb0", "sn0", "sb1", "sn1", "sb2", "sn2", "so"]
               + [n + str(t) for t in range(QT) for n in ("cb", "cn", "co")])
    s_ready, biased, negmax, probs, pt_ready, pt_copied, pv_done, comb, ot_ready, ot_copied = (
        sem(n) for n in ("scores_ready", "scores_biased", "row_max_ready", "probs_ready", "probs_transposed",
                         "probs_copied", "values_summed", "branch_added", "o_transposed", "o_copied"))

    def unit(a):
        return a // 16, a // 8 % 2, a % 8

    class Plan:
        def load(self, e, l):
            e.wait_ge(m["x_done"], 24 * l + 8)
            e.dma_start(winK, m["ins"]["win_k"][l].rearrange("p (b n) -> p b n", b=B)).then_inc(cached, 16)
            e.dma_start(winV, m["ins"]["win_v"][l].rearrange("p (b n) -> p b n", b=2 * B)).then_inc(cached, 16)
            e.dma_start(w1[1], m["ins"]["w1"][l, 1].rearrange("p (r n) -> p r n", r=32)).then_inc(cmp_in, 16)
            with e.Fori(0, B * PAGES) as i:
                page = e.value_load(m["pages"][0:1, bass.DynSlice(i, 1)], min_val=0, max_val=NPOOL - 1)
                e.dma_start(slcP[:, bass.DynSlice(i, 1), :], m["ins"]["slc_pages"][bass.DynSlice(l * NPOOL + page, 1)]
                            .rearrange("a p n -> p a n")).then_inc(cached, 16)

        def tensor(self, pe, l):
            def s_(n):
                pe.wait_ge(S_.sem, S_.at(n, l))

            def v_(n):
                pe.wait_ge(V_.sem, V_.at(n, l))

            for i in range(6):
                s_(f"sq{i}")
                if i >= 2:
                    s_(f"std{i - 2}")
                for a in range(2):
                    mm = pe.matmul(pair[2 + i % 2][:, a, 0:HALF], m["bones"], sqr[:, i % 2, a * HALF:(a + 1) * HALF],
                                   start=True, stop=True)
                mm.then_inc(*T_.step(f"ss{i}"))
            pe.wait_ge(cmp_in, 16 * 18 * (l + 1))
            pe.wait_ge(padded, l + 1)
            s_("gates")
            for k in range(2):
                for r in range(32):
                    pe_col = m["vec"][0:HD, VEC["pe"][0] + 32 * k + r:VEC["pe"][0] + 32 * k + r + 1]
                    mm = pe.matmul(bank(2)[:, k:k + 1], w1[k][0:HD, r, :], pe_col, start=(r == 0), stop=(r == 31))
            mm.then_inc(*T_.step("peb"))
            s_("std5")
            for k in range(2):
                for g in range(2):
                    for r in range(32):
                        o = slice(HD * g, HD * g + HD)
                        mm = pe.matmul(pair[2 + k][:, g, 0:NBLK], w1[k][o, r, :],
                                       cmpT[o, k, r:r + 16 * (NBLK - 1) + 1:16], start=(r == 0), stop=(r == 31))
                mm.then_inc(*T_.step(f"hs{k}"))
            w2 = [m["vec"][:, VEC["w2"][0] + HD * k:VEC["w2"][0] + HD * k + HD] for k in range(2)]
            s_("hs01")
            for g in range(2):
                mm = pe.matmul(bank(0)[HD * g:HD * g + HD, 0:NBLK], w2[0], hs[:, 0, g, :], start=True, stop=True)
            mm.then_inc(*T_.step("ckraw"))
            s_("cksq")
            pe.matmul(bank(1)[:, 0:NBLK], m["bones"], sqr[:, 0, 0:NBLK], start=True, stop=True).then_inc(*T_.step("ckss"))
            s_("hs11")
            for g in range(2):
                pe.matmul(bank(2)[0:NPB, 128 + HD * g:128 + HD * g + HD], hs[:, 1, g, 0:NPB], w2[1], start=True, stop=True)
                mm = pe.matmul(bank(3)[:, HD * g:HD * g + HD], hs[:, 1, g, 32:NBLK], w2[1], start=True, stop=True)
            mm.then_inc(*T_.step("cv"))
            v_("nrm5")
            for b in range(2):
                for t in range(4):
                    pe.transpose(bank(4 + b)[:, P * t:P * t + P], kvT[:, 3 + 2 * b, P * t:P * t + P], ident)
                mm = pe.transpose(bank(6)[0:B, P * b:P * b + P], kvT[:, 3 + 2 * b, T:N], ident)
            mm.then_inc(*T_.step("vt"))
            s_("gates")
            s_("hs11")
            pe.matmul(bank(7)[0:64, 0:24], sel8, gate_tile(gate, 4)[0:B, 0:24], start=True, stop=True).then_inc(*T_.step("g64"))

            v_("qm")
            s_("vrow")
            pe.wait_ge(cached, 16 * 18 * (l + 1))
            for b in range(3):
                if b < 2:
                    if b:
                        s_("st0")
                    for k in range(2):
                        for s in range(B):
                            kk = slcP[:, 2 * s + k, 0:P] if b == 0 else winK[:, s, P * k:P * k + P]
                            mm = pe.matmul(bank(0)[:, 64 * k + 8 * s:64 * k + 8 * s + 8], kk, qm[:, 8 * s:8 * s + 8],
                                           start=True, stop=True)
                    mm.then_inc(*T_.step(f"st{b}"))
                    s_(f"st{b}")
                    if b:
                        v_("sb0")
                    pe.matmul(bank(1)[0:64, PAST:PAST + B], qm, kvT[:, 2 + 2 * b, T:N], start=True, stop=True)
                    for k in range(2):
                        mm = pe.transpose(bank(1)[0:64, P * k:P * k + P], stb[:, 64 * k:64 * k + 64], ident)
                    mm.then_inc(*T_.step(f"srow{b}"))
                else:
                    v_("ck")
                    v_("sb1")
                    pe.matmul(bank(1)[0:64, 0:P], qm, ckT[:, 32:NBLK], start=True, stop=True).then_inc(*T_.step("srow2"))
                v_(f"sn{b}")
                if b:
                    s_(f"spt{b - 1}")
                for k in range(2 if b < 2 else 1):
                    mm = pe.matmul(bank(2)[:, 64 * k:64 * k + 64], spm[0:64, P * k:P * k + P], ident[0:64, 0:64],
                                   start=True, stop=True)
                if b < 2:
                    mm = pe.matmul(bank(2)[0:B, 128:192], spm[0:64, PAST:PAST + B], ident[0:64, 0:64],
                                   start=True, stop=True)
                mm.then_inc(*T_.step(f"spt{b}"))
            s_("spt2")
            pe.matmul(bank(3)[:, 0:64], cvs, spt[:, 384:448], start=True, stop=False, skip_group_check=True)
            for b in range(2):
                pe.matmul(bank(3)[:, 0:64], vrow[0:B, b, 4, :], spt[0:B, 192 * b + 128:192 * b + 192],
                          start=False, stop=False, skip_group_check=True)
                for k in range(2):
                    for s in range(B):
                        vv = slcP[:, 2 * s + k, P:2 * P] if b == 0 else winV[:, 2 * s + k, :]
                        mm = pe.matmul(bank(3)[:, 8 * s:8 * s + 8], vv, spt[:, 192 * b + 64 * k + 8 * s:192 * b + 64 * k + 8 * s + 8],
                                       start=False, stop=(b == 1 and k == 1), skip_group_check=True)
            mm.then_inc(*T_.step("spv"))

            v_("so")
            for t in range(QT):
                if t:
                    v_(f"cb{t - 1}")
                for p in range(8):
                    c, g = p // 2, p % 2
                    o = slice(HD * g, HD * g + HD)
                    mm = pe.matmul(bank(g)[:, NPB * c:NPB * c + NPB], qT[o, c, P * t:P * t + P], ckT[o, 0:NPB],
                                   start=True, stop=True)
                mm.then_inc(*T_.step(f"cs{t}"))
                v_(f"cn{t}")
                for p in range(8):
                    mm = pe.transpose(pair[1][0:NPB, p // 4, P * (p % 4):P * (p % 4) + P], pcb[:, NPB * p:NPB * p + NPB], ident)
                mm.then_inc(*T_.step(f"cpt{t}"))
                s_(f"cpt{t}")
                if t:
                    v_(f"co{t - 1}")
                for p in range(8):
                    mm = pe.matmul(bank(4)[:, HD * p:HD * p + HD], ptc[0:NPB, P * p:P * p + P],
                                   cvp[0:NPB, HD * (p % 2):HD * (p % 2) + HD], start=True, stop=True)
                mm.then_inc(*T_.step(f"cpv{t}"))

            v_(f"co{QT - 1}")

            def scores(a):
                t, b, p = unit(a)
                if a >= 3:
                    pe.wait_ge(biased, UNITS * l + a - 2)
                w = P * (t + 1)
                o = slice(HD * (p % 2), HD * (p % 2) + HD)
                pe.matmul(bank(a % 3)[:, 0:w], qT[o, p // 2, P * t:P * t + P], kvT[o, 2 + 2 * b, 0:w],
                          start=True, stop=True).then_inc(s_ready, 1)

            def turn(a):
                t, _, _ = unit(a)
                pe.wait_ge(probs, UNITS * l + a + 1)
                if a >= 2:
                    pe.wait_ge(pt_copied, UNITS * l + a - 1)
                for k in range(t + 1):
                    mm = pe.transpose(bank(3 + a % 2)[:, P * k:P * k + P], prb[:, a % 3, P * k:P * k + P], ident)
                mm.then_inc(pt_ready, 1)

            def values(a):
                t, b, p = unit(a)
                c = a // 8
                pe.wait_ge(pt_copied, UNITS * l + a + 1)
                if p == 0 and c >= 2:
                    pe.wait_ge(comb, 8 * l + c - 1)
                for k in range(t + 1):
                    mm = pe.matmul(bank(5 + c % 2)[:, HD * p:HD * p + HD], ptb[:, a % 3, P * k:P * k + P],
                                   vrow[:, b, k, HD * (p % 2):HD * (p % 2) + HD], start=(k == 0), stop=(k == t))
                mm.then_inc(pv_done, 1)

            def o_turn(t):
                pe.wait_ge(comb, 8 * l + 2 * t + 2)
                if t:
                    pe.wait_ge(ot_copied, QT * l + t)
                for c in range(4):
                    mm = pe.transpose(bank(7)[:, P * c:P * c + P], oacc[:, t, P * c:P * c + P], ident)
                mm.then_inc(ot_ready, 1)

            for i in range(UNITS + 4):
                if i < UNITS:
                    scores(i)
                if 2 <= i < UNITS + 2:
                    turn(i - 2)
                if i >= 4:
                    values(i - 4)
                if i >= 28 and (i - 28) % 16 == 0:
                    o_turn((i - 28) // 16)
            o_turn(QT - 1)

        def scalar(self, e, l):
            def t_(n):
                e.wait_ge(T_.sem, T_.at(n, l))

            def v_(n):
                e.wait_ge(V_.sem, V_.at(n, l))

            e.dma_start(w1[0], m["ins"]["w1"][l, 0].rearrange("p (r n) -> p r n", r=32)).then_inc(cmp_in, 16)
            with e.Fori(0, B * PAGES) as i:
                page = e.value_load(m["pages"][0:1, bass.DynSlice(i, 1)], min_val=0, max_val=NPOOL - 1)
                e.dma_start(cmpT[:, :, bass.DynSlice(T + P * i, P)],
                            m["ins"]["cmp_pages"][bass.DynSlice(l * NPOOL + page, 1)]
                            .rearrange("a p (k n) -> p (a k) n", k=2)).then_inc(cmp_in, 16)
            for zi in range(10):
                e.wait_ge(m["z_ready"], ZT * l + zi + 1)
                if zi in (4, 5):
                    e.activation(cmpT[:, zi - 4, 0:HALF], pair[zi % 2][:, 0, 0:HALF], ACT.Copy)
                    e.activation(cmpT[:, zi - 4, HALF:T], pair[zi % 2][:, 1, 0:T - HALF], ACT.Copy)
                dst = qT[:, zi, :] if zi < 4 else kvT[:, zi - 4, :]
                e.activation(halves(dst), both(zi % 2), ACT.Copy).then_inc(m["z_used"], 1)
                m["split_hi"](e, l * TILES + m["z_tile"](zi), m["z_tile"](zi))
            e.drain().then_inc(*S_.step("kv"))

            def square(i):
                if i >= 2:
                    t_(f"ss{i - 2}")
                e.activation(sqr[:, i % 2, :], norm6[i], ACT.Square).then_inc(*S_.step(f"sq{i}"))

            def std(i):
                t_(f"ss{i}")
                if i >= 2:
                    v_(f"nrm{i - 2}")
                e.activation(halves(m["rstd"][:, N * (i % 2):N * (i % 2) + N]), both(2 + i % 2), ACT.Sqrt,
                             bias=m["eps"][:, :], scale=1.0 / HD).then_inc(*S_.step(f"std{i}"))

            square(0)
            square(1)
            for i in range(6):
                std(i)
                if i + 2 < 6:
                    square(i + 2)
            e.wait_ge(m["small_ready"], l + 1)
            for at in (m["z_tile"](9) + 1, m["z_tile"](9) + 2):
                m["split_hi"](e, l * TILES + at, at)
            e.activation(m["small"][:, 0:128], bank(0)[:, 0:128], ACT.Copy)
            e.activation(m["small"][0:B, 128:160], bank(0)[0:B, 128:160], ACT.Copy)
            e.drain()
            e.activation(m["gate"][:, :].rearrange("p (t n) -> p t n", t=5),
                         m["small"][:, :].rearrange("p (t n) -> p t n", t=5)[:, :, 0:28], ACT.Sigmoid).then_inc(*S_.step("gates"))
            t_("peb")
            e.activation(peb, bank(2)[:, 0:2], ACT.Copy).then_inc(*S_.step("peb"))
            e.drain()
            for k in range(2):
                t_(f"hs{k}")
                for g in range(2):
                    e.activation(hs[:, k, g, :], pair[2 + k][:, g, 0:NBLK], ACT.Silu,
                                 bias=peb[:, k:k + 1]).then_inc(*S_.step(f"hs{k}{g}"))
            t_("ckraw")
            e.activation(sqr[:, 0, 0:NBLK], bank(0)[:, 0:NBLK], ACT.Square).then_inc(*S_.step("cksq"))
            t_("ckss")
            v_("nrm5")
            e.dma_start(m["outs"]["kv"][l].rearrange("p (k n) -> p k n", k=6), kvT).then_inc(kv_saved, 16)
            e.activation(m["rstd"][:, 0:NBLK], bank(1)[:, 0:NBLK], ACT.Sqrt, bias=m["eps"][:, :],
                         scale=1.0 / HD).then_inc(*S_.step("ckstd"))
            t_("cv")
            e.activation(cvp[0:NPB, :], bank(2)[0:NPB, 128:256], ACT.Copy)
            e.activation(cvs, bank(3)[:, 0:P], ACT.Copy).then_inc(*S_.step("cv"))
            t_("vt")
            for b in range(2):
                e.activation(vrow[:, b, 0:4, :], bank(4 + b).rearrange("p (t n) -> p t n", t=4), ACT.Copy)
            e.activation(vrow[0:B, :, 4, :], bank(6)[0:B, 0:2 * P].rearrange("p (b n) -> p b n", b=2),
                         ACT.Copy).then_inc(*S_.step("vrow"))
            for b in range(3):
                if b < 2:
                    t_(f"st{b}")
                    if b:
                        t_("srow0")
                    e.activation(stb, bank(0)[:, 0:P], ACT.Copy).then_inc(*S_.step(f"st{b}"))
                v_(f"sb{b}")
                w = PAST + B if b < 2 else P
                e.activation(spm[0:64, 0:w], ssm[0:64, 0:w], ACT.Exp, bias=snm[0:64, b, 0:1],
                             accum_out=snm[0:64, b, 1:2]).then_inc(*S_.step(f"sexp{b}"))
                t_(f"spt{b}")
                e.activation(spt[:, 192 * b:192 * b + (128 if b < 2 else 64)], bank(2)[:, 0:(128 if b < 2 else 64)], ACT.Copy) \
                    .then_inc(*(S_.step("spt2") if b == 2 else (spare, 1)))
                if b < 2:
                    e.activation(spt[0:B, 192 * b + 128:192 * b + 192], bank(2)[0:B, 128:192],
                                 ACT.Copy).then_inc(*S_.step(f"spt{b}"))
            for t in range(QT):
                v_(f"cb{t}")
                if t:
                    t_(f"cpt{t - 1}")
                e.activation(pcb, scb, ACT.Exp).then_inc(*S_.step(f"ce{t}"))
                t_(f"cpt{t}")
                if t:
                    t_(f"cpv{t - 1}")
                e.activation(ptc[0:NPB, :].rearrange("p (a n) -> p a n", a=2), pair[1][0:NPB, :, :],
                             ACT.Copy).then_inc(*S_.step(f"cpt{t}"))

            def exp(a):
                w = P * (unit(a)[0] + 1)
                e.wait_ge(negmax, UNITS * l + a + 1)
                if a >= 3:
                    e.wait_ge(pt_ready, UNITS * l + a - 2)
                e.activation(prb[:, a % 3, 0:w], ssb[:, a % 3, 0:w], ACT.Exp, bias=nm[:, a:a + 1],
                             accum_out=rs[:, a:a + 1]).then_inc(probs, 1)

            def copy_pt(a):
                w = P * (unit(a)[0] + 1)
                e.wait_ge(pt_ready, UNITS * l + a + 1)
                if a >= 3:
                    e.wait_ge(pv_done, UNITS * l + a - 2)
                e.activation(ptb[:, a % 3, 0:w], bank(3 + a % 2)[:, 0:w], ACT.Copy).then_inc(pt_copied, 1)

            def o_copy(t):
                e.wait_ge(ot_ready, QT * l + t + 1)
                e.activation(o_a[:, :, P * t:P * t + P], bank(7).rearrange("p (c n) -> p c n", c=4),
                             ACT.Copy).then_inc(ot_copied, 1)

            for i in range(UNITS + 2):
                if i < UNITS:
                    exp(i)
                if i >= 2:
                    copy_pt(i - 2)
                if i >= 30 and (i - 30) % 16 == 0:
                    o_copy((i - 30) // 16)
            o_copy(QT - 1)

        def vector(self, e, l):
            def t_(n):
                e.wait_ge(T_.sem, T_.at(n, l))

            def s_(n):
                e.wait_ge(S_.sem, S_.at(n, l))

            e.memset(cmpT[:, :, T + B * PAST:CMPW], 0.0).then_inc(padded, 1)
            for i in range(6):
                s_(f"std{i}")
                r = m["rstd"][:, N * (i % 2):N * (i % 2) + N]
                e.reciprocal(r, r)
                e.drain()
                e.scalar_tensor_tensor(norm6[i], norm6[i], scalar_of(*gains[i]), r, ALU.mult, ALU.mult)
                if i < 4:
                    e.drain()
                    e.tensor_scalar(norm6[i], norm6[i], HD ** -0.5, None, ALU.mult).then_inc(*V_.step(f"nrm{i}"))
                else:
                    e.drain().then_inc(*V_.step(f"nrm{i}"))
            s_("ckstd")
            e.reciprocal(m["rstd"][:, 0:NBLK], m["rstd"][:, 0:NBLK])
            e.drain()
            e.scalar_tensor_tensor(ckT, bank(0)[:, 0:NBLK], scalar_of("kg", 0), m["rstd"][:, 0:NBLK],
                                   ALU.mult, ALU.mult).then_inc(*V_.step("ck"))
            q4 = qm.rearrange("p (b c g) -> p b c g", c=4, g=2)
            e.memset(qm, 0.0)
            e.drain()
            for g in range(2):
                o = slice(HD * g, HD * g + HD)
                mm = e.tensor_copy(q4[o, :, :, g], qT[o, :, T:N].rearrange("p c b -> p b c"))
            e.drain().then_inc(*V_.step("qm"))
            t_("g64")
            gw = g64w[0:64, :].rearrange("p (b n) -> p b n", b=3)
            e.tensor_tensor(gw, bank(7)[0:64, 0:24].rearrange("p (b n) -> p b n", b=3),
                            pos8.unsqueeze(1).to_broadcast([64, 3, 8]), ALU.mult)
            e.drain()
            e.tensor_reduce(g64[0:64, :], gw, AX_X, ALU.add).then_inc(*V_.step("g64"))
            for b in range(3):
                w = PAST + B if b < 2 else P
                t_(f"srow{b}")
                e.tensor_tensor(ssm[0:64, 0:w], bank(1)[0:64, 0:w], dsm if b < 2 else dcs, ALU.add)
                e.drain()
                e.tensor_reduce(snm[0:64, b, 0:1], ssm[0:64, 0:w], AX_X, ALU.max, negate=True).then_inc(*V_.step(f"sb{b}"))
                s_(f"sexp{b}")
                e.reciprocal(snm[0:64, b, 2:3], snm[0:64, b, 1:2])
                e.drain()
                gi = (1, 2, 0)[b]
                e.tensor_scalar(spm[0:64, 0:w], spm[0:64, 0:w], snm[0:64, b, 2:3], g64[0:64, gi:gi + 1],
                                ALU.mult, ALU.mult).then_inc(*V_.step(f"sn{b}"))
            t_("spv")
            for g in range(2):
                o = slice(HD * g, HD * g + HD)
                e.tensor_copy(o_a[o, :, T:N].rearrange("p c b -> p b c"),
                              bank(3)[o, 0:64].rearrange("p (b c g) -> p b c g", c=4, g=2)[:, :, :, g])
            e.drain().then_inc(*V_.step("so"))
            for t in range(QT):
                s8 = scb.rearrange("p (h n) -> p h n", h=8)
                p8 = pcb.rearrange("p (h n) -> p h n", h=8)
                t_(f"cs{t}")
                for g in range(2):
                    e.tensor_tensor(scb.rearrange("p (c g n) -> p g c n", c=4, g=2)[:, g],
                                    bank(g)[:, 0:4 * NPB].rearrange("p (c n) -> p c n", c=4),
                                    dcmp[:, t, :].rearrange("p (c g n) -> p g c n", c=4, g=2)[:, g], ALU.add)
                e.drain()
                e.tensor_reduce(nm[:, 0:8], s8, AX_X, ALU.max, negate=True)
                e.drain()
                e.tensor_scalar(nm[:, 8:16], nm[:, 0:8], 1e20, None, ALU.min)
                e.drain()
                e.tensor_tensor(s8, s8, nm[:, 8:16].unsqueeze(2).to_broadcast([P, 8, NPB]),
                                ALU.add).then_inc(*V_.step(f"cb{t}"))
                s_(f"ce{t}")
                e.tensor_reduce(rs[:, 0:8], p8, AX_X, ALU.add)
                e.drain()
                e.tensor_scalar(rs[:, 8:16], rs[:, 0:8], 1e-30, None, ALU.max)
                e.drain()
                e.reciprocal(rs[:, 16:24], rs[:, 8:16])
                e.drain()
                e.tensor_tensor(fac[:, 0:8], rs[:, 16:24], gate_tile(gate, t)[:, 0:8], ALU.mult)
                e.drain()
                e.tensor_tensor(p8, p8, fac[:, 0:8].unsqueeze(2).to_broadcast([P, 8, NPB]),
                                ALU.mult).then_inc(*V_.step(f"cn{t}"))
                t_(f"cpv{t}")
                e.tensor_copy(oacc[:, t, :], bank(4)).then_inc(*V_.step(f"co{t}"))
            e.drain()

            def bias(a):
                t, b, p = unit(a)
                w = P * (t + 1)
                e.wait_ge(s_ready, UNITS * l + a + 1)
                if a >= 3:
                    e.wait_ge(probs, UNITS * l + a - 2)
                e.scalar_tensor_tensor(ssb[:, a % 3, 0:w], m["dist"][:, T - w:T], slope(p), bank(a % 3)[:, 0:w],
                                       ALU.mult, ALU.add).then_inc(biased, 1)

            def rowmax(a):
                w = P * (unit(a)[0] + 1)
                e.wait_ge(biased, UNITS * l + a + 1)
                e.tensor_reduce(nm[:, a:a + 1], ssb[:, a % 3, 0:w], AX_X, ALU.max, negate=True).then_inc(negmax, 1)

            def combine(c):
                t, b = c // 2, c % 2
                e.wait_ge(pv_done, UNITS * l + 8 * c + 8)
                e.reciprocal(fac[:, 0:8], rs[:, 8 * c:8 * c + 8])
                e.drain()
                e.tensor_tensor(fac[:, 8:16], fac[:, 0:8], gate_tile(gate, t)[:, 8 + 8 * b:16 + 8 * b], ALU.mult)
                e.drain()
                e.tensor_tensor(tmp.rearrange("p (h n) -> p h n", h=8), bank(5 + c % 2).rearrange("p (h n) -> p h n", h=8),
                                fac[:, 8:16].unsqueeze(2).to_broadcast([P, 8, HD]), ALU.mult)
                e.drain()
                e.tensor_tensor(oacc[:, t, :], oacc[:, t, :], tmp, ALU.add).then_inc(comb, 1)

            for i in range(UNITS + 6):
                if i < UNITS:
                    bias(i)
                if 1 <= i <= UNITS:
                    rowmax(i - 1)
                if i >= 13 and (i - 13) % 8 == 0:
                    combine((i - 13) // 8)
            e.drain()

    spare = sem("sample_probs_copied")
    p = Plan()
    p.kv_saved = kv_saved
    p.ot_copied = ot_copied
    return p


def state_steps(kind):
    vb = [f"vb{i}" for i in range(8)]
    return vb + ["so"], ["so"], ["sdec"] + [f"sa{i}" for i in range(8)]


def state_tensor(pe, l, m, T_, V_, S_, ss, vcol, q, banks):
    for i in range(8):
        pe.wait_ge(V_.sem, V_.at("sdec" if i < 2 else f"sa{i - 2}", l))
        for j in range(4):
            mm = pe.matmul(m["bank"](banks[i % 2])[:, P * j:P * j + P], vcol(4 * i + j).to_broadcast([P, P]), m["ident"],
                           start=True, stop=True)
        mm.then_inc(*T_.step(f"vb{i}"))
    pe.wait_ge(V_.sem, V_.at("sa7", l))
    for i in range(32):
        mm = pe.matmul(m["bank"](banks[2])[:, i:i + 1], ss[:, i, :], q[:, i // 8, T + i % 8:T + i % 8 + 1],
                       start=True, stop=True)
    mm.then_inc(*T_.step("so"))


def state_vector(e, l, m, T_, V_, ss, decay, k, tmp, banks):
    e.tensor_tensor(ss, ss, decay.unsqueeze(2).to_broadcast([P, 32, P]), ALU.mult).then_inc(*V_.step("sdec"))
    for i in range(8):
        e.wait_ge(T_.sem, T_.at(f"vb{i}", l))
        kc = k[:, i // 2, T + 4 * (i % 2):T + 4 * (i % 2) + 4]
        e.tensor_tensor(tmp[:, i % 2, :].rearrange("p (i n) -> p i n", i=4),
                        m["bank"](banks[i % 2]).rearrange("p (i n) -> p i n", i=4),
                        kc.unsqueeze(2).to_broadcast([P, 4, P]), ALU.mult)
        e.drain()
        e.tensor_tensor(ss[:, 4 * i:4 * i + 4, :], ss[:, 4 * i:4 * i + 4, :],
                        tmp[:, i % 2, :].rearrange("p (i n) -> p i n", i=4), ALU.add).then_inc(*V_.step(f"sa{i}"))


def state_scalar(e, l, m, T_, S_, o, banks):
    e.wait_ge(T_.sem, T_.at("so", l))
    e.activation(o[:, :, T:N], m["bank"](banks[2])[:, 0:32].rearrange("p (h b) -> p h b", h=4),
                 ACT.Copy).then_inc(*S_.step("so"))


def norm_steps(name, n):
    s = [f"{name}q0", f"{name}q1"]
    for i in range(n):
        s.append(f"{name}d{i}")
        if i + 2 < n:
            s.append(f"{name}q{i + 2}")
    return [f"{name}s{i}" for i in range(n)], s, [f"{name}n{i}" for i in range(n)]


def norm_tensor(pe, l, m, T_, S_, name, n, sqr):
    for i in range(n):
        pe.wait_ge(S_.sem, S_.at(f"{name}q{i}", l))
        if i >= 2:
            pe.wait_ge(S_.sem, S_.at(f"{name}d{i - 2}", l))
        for a in range(2):
            mm = pe.matmul(m["pair"][2 + i % 2][:, a, 0:HALF], m["ones"], sqr[:, i % 2, a * HALF:(a + 1) * HALF],
                           start=True, stop=True)
        mm.then_inc(*T_.step(f"{name}s{i}"))


def norm_scalar(e, l, m, T_, S_, V_, name, bufs, sqr, scale, ready=None):
    n = len(bufs)

    def square(i):
        if ready is not None:
            ready(i)
        if i >= 2:
            e.wait_ge(T_.sem, T_.at(f"{name}s{i - 2}", l))
        e.activation(sqr[:, i % 2, :], bufs[i], ACT.Square).then_inc(*S_.step(f"{name}q{i}"))

    square(0)
    square(1)
    for i in range(n):
        e.wait_ge(T_.sem, T_.at(f"{name}s{i}", l))
        if i >= 2:
            e.wait_ge(V_.sem, V_.at(f"{name}n{i - 2}", l))
        e.activation(m["halves"](m["rstd"][:, N * (i % 2):N * (i % 2) + N]), m["both"](2 + i % 2), ACT.Sqrt,
                     bias=m["eps"][:, :], scale=scale).then_inc(*S_.step(f"{name}d{i}"))
        if i + 2 < n:
            square(i + 2)


def norm_vector(e, l, m, S_, V_, name, bufs, gain, after):
    for i, b in enumerate(bufs):
        e.wait_ge(S_.sem, S_.at(f"{name}d{i}", l))
        r = m["rstd"][:, N * (i % 2):N * (i % 2) + N]
        e.reciprocal(r, r)
        e.drain()
        e.scalar_tensor_tensor(b, b, gain(i), r, ALU.mult, ALU.mult)
        if after(i) is None:
            e.drain().then_inc(*V_.step(f"{name}n{i}"))
        else:
            e.drain()
            e.tensor_tensor(b, b, after(i), ALU.mult).then_inc(*V_.step(f"{name}n{i}"))


def delta_plan(m):
    part, sem, bank, pair, both, halves = m["part"], m["sem"], m["bank"], m["pair"], m["both"], m["halves"]
    scalar_of, vec_of, gate, ident, ones, upper, level, o_d = (
        m["scalar_of"], m["vec_of"], m["gate"], m["ident"], m["ones"], m["upper"], m["level"], m["o_d"])

    cx = part(0, 12 * 515, 12)
    xs = part(6180, 12 * B * 4).rearrange("p (c b j) -> p c b j", c=12, b=B)
    cy = part(6564, 12 * N, 12)
    dz = part(12804, 4 * N, 4)
    ss = part(14884, 32 * P, 32)
    sqr = part(18980, 2 * N, 2)

    def four(at):
        return part(at, 512, 4)

    S, dec, at_, lt, ta, tb, yb, ls0, ls1, rb, vn, eg = (four(20020 + 512 * i) for i in range(12))
    ls = (ls0, ls1)
    ktl, vr, qt = four(0), four(512), four(1024)
    tmp = part(1536, 1024, 2)
    cin = part(21044, 288)
    cout = part(2700, 36 + 288)
    xw = part(21400, 128).rearrange("p (c b j) -> p c b j", c=4, b=B)
    gx, ga, gl, gd = (part(26164 + 20 * i, 20) for i in range(4))
    gc, egc, ktf, neg, ea = (part(26244 + 4 * i, 4) for i in range(5))
    egs = part(26264, 32)
    vns = part(26296, 32)

    n_t, n_s, n_v = norm_steps("l", 8)
    o_t, o_s, o_v = norm_steps("o", 4)
    st_t, st_s, st_v = state_steps("d")
    lv = range(1, 7)
    tile_t = ["gb", "kk", "rows", "y0"] + [n for i in lv for n in (f"y{i}", f"ty{i}")] + ["ks", "vn", "o", "s"]
    tile_s = ["exp", "vr"] + [f"y{i}" for i in lv] + ["vn", "o"]
    tile_v = ["dec", "lt", "qt", "kt"] + [f"t{i}" for i in range(7)] + ["r", "s"]
    T_ = Steps(sem("delta_tensor_step"), n_t + [f"{n}.{t}" for t in range(QT) for n in tile_t] + ["sk"] + st_t + o_t)
    S_ = Steps(sem("delta_scalar_step"), ["ge", "gl"] + ["silu0", "silu1", "silu2"] + n_s
               + [f"{n}.{t}" for t in range(QT) for n in tile_s] + ["seg"] + st_s + o_s)
    V_ = Steps(sem("delta_vector_step"), ["pad", "ga", "cin", "conv0", "conv1", "conv2", "g"] + n_v
               + [f"{n}.{t}" for t in range(QT) for n in tile_v] + ["svn"] + st_v + o_v)
    P_ = Steps(sem("delta_pool_step"), [f"ls{i}.{t}" for t in range(QT) for i in range(7)])
    conv_in, states_in, saved = sem("conv_state_loaded"), sem("delta_states_loaded"), sem("delta_outputs_saved")

    def each_head(ap):
        return ap.unsqueeze(1).to_broadcast([P, 4, P])

    def cols(ap):
        return ap.unsqueeze(2).to_broadcast([P, 4, P])

    def heads(i):
        return bank(i).rearrange("p (h n) -> p h n", h=4)

    class Plan:
        def pool(self, e, l):
            for t in range(QT):
                e.wait_ge(V_.sem, V_.at(f"lt.{t}", l))
                for i in range(7):
                    if i >= 2:
                        e.wait_ge(T_.sem, T_.at(f"y{i - 2}.{t}", l))
                    elif t:
                        e.wait_ge(T_.sem, T_.at(f"y{5 + i}.{t - 1}", l))
                    if i == 2:
                        e.wait_ge(V_.sem, V_.at(f"t0.{t}", l))
                    e.tensor_tensor(ls[i % 2], lt, each_head(level[:, i, :]), ALU.mult).then_inc(*P_.step(f"ls{i}.{t}"))

        def tensor(self, pe, l):
            def w(steps, n):
                pe.wait_ge(steps.sem, steps.at(n, l))

            norm_tensor(pe, l, m, T_, S_, "l", 8, sqr)
            w(V_, "g")
            w(V_, "ln7")
            for t in range(QT):
                k = [cy[:, 4 + h, P * t:P * t + P] for h in range(4)]
                q = [cy[:, h, P * t:P * t + P] for h in range(4)]
                v = [cy[:, 8 + h, P * t:P * t + P] for h in range(4)]
                if t:
                    w(V_, f"t6.{t - 1}")
                    w(S_, f"o.{t - 1}")
                pe.matmul(bank(7)[:, 0:4], upper, gd[:, 4 * t:4 * t + 4], start=True, stop=True)
                for h in range(4):
                    pe.matmul(heads(6)[:, h, :], gd[:, 4 * t + h:4 * t + h + 1].to_broadcast([P, P]), upper,
                              start=True, stop=True)
                    b = gate_tile(gate, t)[:, 24 + h:25 + h]
                    mm = pe.matmul(heads(5)[:, h, :], b.to_broadcast([P, P]), ident, start=True, stop=True)
                mm.then_inc(*T_.step(f"gb.{t}"))
                if t:
                    w(V_, f"s.{t - 1}")
                for h in range(4):
                    pe.matmul(heads(4)[:, h, :], k[h], k[h], start=True, stop=True)
                    mm = pe.matmul(heads(3)[:, h, :], k[h], q[h], start=True, stop=True)
                mm.then_inc(*T_.step(f"kk.{t}"))
                for h in range(4):
                    pe.transpose(heads(2)[:, h, :], k[h], ident)
                    mm = pe.transpose(heads(1)[:, h, :], v[h], ident)
                mm.then_inc(*T_.step(f"rows.{t}"))
                w(P_, f"ls0.{t}")
                for h in range(4):
                    mm = pe.matmul(heads(0)[:, h, :], ls[0][:, h, :], ident, start=True, stop=True)
                mm.then_inc(*T_.step(f"y0.{t}"))
                for i in lv:
                    w(V_, f"t{i - 1}.{t}")
                    w(P_, f"ls{i}.{t}")
                    for h in range(4):
                        mm = pe.matmul(heads(0)[:, h, :], ls[i % 2][:, h, :], ta[:, h, :], start=True, stop=True)
                    mm.then_inc(*T_.step(f"y{i}.{t}"))
                    w(S_, f"y{i}.{t}")
                    for h in range(4):
                        if i < 6:
                            pe.matmul(heads(6)[:, h, :], tb[:, h, :], yb[:, h, :], start=True, stop=True)
                        mm = pe.matmul(heads(7)[:, h, :], yb[:, h, :], tb[:, h, :], start=True, stop=True)
                    mm.then_inc(*T_.step(f"ty{i}.{t}"))
                for h in range(4):
                    mm = pe.matmul(heads(4)[:, h, :], k[h], S[:, h, :], start=True, stop=True)
                mm.then_inc(*T_.step(f"ks.{t}"))
                w(V_, f"r.{t}")
                for h in range(4):
                    mm = pe.matmul(heads(3)[:, h, :], tb[:, h, :], rb[:, h, :], start=True, stop=True)
                mm.then_inc(*T_.step(f"vn.{t}"))
                w(S_, f"vn.{t}")
                for h in range(4):
                    pe.matmul(heads(5)[:, h, :], S[:, h, :], qt[:, h, :], start=True, stop=False)
                    mm = pe.matmul(heads(5)[:, h, :], vn[:, h, :], at_[:, h, :], start=False, stop=True)
                mm.then_inc(*T_.step(f"o.{t}"))
                for h in range(4):
                    mm = pe.matmul(heads(4)[:, h, :], ktl[:, h, :], vn[:, h, :], start=True, stop=True)
                mm.then_inc(*T_.step(f"s.{t}"))
            w(V_, "t6.3")
            pe.wait_ge(states_in, 16 * (l + 1))
            for h in range(4):
                pe.matmul(bank(7)[:, 8 * h:8 * h + 8], gd[0:B, 16 + h:17 + h].to_broadcast([B, P]), ident[0:B, 0:B],
                          start=True, stop=True)
                pe.matmul(bank(7)[:, 32 + 8 * h:40 + 8 * h], gate_tile(gate, 4)[0:B, 24 + h:25 + h].to_broadcast([B, P]),
                          ident[0:B, 0:B], start=True, stop=True)
            for i in range(32):
                mm = pe.matmul(bank(7)[:, 64 + i:65 + i], ss[:, i, :], cy[:, 4 + i // 8, T + i % 8:T + i % 8 + 1],
                               start=True, stop=True)
            mm.then_inc(*T_.step("sk"))
            w(S_, "o.3")
            state_tensor(pe, l, m, T_, V_, S_, ss, lambda i: vns[:, i:i + 1], cy, (5, 6, 0))
            norm_tensor(pe, l, m, T_, S_, "o", 4, sqr)

        def scalar(self, e, l):
            def w(steps, n):
                e.wait_ge(steps.sem, steps.at(n, l))

            e.wait_ge(m["A"].kv_saved, 16 * (l + 1))
            e.dma_start(cin, m["ins"]["conv_in"][l]).then_inc(conv_in, 16)
            e.dma_start(ss, m["ins"]["dn_in"][l].rearrange("p (i n) -> p i n", i=32)).then_inc(states_in, 16)
            w(V_, "ga")
            e.activation(ga, ga, ACT.Exp, scale=-1.0)
            e.activation(ea, vec_of("alog"), ACT.Exp).then_inc(*S_.step("ge"))
            e.drain()
            e.activation(gl, ga, ACT.Ln, bias=ones[:, 0:1]).then_inc(*S_.step("gl"))
            for zi in range(10, 26):
                e.wait_ge(m["z_ready"], ZT * l + zi + 1)
                c = zi - 10
                if c == 0:
                    w(V_, "pad")
                if c < 12:
                    e.activation(cx[:, c, 3:3 + HALF], pair[zi % 2][:, 0, 0:HALF], ACT.Copy)
                    e.activation(cx[:, c, 3 + HALF:3 + T], pair[zi % 2][:, 1, 0:T - HALF], ACT.Copy)
                    e.activation(xs[:, c, :, 3], pair[zi % 2][:, 1, T - HALF:HALF], ACT.Copy).then_inc(m["z_used"], 1)
                else:
                    e.activation(halves(dz[:, c - 12, :]), both(zi % 2), ACT.Silu).then_inc(m["z_used"], 1)
                m["split_hi"](e, l * TILES + m["z_tile"](zi), m["z_tile"](zi))
            for g in range(3):
                w(V_, f"conv{g}")
                e.activation(cy[:, 4 * g:4 * g + 4, :], cy[:, 4 * g:4 * g + 4, :], ACT.Silu).then_inc(*S_.step(f"silu{g}"))
            e.drain()
            norm_scalar(e, l, m, T_, S_, V_, "l", [cy[:, i, :] for i in range(8)], sqr, 1.0)
            for t in range(QT):
                w(V_, f"dec.{t}")
                if t:
                    w(T_, f"o.{t - 1}")
                e.activation(dec, dec, ACT.Exp)
                e.activation(eg, heads(6), ACT.Exp)
                e.activation(egc, gc, ACT.Exp)
                e.activation(ktf, ktf, ACT.Exp).then_inc(*S_.step(f"exp.{t}"))
                w(T_, f"rows.{t}")
                e.activation(vr, heads(1), ACT.Copy).then_inc(*S_.step(f"vr.{t}"))
                for i in lv:
                    w(T_, f"y{i}.{t}")
                    e.activation(yb, heads(0), ACT.Copy).then_inc(*S_.step(f"y{i}.{t}"))
                w(T_, f"vn.{t}")
                e.activation(vn, heads(3), ACT.Copy).then_inc(*S_.step(f"vn.{t}"))
                w(T_, f"o.{t}")
                e.activation(o_d[:, :, P * t:P * t + P], heads(5), ACT.Copy).then_inc(*S_.step(f"o.{t}"))
            w(T_, "sk")
            e.activation(egs, bank(7)[:, 0:32], ACT.Exp).then_inc(*S_.step("seg"))
            state_scalar(e, l, m, T_, S_, o_d, (5, 6, 0))
            e.drain()
            e.dma_start(m["outs"]["conv_p"][l], cout[:, 0:36]).then_inc(saved, 16)
            e.dma_start(m["outs"]["conv_s"][l], cout[:, 36:324]).then_inc(saved, 16)
            e.dma_start(m["outs"]["dn_p"][l].rearrange("p (h n) -> p h n", h=4), S).then_inc(saved, 16)
            e.dma_start(m["outs"]["dn_s"][l].rearrange("p (i n) -> p i n", i=32), ss).then_inc(saved, 16)
            norm_scalar(e, l, m, T_, S_, V_, "o", [o_d[:, i, :] for i in range(4)], sqr, 1.0 / P)

        def vector(self, e, l):
            def w(steps, n):
                e.wait_ge(steps.sem, steps.at(n, l))

            def v3(ap, n=5):
                return ap.rearrange("p (t h) -> p t h", t=n)

            e.wait_ge(m["A"].ot_copied, QT * (l + 1))
            e.wait_ge(m["A"].kv_saved, 16 * (l + 1))
            e.memset(cx[:, :, 0:3], 0.0).then_inc(*V_.step("pad"))
            e.tensor_tensor(v3(gx), m["small"][:, :].rearrange("p (t n) -> p t n", t=5)[:, :, 28:32],
                            vec_of("dtb").unsqueeze(1).to_broadcast([P, 5, 4]), ALU.add)
            e.drain()
            e.scalar_tensor_tensor(ga, gx, -1.0, gx, ALU.mult, ALU.max).then_inc(*V_.step("ga"))
            e.wait_ge(conv_in, 16 * (l + 1))
            e.tensor_copy(xs[:, :, :, 0:3], cin.rearrange("p (c b j) -> p c b j", c=12, b=B)).then_inc(*V_.step("cin"))
            e.drain()
            cw = vec_of("conv").rearrange("p (c j) -> p c j", j=4)
            for g in range(3):
                e.wait_ge(m["z_used"], ZT * l + 10 + 4 * g + 4)
                for j in range(4):
                    for c in range(4 * g, 4 * g + 4):
                        if j == 0:
                            e.tensor_scalar(cy[:, c, 0:T], cx[:, c, 0:T], cw[:, c, 0:1], None, ALU.mult)
                        else:
                            e.scalar_tensor_tensor(cy[:, c, 0:T], cx[:, c, j:j + T], cw[:, c, j:j + 1], cy[:, c, 0:T],
                                                   ALU.mult, ALU.add)
                    if j == 0:
                        e.tensor_tensor(xw, xs[:, 4 * g:4 * g + 4], cw[:, 4 * g:4 * g + 4, :].unsqueeze(2)
                                        .to_broadcast([P, 4, B, 4]), ALU.mult)
                    if j == 2:
                        e.tensor_reduce(cy[:, 4 * g:4 * g + 4, T:N], xw, AX_X, ALU.add)
                    e.drain() if j < 3 else e.drain().then_inc(*V_.step(f"conv{g}"))
            e.tensor_copy(cout[:, 36:324].rearrange("p (c b j) -> p c b j", c=12, b=B), xs[:, :, :, 1:4])
            e.tensor_copy(cout[:, 0:36].rearrange("p (c j) -> p c j", c=12), cx[:, :, T:T + 3])
            w(S_, "gl")
            e.tensor_scalar(gx, gx, 0.0, None, ALU.max)
            e.drain()
            e.tensor_tensor(gx, gx, gl, ALU.add)
            e.drain()
            e.scalar_tensor_tensor(v3(gd), v3(gx), -1.0, ea.unsqueeze(1).to_broadcast([P, 5, 4]),
                                   ALU.mult, ALU.mult).then_inc(*V_.step("g"))
            e.memset(S, 0.0)
            norm_vector(e, l, m, S_, V_, "l", [cy[:, i, :] for i in range(8)],
                        lambda i: P ** -0.5 if i < 4 else 1.0, lambda i: None)
            for t in range(QT):
                k4 = slice(P * t, P * t + P)
                w(T_, f"gb.{t}")
                e.tensor_copy(gc, bank(7)[:, 0:4])
                e.drain()
                for h in range(4):
                    e.tensor_scalar(dec[:, h, :], heads(6)[:, h, :], gc[:, h:h + 1], 0.0, ALU.subtract, ALU.min)
                e.tensor_tensor(ktf, heads(6)[:, :, P - 1], gc, ALU.subtract)
                e.drain().then_inc(*V_.step(f"dec.{t}"))
                w(S_, f"exp.{t}")
                e.tensor_tensor(dec, dec, each_head(upper), ALU.mult)
                e.tensor_scalar(neg, egc, -1.0, None, ALU.mult)
                e.drain()
                w(T_, f"kk.{t}")
                e.tensor_tensor(lt, heads(4), dec, ALU.mult)
                e.tensor_tensor(at_, heads(3), dec, ALU.mult)
                e.drain()
                e.tensor_tensor(lt, lt, heads(5), ALU.mult).then_inc(*V_.step(f"lt.{t}"))
                e.tensor_tensor(qt, cy[:, 0:4, k4], eg, ALU.mult).then_inc(*V_.step(f"qt.{t}"))
                w(T_, f"rows.{t}")
                e.tensor_tensor(ktl, heads(2), cols(ktf), ALU.mult).then_inc(*V_.step(f"kt.{t}"))
                w(T_, f"y0.{t}")
                e.tensor_tensor(ta, each_head(ident), heads(0), ALU.subtract)
                e.tensor_tensor(tb, each_head(ident), ls[0], ALU.subtract)
                e.drain().then_inc(*V_.step(f"t0.{t}"))
                for i in lv:
                    w(T_, f"ty{i}.{t}")
                    if i < 6:
                        e.tensor_tensor(ta, ta, heads(6), ALU.subtract)
                    e.tensor_tensor(tb, tb, heads(7), ALU.subtract)
                    e.drain().then_inc(*V_.step(f"t{i}.{t}"))
                w(T_, f"ks.{t}")
                w(S_, f"vr.{t}")
                for h in range(4):
                    e.scalar_tensor_tensor(rb[:, h, :], heads(4)[:, h, :], neg[:, h:h + 1], vr[:, h, :],
                                           ALU.mult, ALU.add)
                e.drain()
                e.tensor_tensor(rb, rb, cols(gate_tile(gate, t)[:, 24:28]), ALU.mult).then_inc(*V_.step(f"r.{t}"))
                w(T_, f"s.{t}")
                for h in range(4):
                    e.scalar_tensor_tensor(S[:, h, :], S[:, h, :], eg[:, h, P - 1:P], heads(4)[:, h, :],
                                           ALU.mult, ALU.add)
                e.drain().then_inc(*V_.step(f"s.{t}"))
            w(S_, "seg")
            v32 = vns.rearrange("p (h b) -> p h b", h=4)
            e.tensor_tensor(vns, bank(7)[:, 64:96], egs, ALU.mult)
            e.drain()
            e.tensor_tensor(v32, cy[:, 8:12, T:N], v32, ALU.subtract)
            e.drain()
            e.tensor_tensor(vns, vns, bank(7)[:, 32:64], ALU.mult).then_inc(*V_.step("svn"))
            state_vector(e, l, m, T_, V_, ss, egs, cy[:, 4:8], tmp, (5, 6, 0))
            norm_vector(e, l, m, S_, V_, "o", [o_d[:, i, :] for i in range(4)],
                        lambda i: scalar_of("dng"), lambda i: dz[:, i, :])

    p = Plan()
    p.saved, p.T_, p.S_, p.V_ = saved, T_, S_, V_
    return p


def hgrn_plan(m):
    part, sem, bank, pair, both, halves = m["part"], m["sem"], m["bank"], m["pair"], m["both"], m["halves"]
    scalar_of, ident, ones, level, o_h = m["scalar_of"], m["ident"], m["ones"], m["level"], m["o_h"]

    lf, kin, q, vT, og, gc, ex, qk = (part(4 * N * i, 4 * N, 4) for i in range(8))
    am = part(0, 2048).rearrange("p (t h n) -> p t h n", t=QT, h=4)
    qt = vT
    ktr = part(16640, 2048).rearrange("p (t h n) -> p t h n", t=QT, h=4)
    vr = part(18688, 2048).rearrange("p (t h n) -> p t h n", t=QT, h=4)
    ss = part(20736, 32 * P, 32)
    S = part(24832, 512, 4)
    fs = part(25344, 32)
    egl = part(25376, 16, 4)
    lbc = part(25392, 4)
    oml = part(25396, 4)
    tmp = part(4 * N * 5, 1024, 2)
    sqr = part(4 * N * 6, 2 * N, 2)
    scan = m["const_of"]("scanmask")
    i32 = [level[:, i, :].bitcast(I32).unsqueeze(1).to_broadcast([P, 4, P]) for i in range(7)]

    st_t, st_s, st_v = state_steps("h")
    o_t, o_s, o_v = norm_steps("o", 4)
    T_ = Steps(sem("hgrn_tensor_step"), ["vrows", "ktr", "ad"] + [f"a{i}" for i in range(7)]
               + [n + str(t) for t in range(QT) for n in ("o", "s")] + st_t + o_t)
    S_ = Steps(sem("hgrn_scalar_step"), ["z", "ln", "e0", "vr", "ke", "ktr"] + [f"e{i}" for i in range(1, 8)]
               + [f"o{t}" for t in range(QT)] + st_s + o_s)
    V_ = Steps(sem("hgrn_vector_step"), ["f", "scan", "ka", "kt", "ad"]
               + ["arg0"] + [n for i in range(7) for n in ([f"qk{i}"] + [f"arg{i + 1}"] * (i < 6) + [f"a{i}"])]
               + [f"s{t}" for t in range(QT)] + st_v + o_v)
    states_in, saved = sem("hgrn_states_loaded"), sem("hgrn_outputs_saved")

    def halves_of(ap, n):
        return ap[:, :, 0:T].rearrange("p h (b s n) -> p h b s n", s=2, n=n)

    class Plan:
        def tensor(self, pe, l):
            def w(steps, n):
                pe.wait_ge(steps.sem, steps.at(n, l))

            def tile(ap, t, h):
                return ap[:, h, P * t:P * t + P]

            w(S_, "z")
            for t in range(QT):
                for h in range(4):
                    mm = pe.transpose(bank(t)[:, P * h:P * h + P], tile(vT, t, h), ident)
            mm.then_inc(*T_.step("vrows"))
            w(V_, "kt")
            for t in range(QT):
                for h in range(4):
                    mm = pe.transpose(bank(4 + t)[:, P * h:P * h + P], tile(qk, t, h), ident)
            mm.then_inc(*T_.step("ktr"))
            w(S_, "vr")
            for t in range(QT):
                for h in range(4):
                    mm = pe.matmul(bank(t)[:, P * h:P * h + P], tile(kin, t, h), tile(q, t, h), start=True, stop=True)
            mm.then_inc(*T_.step("ad"))
            w(S_, "ktr")
            for i in range(7):
                w(V_, f"qk{i}")
                if i:
                    w(V_, f"a{i - 2}" if i >= 2 else "ad")
                for t in range(QT):
                    for h in range(4):
                        mm = pe.matmul(bank(4 * (1 - i % 2) + t)[:, P * h:P * h + P], tile(qk, t, h), tile(qk, t, h),
                                       start=True, stop=True)
                mm.then_inc(*T_.step(f"a{i}"))
            w(V_, "a6")
            for t in range(QT):
                if t:
                    w(V_, f"s{t - 1}")
                    w(S_, f"o{t - 1}")
                for h in range(4):
                    pe.matmul(bank(4)[:, P * h:P * h + P], S[:, h, :], tile(qt, t, h), start=True, stop=False)
                    mm = pe.matmul(bank(4)[:, P * h:P * h + P], vr[:, t, h, :], am[:, t, h, :], start=False, stop=True)
                mm.then_inc(*T_.step(f"o{t}"))
                for h in range(4):
                    mm = pe.matmul(bank(5)[:, P * h:P * h + P], ktr[:, t, h, :], vr[:, t, h, :], start=True, stop=True)
                mm.then_inc(*T_.step(f"s{t}"))
            w(S_, "o3")
            state_tensor(pe, l, m, T_, V_, S_, ss, lambda i: vT[:, i // 8, T + i % 8:T + i % 8 + 1], q, (1, 2, 0))
            norm_tensor(pe, l, m, T_, S_, "o", 4, sqr)

        def wait_mixed(self, pe, l):
            pe.wait_ge(V_.sem, V_.at("on3", l))

        def scalar(self, e, l):
            def w(steps, n):
                e.wait_ge(steps.sem, steps.at(n, l))

            for zi in range(26, 42):
                e.wait_ge(m["z_ready"], ZT * l + zi + 1)
                c, src = (zi - 26) % 4, both(zi % 2)
                if zi == 26:
                    e.wait_ge(D_saved, 64 * (l + 1))
                    w(m["D"].V_, "on3")
                    e.dma_start(ss, m["ins"]["hg_in"][l].rearrange("p (i n) -> p i n", i=32)).then_inc(states_in, 16)
                if zi < 30:
                    e.activation(halves(lf[:, c, :]), src, ACT.Sigmoid)
                    e.activation(halves(kin[:, c, :]), src, ACT.Sigmoid, scale=-1.0).then_inc(m["z_used"], 1)
                else:
                    dst, f = ((vT, ACT.Copy), (q, ACT.Silu), (og, ACT.Sigmoid))[(zi - 30) // 4]
                    e.activation(halves(dst[:, c, :]), src, f).then_inc(m["z_used"], 1)
                m["split_hi"](e, l * TILES + m["z_tile"](zi), m["z_tile"](zi))
            e.drain().then_inc(*S_.step("z"))
            w(V_, "f")
            e.activation(lf, lf, ACT.Ln).then_inc(*S_.step("ln"))
            w(V_, "scan")
            e.activation(ex[:, :, 0:T], gc[:, :, 0:T], ACT.Exp).then_inc(*S_.step("e0"))
            w(T_, "vrows")
            for t in range(QT):
                a = e.activation(vr[:, t, :, :], bank(t).rearrange("p (h n) -> p h n", h=4), ACT.Copy)
            a.then_inc(*S_.step("vr"))
            w(V_, "ka")
            e.activation(qk[:, :, 0:T], qk[:, :, 0:T], ACT.Exp).then_inc(*S_.step("ke"))
            w(T_, "ktr")
            for t in range(QT):
                a = e.activation(ktr[:, t, :, :], bank(4 + t).rearrange("p (h n) -> p h n", h=4), ACT.Copy)
            a.then_inc(*S_.step("ktr"))
            for i in range(7):
                w(V_, f"arg{i}")
                e.activation(ex[:, :, 0:T], ex[:, :, 0:T], ACT.Exp).then_inc(*S_.step(f"e{i + 1}"))
            for t in range(QT):
                w(T_, f"o{t}")
                e.activation(o_h[:, :, P * t:P * t + P], bank(4).rearrange("p (h n) -> p h n", h=4),
                             ACT.Copy).then_inc(*S_.step(f"o{t}"))
            state_scalar(e, l, m, T_, S_, o_h, (1, 2, 0))
            e.drain()
            e.dma_start(m["outs"]["hg_p"][l].rearrange("p (h n) -> p h n", h=4), S).then_inc(saved, 16)
            e.dma_start(m["outs"]["hg_s"][l].rearrange("p (i n) -> p i n", i=32), ss).then_inc(saved, 16)
            norm_scalar(e, l, m, T_, S_, V_, "o", [o_h[:, i, :] for i in range(4)], sqr, 1.0 / P)

        def vector(self, e, l):
            def w(steps, n):
                e.wait_ge(steps.sem, steps.at(n, l))

            e.wait_ge(D_saved, 64 * (l + 1))
            e.tensor_copy(lbc, m["lb"][:, bass.DynSlice(4 * l, 4)])
            e.drain()
            e.tensor_scalar(oml, lbc, -1.0, 1.0, ALU.mult, ALU.add)
            e.drain()
            w(S_, "z")
            for c in range(4):
                e.tensor_scalar(lf[:, c, :], lf[:, c, :], oml[:, c:c + 1], lbc[:, c:c + 1], ALU.mult, ALU.add)
                e.tensor_scalar(kin[:, c, :], kin[:, c, :], oml[:, c:c + 1], None, ALU.mult)
            e.drain()
            e.tensor_scalar(lf, lf, 1e-18, None, ALU.max)
            e.tensor_scalar(q, q, P ** -0.5, None, ALU.mult)
            e.drain()
            e.tensor_copy(fs.rearrange("p (h b) -> p h b", h=4), lf[:, :, T:N]).then_inc(*V_.step("f"))
            w(S_, "ln")
            for c in range(4):
                e.tensor_tensor_scan(gc[:, c, 0:T], scan, lf[:, c, 0:T], 0.0, ALU.mult, ALU.add)
            e.memset(S, 0.0)
            e.drain().then_inc(*V_.step("scan"))
            ends = gc[:, :, 0:T].rearrange("p h (t n) -> p h t n", t=QT)
            e.tensor_tensor(qk[:, :, 0:T].rearrange("p h (t n) -> p h t n", t=QT),
                            ends[:, :, :, P - 1:P].to_broadcast([P, 4, QT, P]), ends, ALU.subtract).then_inc(*V_.step("ka"))
            w(S_, "e0")
            e.tensor_copy(egl, ex[:, :, P - 1:T:P])
            w(S_, "vr")
            e.tensor_tensor(qt[:, :, 0:T], q[:, :, 0:T], ex[:, :, 0:T], ALU.mult)
            w(S_, "ke")
            e.tensor_tensor(qk[:, :, 0:T], qk[:, :, 0:T], kin[:, :, 0:T], ALU.mult).then_inc(*V_.step("kt"))
            w(T_, "ad")
            for t in range(QT):
                d = e.tensor_tensor(am[:, t, :, :], bank(t).rearrange("p (h n) -> p h n", h=4),
                                    ident.unsqueeze(1).to_broadcast([P, 4, P]), ALU.mult)
            d.then_inc(*V_.step("ad"))

            def argument(i):
                n = 1 << i
                g5, e5 = halves_of(gc, n), halves_of(ex, n)
                for h in range(4):
                    r = g5[:, h, :, 0, n - 1:n].to_broadcast([P, T // (2 * n), n])
                    e.tensor_tensor(e5[:, h, :, 1, :], g5[:, h, :, 1, :], r, ALU.subtract)
                    d = e.tensor_tensor(e5[:, h, :, 0, :], r, g5[:, h, :, 0, :], ALU.subtract)
                return d

            argument(0).then_inc(*V_.step("arg0"))
            for i in range(7):
                n = 1 << i
                w(S_, f"e{i + 1}")
                w(T_, f"a{i - 1}" if i else "ktr")
                e5, k5, q5, o5 = (halves_of(a, n) for a in (ex, kin, q, qk))
                e.tensor_tensor(o5[:, :, :, 1, :], q5[:, :, :, 1, :], e5[:, :, :, 1, :], ALU.mult)
                e.tensor_tensor(o5[:, :, :, 0, :], k5[:, :, :, 0, :], e5[:, :, :, 0, :],
                                ALU.mult)
                e.drain().then_inc(*V_.step(f"qk{i}"))
                if i < 6:
                    argument(i + 1).then_inc(*V_.step(f"arg{i + 1}"))
                w(T_, f"a{i}")
                e.sem_inc(m["turns"], 1)
                for t in range(QT):
                    d = e.copy_predicated(am[:, t, :, :], i32[i],
                                          bank(4 * (1 - i % 2) + t).rearrange("p (h n) -> p h n", h=4))
                d.then_inc(*V_.step(f"a{i}"))
            for t in range(QT):
                w(T_, f"s{t}")
                for h in range(4):
                    e.scalar_tensor_tensor(S[:, h, :], S[:, h, :], egl[:, h, t:t + 1], bank(5)[:, P * h:P * h + P],
                                           ALU.mult, ALU.add)
                e.drain().then_inc(*V_.step(f"s{t}"))
            e.wait_ge(states_in, 16 * (l + 1))
            state_vector(e, l, m, T_, V_, ss, fs, kin, tmp, (1, 2, 0))
            norm_vector(e, l, m, S_, V_, "o", [o_h[:, i, :] for i in range(4)],
                        lambda i: scalar_of("hgg"), lambda i: og[:, i, :])
            e.wait_ge(saved, 32 * (l + 1))
            e.sem_inc(m["turns"], 1)

    D_saved = m["D"].saved
    p = Plan()
    p.saved = saved
    return p


def hybrid_step_kernel(nc, ins, outs):
    ctx = ExitStack()
    with ctx:
        def sb(name, width, parts=P, dtype=F32):
            return ctx.enter_context(nc.sbuf_tensor(name, [parts, width], dtype))

        def sem(name):
            return ctx.enter_context(nc.semaphore(name))

        def blocks(ap, n):
            return ap.rearrange("p (k n) -> p k n", k=n)

        def halves(ap):
            return ap.rearrange("p (a n) -> p a n", a=2)

        x = blocks(sb("x", KD * N)[:, :], KD)
        h_hi, h_lo = (blocks(sb(f"h_{n}", KD * N, dtype=F16)[:, :], KD) for n in ("hi", "lo"))
        raw = [blocks(sb(f"raw{i}", KD * P)[:, :], KD) for i in range(2)]
        w_hi = [blocks(sb(f"w_hi{i}", KD * P, dtype=F16)[:, :], KD) for i in range(4)]
        w_lo = [blocks(sb(f"w_lo{i}", KD * P, dtype=F16)[:, :], KD) for i in range(4)]
        const = sb("const", NCONST)
        vecs = sb("vecs", L * NVEC)
        vec = sb("vec", NVEC)
        lbl = sb("lbl", 8)
        lbw = sb("lbw", 24)
        lb = sb("lb", 8)
        eps = sb("eps", 1)
        rstd = sb("rstd", 2 * N)
        mixed = sb("mixed", 12 * N)
        o_a, o_d, o_h = (blocks(mixed[:, i * 4 * N:(i + 1) * 4 * N], 4) for i in range(3))
        small = sb("small", 5 * 32)
        gate = sb("gate", 5 * 28)
        pages = ctx.enter_context(nc.sbuf_tensor("page_ids", [1, B * PAGES], I32))
        ARENA = 26340
        arena = sb("arena", ARENA)

        def part(at, width, n=None, parts=P):
            assert at + width <= ARENA
            ap = arena[0:parts, at:at + width]
            return ap if n is None else blocks(ap, n)

        def const_of(name, parts=P):
            o, w = CONST[name]
            return const[0:parts, o:o + w]

        ident, ones, bones, upper = (const_of(n) for n in ("ident", "ones", "bones", "upper"))
        level = blocks(const_of("level"), 7)
        dist = const_of("dist")

        def vec_of(name):
            o, w = VEC[name]
            return vec[:, o:o + w]

        def scalar_of(name, i=0, parts=P):
            o, _ = VEC[name]
            return vec[0:parts, o + i:o + i + 1]

        pair = [ctx.enter_context(nc.psum_tensor(f"pair{i}", [P, 2, 512], F32)) for i in range(4)]

        def bank(i):
            return pair[i // 2][:, i % 2, :]

        def both(i):
            return pair[i][:, :, 0:HALF]

        def two(at, n):
            w = part(at, n * N).bitcast(F16)
            return blocks(w[:, 0:n * N], n), blocks(w[:, n * N:2 * n * N], n)

        act_hi, act_lo = two(0, FC)
        sq = part(FC * N, KD * N, KD)
        sg = part(FC * N + KD * N, 4 * HALF, 4)
        merged = part(0, KD * N, KD)
        mgate = part(KD * N, 2 * N, 2)
        mprod = part((KD + 2) * N, 2 * N, 2)
        merged_hi, merged_lo = two((KD + 4) * N, KD)
        o_hi, o_lo = two((2 * KD + 4) * N, 12)
        hf = part(FC * N + KD * N, 2 * N, 2)

        loaded = sem("constants_loaded")
        x_loaded = sem("x_loaded")
        setup = sem("setup_done")
        landed = [sem(f"raw{i}_landed") for i in range(2)]
        w_hi_done = sem("weight_hi_done")
        w_split = sem("weight_split")
        w_used = sem("weight_used")
        hf_done = sem("h_float_done")
        h_hi_done = sem("h_hi_done")
        act_hi_done = sem("act_hi_done")
        act_done = sem("act_done")
        o_hi_done = sem("o_hi_done")
        o_done = sem("o_split")
        merged_hi_done = sem("merged_hi_done")
        merged_done = sem("merged_split")
        gates_ready = sem("merge_gates_ready")
        vec_ready = sem("layer_vectors_ready")
        x_done = sem("x_block_done")
        sq_done = sem("x_block_squared")
        ss_done = sem("norm_sum_done")
        std_done = sem("norm_std_done")
        h_done = sem("h_block_done")
        gu_ready = sem("gate_up_ready")
        silu_done = sem("silu_done")
        gu_free = sem("gate_up_used")
        proj_ready = sem("projection_ready")
        z_ready = sem("z_block_ready")
        z_used = sem("z_block_used")
        small_ready = sem("small_ready")
        mg_ready = sem("merge_product_ready")
        mg_gate = sem("merge_gate_done")
        mg_used = sem("merge_product_used")
        y_stored = sem("y_stored")
        turns = sem("waits_passed")
        lbx = sem("lower_bound_step")


        def fetch(sp, n, src, s, k=KD, w=P):
            sp.wait_ge(w_split, n + 1)
            sp.dma_start(raw[s % 2][:, 0:k, 0:w], src.rearrange("a p (k n) -> p (a k) n", k=k)).then_inc(landed[s % 2], 16)

        def split_hi(e, n, s):
            e.wait_ge(landed[s % 2], 8 * (n + 4 - s % 2) + 16)
            e.activation(w_hi[s % 4], raw[s % 2], ACT.Copy).then_inc(w_hi_done, 1)

        def split_lo(e, n, s):
            e.wait_ge(w_hi_done, n + 1)
            e.tensor_tensor(w_lo[s % 4], raw[s % 2], w_hi[s % 4], ALU.subtract).then_inc(w_split, 1)

        def product(pe, out, s, x_hi, x_lo, ks, first, last):
            for i, (kw, kx) in enumerate(ks):
                for p, (w, xx) in enumerate(((w_hi, x_hi), (w_hi, x_lo), (w_lo, x_hi))):
                    mm = pe.matmul(out, w[s % 4][:, kw, :], xx(kx), start=(first and i == 0 and p == 0),
                                   stop=(last and i == len(ks) - 1 and p == 2))
            return mm

        def columns(ap, a):
            return lambda k: ap[:, k, a * HALF:(a + 1) * HALF]

        AT_FFN = (0, 156)
        AT_Z, AT_MERGE, AT_OUT = 68, 112, 148

        def z_tile(zi):
            return AT_Z + (zi if zi < 10 else zi + 2)

        env = dict(split_hi=split_hi, split_lo=split_lo, z_tile=z_tile,
                   bank=bank, bones=bones, both=both, const_of=const_of, dist=dist, eps=eps, gate=gate,
                   h_done=h_done, halves=halves, ident=ident, ins=ins, lb=lb, level=level, mixed=mixed,
                   o_a=o_a, o_d=o_d, o_h=o_h, ones=ones, outs=outs, pages=pages, pair=pair, part=part,
                   rstd=rstd, scalar_of=scalar_of, sem=sem, small=small, small_ready=small_ready, turns=turns,
                   upper=upper, vec=vec, vec_of=vec_of, x_done=x_done, z_ready=z_ready, z_used=z_used)
        A = env["A"] = attention_plan(env)
        D = env["D"] = delta_plan(env)
        G = hgrn_plan(env)
        block = ctx.enter_context(nc.Block())

        @block.sync
        def _(sp):
            sp.dma_start(x, ins["x"]).then_inc(x_loaded, 16)
            sp.dma_start(const[:, :], ins["const"]).then_inc(loaded, 16)
            sp.dma_start(vecs[:, :].rearrange("p (l n) -> p l n", l=L),
                         ins["vec"].rearrange("l p n -> p l n")).then_inc(loaded, 16)
            sp.dma_start(lbl[:, :], ins["lb"]).then_inc(loaded, 16)
            sp.dma_start(pages[:, :], ins["pages"]).then_inc(loaded, 16)
            sp.sem_inc(w_split, 2)

            with sp.Fori(0, L) as l:
                def ffn(f):
                    n = l * TILES + AT_FFN[f]
                    with sp.Fori(0, FC // 2) as r:
                        for s in range(4):
                            fetch(sp, n + 4 * r + s, ins["w_up"][2 * l + f, bass.DynSlice(4 * r + s, 1)], s)
                    with sp.Fori(0, 2) as r:
                        for s in range(12):
                            j = s % 3
                            o = sum(DOWN[:j]) * P
                            src = ins["w_dn"][2 * l + f, bass.DynSlice(4 * r + s // 3, 1)]
                            fetch(sp, n + 44 + 12 * r + s, src[:, :, o:o + DOWN[j] * P], s, DOWN[j])

                ffn(0)
                for s in range(44):
                    n = l * TILES + AT_Z + s
                    if s in (10, 11):
                        fetch(sp, n, ins["w_sm"][bass.DynSlice(l, 1)], s, KD, 32)
                    else:
                        zi = s if s < 10 else s - 2
                        fetch(sp, n, ins["w_z"][l, zi:zi + 1], s)
                with sp.Fori(0, 3) as i:
                    for s in range(12):
                        d, j = s // 3, s % 3
                        src = (ins["w_wb"][l, bass.DynSlice(4 * i + d, 1)] if j == 1 else
                               ins["w_mg"][l, bass.DynSlice(8 * i + 2 * d + j // 2, 1)])
                        fetch(sp, l * TILES + AT_MERGE + 12 * i + s, src, s)
                with sp.Fori(0, 2) as r:
                    for s in range(4):
                        fetch(sp, l * TILES + AT_OUT + 4 * r + s, ins["w_out"][l, bass.DynSlice(4 * r + s, 1)], s)
                ffn(1)
            for s in range(4):
                fetch(sp, L * TILES + s, ins["w_up"][0, s:s + 1], s)
            sp.wait_ge(x_done, 8 * (3 * L + 1))
            sp.dma_start(outs["y"].rearrange("p (k n) -> p k n", k=KD), x).then_inc(y_stored, 16)
            sp.wait_ge(y_stored, 16)
            for s in range(2):
                sp.wait_ge(landed[s], 8 * (L * TILES + 4))
            sp.wait_ge(G.saved, 32 * L)

        @block.tensor
        def _(pe):
            pe.wait_ge(loaded, 64)

            def norm(l, s):
                for k in range(KD):
                    pe.wait_ge(sq_done, 8 * (3 * l + s) + k + 1)
                    for a in range(2):
                        mm = pe.matmul(pair[3][:, a, 0:HALF], ones, sq[:, k, a * HALF:(a + 1) * HALF],
                                       start=(k == 0), stop=(k == KD - 1), skip_group_check=True)
                mm.then_inc(ss_done, 1)

            def ffn(l, f):
                n = l * TILES + AT_FFN[f]
                with pe.Fori(0, FC // 2) as r:
                    pe.wait_ge(h_done, 8 * (3 * l + 2 * f + 1))
                    for j in range(2):
                        pe.wait_ge(w_split, n + 4 * r + 2 * j + 1 + 3)
                        for a in range(2):
                            q = 2 * j + a
                            pe.wait_ge(gu_free, 44 * (2 * l + f) + 4 * r + q + 1)
                            for gu in range(2):
                                mm = product(pe, pair[q][:, gu, 0:HALF], 2 * j + gu, columns(h_hi, a), columns(h_lo, a),
                                             [(k, k) for k in range(KD)], True, True)
                            mm.then_inc(gu_ready, 1)
                with pe.Fori(0, 2) as r:
                    pe.wait_ge(act_done, 44 * (2 * l + f + 1) + 4)
                    for b in range(4):
                        pe.wait_ge(x_done, 8 * (3 * l + 2 * f) + 4 * r + b + 7)
                        for a in range(2):
                            for j in range(3):
                                if a == 0:
                                    pe.wait_ge(w_split, n + 44 + 12 * r + 3 * b + j + 3)
                                mm = product(pe, pair[b % 2][:, a, 0:HALF], 3 * b + j, columns(act_hi, a), columns(act_lo, a),
                                             [(k, 8 * j + k) for k in range(DOWN[j])], j == 0, j == 2)
                                if a == 1 and j < 2:
                                    mm.then_inc(w_used, 1)
                        mm.then_inc(proj_ready, 1)

            def z_block(l, zi):
                pe.wait_ge(w_split, l * TILES + z_tile(zi) + 3)
                if zi >= 2:
                    pe.wait_ge(z_used, ZT * l + zi - 1)
                for a in range(2):
                    mm = product(pe, pair[zi % 2][:, a, 0:HALF], z_tile(zi), columns(h_hi, a), columns(h_lo, a),
                                 [(k, k) for k in range(KD)], True, True)
                mm.then_inc(z_ready, 1)

            def z_small(l):
                pe.wait_ge(w_split, l * TILES + AT_Z + 11 + 3)
                pe.wait_ge(z_used, ZT * l + 9)
                s = (AT_Z + 10) % 4
                for t in range(5):
                    w = P if t < 4 else B
                    for k in range(KD):
                        for p, (hh, ww) in enumerate(((h_hi, w_hi), (h_hi, w_lo), (h_lo, w_hi))):
                            mm = pe.matmul(bank(0)[0:w, 32 * t:32 * t + 32], hh[:, k, P * t:P * t + w],
                                           ww[s][:, k, 0:32], start=(k == 0 and p == 0), stop=(k == KD - 1 and p == 2))
                mm.then_inc(small_ready, 1)

            def merge(l):
                for i in range(3):
                    for b in range(KD):
                        d, odd = b // 2, b % 2
                        at = AT_MERGE + 12 * i + 3 * d
                        if i == 0 and b == 0:
                            G.wait_mixed(pe, l)
                        pe.wait_ge(w_split, l * TILES + at + 2 * odd + 3)
                        pe.wait_ge(mg_used, 24 * l + 8 * i + b + 1)
                        for a in range(2):
                            mm = product(pe, pair[2 * odd][:, a, 0:HALF], at + 2 * odd, columns(h_hi, a), columns(h_lo, a),
                                         [(k, k) for k in range(KD)], True, True)
                        mm.then_inc(gates_ready, 1)
                        if b == 0:
                            pe.wait_ge(o_done, 12 * l + 4 * i + 4)
                        pe.wait_ge(w_split, l * TILES + at + 1 + 3)
                        for a in range(2):
                            mm = product(pe, pair[2 * odd + 1][:, a, 0:HALF], at + 1, columns(o_hi, a), columns(o_lo, a),
                                         [(4 * odd + k, 4 * i + k) for k in range(4)], True, True)
                        mm.then_inc(mg_ready, 1)
                for b in range(KD):
                    pe.wait_ge(w_split, l * TILES + AT_OUT + b + 3)
                    pe.wait_ge(x_done, 8 * (3 * l + 1) + b + 7)
                    for a in range(2):
                        for k in range(KD):
                            if b == 0 and a == 0:
                                pe.wait_ge(merged_done, 8 * l + k + 1)
                            mm = product(pe, pair[b % 2][:, a, 0:HALF], AT_OUT + b, columns(merged_hi, a),
                                         columns(merged_lo, a), [(k, k)], k == 0, k == KD - 1)
                    mm.then_inc(proj_ready, 1)

            with pe.Fori(0, L) as l:
                norm(l, 0)
                ffn(l, 0)
                norm(l, 1)
                pe.wait_ge(h_done, 8 * (3 * l + 2))
                for zi in range(10):
                    z_block(l, zi)
                z_small(l)
                A.tensor(pe, l)
                for zi in range(10, 26):
                    z_block(l, zi)
                D.tensor(pe, l)
                for zi in range(26, 42):
                    z_block(l, zi)
                G.tensor(pe, l)
                merge(l)
                norm(l, 2)
                ffn(l, 1)

        @block.scalar
        def _(act_e):
            act_e.wait_ge(setup, 1)
            act_e.wait_ge(lbx, 1)
            act_e.activation(lbw[:, 4:12], lbw[:, 4:12], ACT.Exp).then_inc(lbx, 1)
            for s in range(4):
                split_hi(act_e, s - 4, s)
            for k in range(KD):
                act_e.wait_ge(x_done, k + 1)
                act_e.activation(sq[:, k, :], x[:, k, :], ACT.Square).then_inc(sq_done, 1)

            def norm(l, s):
                act_e.wait_ge(ss_done, 3 * l + s + 1)
                act_e.activation(halves(rstd[:, 0:N]), both(3), ACT.Sqrt, bias=eps[:, :],
                                 scale=1.0 / (KD * P)).then_inc(std_done, 1)
                for k in range(KD):
                    act_e.wait_ge(hf_done, 8 * (3 * l + s) + k + 1)
                    act_e.activation(h_hi[:, k, :], hf[:, k % 2, :], ACT.Copy).then_inc(h_hi_done, 1)

            def square(l, s, k):
                act_e.wait_ge(x_done, 8 * (3 * l + s) + k + 9)
                act_e.activation(sq[:, bass.DynSlice(k, 1), :], x[:, bass.DynSlice(k, 1), :],
                                 ACT.Square).then_inc(sq_done, 1)

            def ffn(l, f):
                n = l * TILES + AT_FFN[f]
                with act_e.Fori(0, FC // 2) as r:
                    for q in range(4):
                        t = 44 * (2 * l + f) + 4 * r + q
                        act_e.wait_ge(gu_ready, t + 1)
                        act_e.wait_ge(act_done, t + 1)
                        act_e.activation(sg[:, q, :], pair[q][:, 0, 0:HALF], ACT.Silu).then_inc(silu_done, 1)
                        if q % 2:
                            split_hi(act_e, n + 4 * r + q - 1, q - 1)
                            split_hi(act_e, n + 4 * r + q, q)
                        act_e.wait_ge(gu_free, t + 5)
                        act_e.activation(act_hi[:, bass.DynSlice(2 * r + q // 2, 1), (q % 2) * HALF:(q % 2 + 1) * HALF],
                                         sg[:, q:q + 1, :], ACT.Copy).then_inc(act_hi_done, 1)
                with act_e.Fori(0, 2) as r:
                    for b in range(4):
                        for j in range(2):
                            act_e.wait_ge(w_used, 16 * (2 * l + f) + 8 * r + 2 * b + j + 1)
                            split_hi(act_e, n + 44 + 12 * r + 3 * b + j, 3 * b + j)
                        act_e.wait_ge(proj_ready, 8 * (3 * l + 2 * f) + 4 * r + b + 1)
                        split_hi(act_e, n + 44 + 12 * r + 3 * b + 2, 3 * b + 2)
                        square(l, 2 * f, 4 * r + b)

            def merge(l):
                for c in range(12):
                    if c == 0:
                        G.wait_mixed(act_e, l)
                    act_e.activation(o_hi[:, c, :], mixed[:, c * N:(c + 1) * N], ACT.Copy).then_inc(o_hi_done, 1)
                with act_e.Fori(0, 3) as i:
                    for b in range(KD):
                        d, odd = b // 2, b % 2
                        n = l * TILES + AT_MERGE + 12 * i + 3 * d
                        act_e.wait_ge(gates_ready, 24 * l + 8 * i + b + 1)
                        act_e.wait_ge(mg_used, 24 * l + 8 * i + b + 1)
                        act_e.activation(halves(mgate[:, odd, :]), both(2 * odd), ACT.Sigmoid).then_inc(mg_gate, 1)
                        if odd:
                            act_e.wait_ge(mg_ready, 24 * l + 8 * i + b + 1)
                            split_hi(act_e, n + 1, 3 * d + 1)
                            split_hi(act_e, n + 2, 3 * d + 2)
                        else:
                            split_hi(act_e, n, 3 * d)
                for b in range(KD):
                    act_e.wait_ge(mg_used, 24 * l + 16 + b + 3)
                    act_e.activation(merged_hi[:, b, :], merged[:, b, :], ACT.Copy).then_inc(merged_hi_done, 1)
                for b in range(KD):
                    act_e.wait_ge(proj_ready, 8 * (3 * l + 1) + b + 1)
                    split_hi(act_e, l * TILES + AT_OUT + b, b)
                    square(l, 1, b)

            with act_e.Fori(0, L) as l:
                A.load(act_e, l)
                norm(l, 0)
                ffn(l, 0)
                norm(l, 1)
                A.scalar(act_e, l)
                D.scalar(act_e, l)
                G.scalar(act_e, l)
                merge(l)
                norm(l, 2)
                ffn(l, 1)

        @block.vector
        def _(dve):
            dve.memset(eps[:, :], EPS)
            dve.memset(small[:, :], 0.0).then_inc(setup, 1)
            dve.sem_inc(gu_free, 4)
            dve.sem_inc(act_done, 4)
            dve.sem_inc(mg_used, 2)
            dve.wait_ge(loaded, 64)
            a0, a1 = lbl[:, 0:4], lbl[:, 4:8]
            mx, e0, e1, r0 = (lbw[:, 4 * i:4 * i + 4] for i in range(4))
            dve.tensor_tensor(mx, a0, a1, ALU.max)
            dve.drain()
            dve.tensor_tensor(e0, a0, mx, ALU.subtract)
            dve.tensor_tensor(e1, a1, mx, ALU.subtract)
            dve.drain().then_inc(lbx, 1)
            dve.wait_ge(lbx, 2)
            dve.tensor_tensor(r0, e0, e1, ALU.add)
            dve.drain()
            dve.reciprocal(mx, r0)
            dve.drain()
            dve.tensor_tensor(e0, e0, mx, ALU.mult)
            dve.tensor_tensor(e1, e1, mx, ALU.mult)
            dve.drain()
            dve.tensor_tensor(lb[:, 0:4], e0, e0, ALU.subtract)
            dve.tensor_tensor(r0, e0, e1, ALU.add)
            dve.drain()
            dve.tensor_tensor(lb[:, 4:8], r0, e0, ALU.subtract)
            dve.wait_ge(x_loaded, 16)
            dve.sem_inc(x_done, 8)

            def norm(l, s, gain):
                dve.wait_ge(std_done, 3 * l + s + 1)
                dve.reciprocal(rstd[:, 0:N], rstd[:, 0:N])
                dve.drain()
                for k in range(KD + 1):
                    if 2 <= k < KD:
                        dve.wait_ge(h_done, 8 * (3 * l + s) + k - 1)
                    if k < KD:
                        dve.scalar_tensor_tensor(hf[:, k % 2, :], x[:, k, :], scalar_of(gain, k), rstd[:, 0:N],
                                                 ALU.mult, ALU.mult).then_inc(hf_done, 1)
                    if k:
                        dve.wait_ge(h_hi_done, 8 * (3 * l + s) + k)
                        dve.tensor_tensor(h_lo[:, k - 1, :], hf[:, (k - 1) % 2, :], h_hi[:, k - 1, :],
                                          ALU.subtract).then_inc(h_done, 1)

            def ffn(l, f):
                with dve.Fori(0, FC // 2) as r:
                    for q in range(4):
                        dve.wait_ge(silu_done, 44 * (2 * l + f) + 4 * r + q + 1)
                        dve.tensor_tensor(sg[:, q, :], sg[:, q, :], pair[q][:, 1, 0:HALF], ALU.mult).then_inc(gu_free, 1)
                        dve.wait_ge(act_hi_done, 44 * (2 * l + f) + 4 * r + q + 1)
                        c, cols = bass.DynSlice(2 * r + q // 2, 1), slice((q % 2) * HALF, (q % 2 + 1) * HALF)
                        dve.tensor_tensor(act_lo[:, c, cols], sg[:, q:q + 1, :], act_hi[:, c, cols],
                                          ALU.subtract).then_inc(act_done, 1)
                residual(l, 2 * f, 0.5)

            def residual(l, s, scale):
                with dve.Fori(0, KD // 2) as r:
                    for j in range(2):
                        dve.wait_ge(proj_ready, 8 * (3 * l + s) + 2 * r + j + 1)
                        xk = x[:, bass.DynSlice(2 * r + j, 1), :].rearrange("p k (a n) -> p (k a) n", a=2)
                        dve.scalar_tensor_tensor(xk, both(j), scale, xk, ALU.mult, ALU.add).then_inc(x_done, 1)

            def merge(l):
                for c in range(12):
                    dve.wait_ge(o_hi_done, 12 * l + c + 1)
                    dve.tensor_tensor(o_lo[:, c, :], mixed[:, c * N:(c + 1) * N], o_hi[:, c, :],
                                      ALU.subtract).then_inc(o_done, 1)
                for i in range(3):
                    with dve.Fori(0, KD // 2) as r:
                        for j in range(2):
                            dve.wait_ge(mg_gate, 24 * l + 8 * i + 2 * r + j + 1)
                            dve.wait_ge(mg_ready, 24 * l + 8 * i + 2 * r + j + 1)
                            out = merged[:, bass.DynSlice(2 * r + j, 1), :].rearrange("p k (a n) -> p (k a) n", a=2)
                            g = halves(mgate[:, j, :])
                            if i == 0:
                                dve.tensor_tensor(out, g, both(2 * j + 1), ALU.mult).then_inc(mg_used, 1)
                            else:
                                t = halves(mprod[:, j, :])
                                dve.tensor_tensor(t, g, both(2 * j + 1), ALU.mult)
                                dve.drain()
                                dve.tensor_tensor(out, out, t, ALU.add).then_inc(mg_used, 1)

            with dve.Fori(0, L) as l:
                dve.tensor_copy(vec[:, :], vecs[:, bass.DynSlice(l * NVEC, NVEC)])
                dve.drain()
                norm(l, 0, "ffn1")
                ffn(l, 0)
                norm(l, 1, "mix")
                A.vector(dve, l)
                D.vector(dve, l)
                G.vector(dve, l)
                merge(l)
                for b in range(KD):
                    dve.wait_ge(merged_hi_done, 8 * l + b + 1)
                    dve.tensor_tensor(merged_lo[:, b, :], merged[:, b, :], merged_hi[:, b, :],
                                      ALU.subtract).then_inc(merged_done, 1)
                residual(l, 1, 1.0)
                norm(l, 2, "ffn2")
                ffn(l, 1)

        @block.gpsimd
        def _(pool):
            for s in range(4):
                split_lo(pool, s, s)

            def lo_tiles(n, count):
                with pool.Fori(0, count // 4) as r:
                    for s in range(4):
                        split_lo(pool, n + 4 * r + s, s)

            with pool.Fori(0, L) as l:
                lo_tiles(l * TILES + 4, AT_Z + 28)
                D.pool(pool, l)
                lo_tiles(l * TILES + 4 + AT_Z + 28, TILES - AT_Z - 28)


def _constants():
    import numpy as np
    big = np.float32(-1e30)
    c = np.zeros((P, NCONST), np.float32)

    def put(name, a):
        o, w = CONST[name]
        a = np.asarray(a, np.float32).reshape(a.shape[0], -1)
        assert a.shape[1] == w, name
        c[:a.shape[0], o:o + w] = a

    p = np.arange(P)
    put("ident", np.eye(P))
    put("ones", np.ones((P, P)))
    put("bones", (p[:, None] // HD == p[None] // HD))
    put("upper", (p[:, None] <= p[None]))
    lev = []
    for s in (1, 2, 4, 8, 16, 32, 64):
        j, i = p[:, None], p[None]
        lev.append((j // (2 * s) == i // (2 * s)) & (j % (2 * s) < s) & (i % (2 * s) >= s))
    put("level", np.stack(lev, 1))
    d = np.arange(T)[None] - (T - P) - p[:, None]
    put("dist", np.where(d <= 0, d, big))
    t, pos, n = np.arange(QT), np.arange(8), np.arange(NPB)
    d = 16 * n + 31 - P * t[None, :, None, None] - p[:, None, None, None] + 0 * pos[None, None, :, None]
    sl = np.array([slope(x) for x in range(8)])
    put("dcmp", np.where(d <= 0, d * sl[None, None, :, None], big))
    m = np.arange(64)
    d = np.concatenate([np.broadcast_to(np.arange(PAST) - PAST, (64, PAST)),
                        np.where(np.arange(B)[None] == m[:, None] // 8, 0.0, big)], 1)
    put("dsm", d * sl[m % 8][:, None])
    k = np.arange(128)
    d = np.where((k[None] // 16 == m[:, None] // 8) & (k[None] % 16 <= 14), 16 * (k[None] % 16) + 31 - PAST, big)
    put("dcs", d * sl[m % 8][:, None])
    put("sel8", (np.arange(8)[:, None] == m[None] // 8))
    put("pos8", (m[:, None] % 8 == np.arange(8)[None]))
    put("scanmask", np.broadcast_to(np.arange(T) % P != 0, (P, T)))
    put("slope64", sl[m % 8][:, None])
    return c


def _layout(v):
    import numpy as np
    v = {k: np.asarray(a) for k, a in v.items()}
    f = np.ascontiguousarray
    out = {}
    x = np.concatenate([v["x_prompt"][0], v["x_sample"][:, 0]], 0)
    out["x"] = f(x.T.reshape(KD, P, N).transpose(1, 0, 2))
    out["const"] = _constants()
    ups, downs = [], []
    for l in range(L):
        for s in ("ffn1", "ffn2"):
            w = v[s + "_w_gu"][l].reshape(KD, P, 2, FC, P)
            ups.append(w.transpose(3, 2, 1, 0, 4).reshape(2 * FC, P, KD * P))
            w = v[s + "_w_down"][l].reshape(FC, P, KD, P)
            downs.append(w.transpose(2, 1, 0, 3).reshape(KD, P, FC * P))
    out["w_up"], out["w_dn"] = f(np.stack(ups)), f(np.stack(downs))
    w = v["w_in"]
    q = w[:, :, 0:512].reshape(L, 1024, 2, 4, HD).transpose(0, 1, 3, 2, 4).reshape(L, 1024, 512)
    z = np.concatenate([q, w[:, :, 512:1280], w[:, :, 1304:2840], w[:, :, 2848:5408]], 2)
    out["w_z"] = f(z.reshape(L, KD, P, ZT, P).transpose(0, 3, 2, 1, 4).reshape(L, ZT, P, KD * P))
    g = w[:, :, 1280:1304].reshape(L, 1024, 2, 4, 3).transpose(0, 1, 4, 3, 2).reshape(L, 1024, 24)
    sm = np.concatenate([g, w[:, :, 2840:2848]], 2)
    out["w_sm"] = f(sm.reshape(L, KD, P, 32).transpose(0, 2, 1, 3).reshape(L, P, KD * 32))
    mg = w[:, :, 5408:].reshape(L, KD, P, 24, P).transpose(0, 3, 2, 1, 4)
    wb = v["w_branch"].reshape(L, 3, 512, 1024)
    wa = wb[:, 0].reshape(L, 2, 4, HD, 1024).transpose(0, 2, 1, 3, 4).reshape(L, 1, 512, 1024)
    wb = np.concatenate([wa, wb[:, 1:]], 1).reshape(L, 3, 4, P, KD, P).transpose(0, 1, 4, 3, 2, 5)
    out["w_mg"] = f(mg.reshape(L, 24, P, KD * P))
    out["w_wb"] = f(wb.reshape(L, 3, 4, 2, P, 4, P).transpose(0, 1, 2, 4, 3, 5, 6).reshape(L, 12, P, KD * P))
    out["w_out"] = f(v["w_out"].reshape(L, KD, P, KD, P).transpose(0, 3, 2, 1, 4).reshape(L, KD, P, KD * P))
    w1 = v["nsa_cmp_w1"].transpose(0, 1, 3, 2, 4).reshape(L, 2, HD, 32 * P)
    out["w1"] = f(np.concatenate([w1, w1], 2))
    vec = np.zeros((L, P, NVEC), np.float32)

    def put(name, a):
        o, n = VEC[name]
        vec[:, :, o:o + n] = a.reshape(L, P, n)

    for s, k in (("ffn1", "ffn1_norm"), ("mix", "mix_norm"), ("ffn2", "ffn2_norm")):
        put(s, v[k].reshape(L, KD, P).transpose(0, 2, 1))
    put("conv", v["dn_conv_w"].reshape(L, 4, 12, P).transpose(0, 3, 2, 1))
    put("qg", np.concatenate([v["nsa_q_norm"]] * 2, 1))
    put("kg", np.concatenate([v["nsa_k_norm"].transpose(0, 2, 1)] * 2, 1))
    put("dng", v["dn_out_norm"])
    put("hgg", v["hg_out_norm"])
    put("alog", np.broadcast_to(v["dn_A_log"][:, None], (L, P, 4)))
    put("dtb", np.broadcast_to(v["dn_dt_bias"][:, None], (L, P, 4)))
    pe = v["nsa_cmp_pe"].transpose(0, 3, 1, 2).reshape(L, HD, 64)
    put("pe", np.concatenate([pe, pe], 1))
    put("w2", v["nsa_cmp_w2"].transpose(0, 2, 1, 3))
    out["vec"] = vec
    out["lb"] = f(v["hg_lb_logits"].reshape(L, 4, P).transpose(2, 0, 1).reshape(P, 8))
    out["pages"] = f(v["page_table"].reshape(1, B * PAGES))
    c = v["cache_cmp_kv"]
    out["cmp_pages"] = f(c.transpose(0, 1, 4, 5, 3, 2).reshape(L * NPOOL, P, 2 * P))
    c = v["cache_slc_kv"]
    sk = c[:, :, :, 0].transpose(0, 1, 3, 4, 2).reshape(L * NPOOL, P, P)
    sv = c[:, :, :, 1].reshape(L * NPOOL, P, P)
    out["slc_pages"] = f(np.stack([sk, sv], 2).reshape(L * NPOOL, P, 2 * P))
    c = v["cache_win_kv"]
    out["win_k"] = f(c[:, :, :, 0].transpose(0, 3, 4, 1, 2).reshape(L, P, B * PAST))
    out["win_v"] = f(c[:, :, :, 1].reshape(L, B, PAGES, P, P).transpose(0, 3, 1, 2, 4).reshape(L, P, B * PAST))
    out["conv_in"] = f(v["state_dn_conv"].reshape(L, B, 3, 12, P).transpose(0, 4, 3, 1, 2).reshape(L, P, 12 * B * 3))
    for k in ("dn", "hg"):
        out[k + "_in"] = f(v[f"state_{k}_S"].transpose(0, 3, 2, 1, 4).reshape(L, P, 32 * P))
    return out


_OUTS = [("y", (P, KD * N)), ("kv", (L, P, 6 * N)), ("conv_p", (L, P, 12 * 3)), ("conv_s", (L, P, 12 * B * 3)),
         ("dn_p", (L, P, 4 * P)), ("dn_s", (L, P, 32 * P)), ("hg_p", (L, P, 4 * P)), ("hg_s", (L, P, 32 * P))]


def kernel(**inputs):
    import numpy as np
    import concourse.bacc as _bacc
    from concourse.bass_utils import run_bass_kernel_spmd as _run

    nc = _bacc.Bacc("TRN2", target_bir_lowering=False, num_devices=1)
    arrays, ins, outs = {}, {}, {}
    for name, a in _layout(inputs).items():
        arrays["in_" + name] = a
        ins[name] = nc.dram_tensor("in_" + name, a.shape, mybir.dt.from_np(a.dtype), kind="ExternalInput").ap()
    for name, shape in _OUTS:
        outs[name] = nc.dram_tensor("out_" + name, shape, F32, kind="ExternalOutput").ap()
    hybrid_step_kernel(nc, ins, outs)
    r = _run(nc, [arrays], core_ids=[0]).results[0]
    g = {name: np.asarray(r["out_" + name]) for name, _ in _OUTS}

    y = g["y"].reshape(P, KD, N).transpose(2, 1, 0).reshape(N, KD * P)
    kv = g["kv"].reshape(L, 2, HD, 3, 2, N).transpose(0, 3, 5, 4, 1, 2)
    kvp = [kv[:, i, :T].reshape(L, 1, T, 2, 2, HD) for i in range(3)]
    kvs = [kv[:, i, T:].reshape(L, B, 1, 2, 2, HD) for i in range(3)]
    conv_p = g["conv_p"].reshape(L, P, 12, 3).transpose(0, 3, 2, 1).reshape(L, 1, 3, 12 * P)
    conv_s = g["conv_s"].reshape(L, P, 12, B, 3).transpose(0, 3, 4, 2, 1).reshape(L, B, 3, 12 * P)
    res = [y[:T].reshape(1, T, KD * P), y[T:].reshape(B, 1, KD * P)]
    for i in range(3):
        res += [kvp[i], kvs[i]]
    res += [conv_p, conv_s]
    for k in ("dn", "hg"):
        res.append(g[k + "_p"].reshape(L, P, 4, P).transpose(0, 2, 1, 3).reshape(L, 1, 4, P, P))
        res.append(g[k + "_s"].reshape(L, P, 4, B, P).transpose(0, 3, 2, 1, 4).reshape(L, B, 4, P, P))
    return tuple(np.ascontiguousarray(a) for a in res)
```

```python
from contextlib import ExitStack

import concourse.bass as bass
from concourse import mybir

F32 = mybir.dt.float32
F16 = mybir.dt.float16
I32 = mybir.dt.int32
ALU = mybir.AluOpType
ACT = mybir.ActivationFunctionType
AX_X = mybir.AxisListType.X

P = 128
L = 2
T = 512
B = 8
N = T + B
HALF = N // 2
KD = 8
FC = 22
DOWN = (8, 8, 6)
TILES = 224
PAST = 256
NPOOL = 20
PAGES = 2
HD = 64
NBLK = 160
CMPW = T + B * PAST + 32
NPB = 31
QT = T // P
EPS = 1e-6
ZT = 42

CONST = {}
_at = 0
for _name, _w in (("ident", 128), ("ones", 128), ("bones", 128), ("upper", 128), ("level", 7 * 128),
                  ("dist", 512), ("dcmp", 4 * 8 * NPB), ("dsm", PAST + B), ("dcs", 128),
                  ("sel8", 64), ("pos8", 8), ("scanmask", 512)):
    CONST[_name] = (_at, _w)
    _at += _w
NCONST = _at

VEC = {}
_at = 0
for _name, _w in (("ffn1", 8), ("mix", 8), ("ffn2", 8), ("conv", 48), ("qg", 1), ("kg", 3), ("dng", 1),
                  ("hgg", 1), ("alog", 4), ("dtb", 4), ("pe", 64), ("w2", 128)):
    VEC[_name] = (_at, _w)
    _at += _w
NVEC = _at


def slope(pos):
    return 2.0 ** -(4 * (pos % 2) + pos // 2 + 1)


class Steps:

    def __init__(self, sem, names, reps=1):
        self.sem, self.names, self.reps, self.made = sem, names, reps, 0
        self.index = {n: i + 1 for i, n in enumerate(names)}

    def at(self, name, l, r=0):
        return (l * self.reps + r) * len(self.names) + self.index[name]

    def step(self, name):
        assert self.names[self.made % len(self.names)] == name, (name, self.names[self.made % len(self.names)])
        self.made += 1
        return self.sem, 1


def blocks_of(ap, n):
    return ap.rearrange("p (k n) -> p k n", k=n)


SUMS = (0, P, 2 * P, 3 * P, N - P)
PIECES = ((0, 0, P), (1, P, 2 * P), (2, 2 * P, HALF), (2, HALF, 3 * P), (3, 3 * P, T), (4, T, N))


def spread(pe, pair, ident, factors, groups=1):
    w = P // groups
    for j, c0, c1 in PIECES:
        a = c0 // HALF
        for g in range(groups):
            f = factors[:, groups * j + g:groups * j + g + 1].to_broadcast([P, w])
            mm = pe.matmul(pair[w * g:w * g + w, a, c0 - a * HALF:c1 - a * HALF], f,
                           ident[:, c0 - SUMS[j]:c1 - SUMS[j]], start=True, stop=True)
    return mm


def gate_tile(gate, t):
    return gate[:, 28 * t:28 * t + 28]


def attention_plan(m):
    part, sem, bank, pair, both, halves = m["part"], m["sem"], m["bank"], m["pair"], m["both"], m["halves"]
    const_of, scalar_of, gate, ident, o_a = m["const_of"], m["scalar_of"], m["gate"], m["ident"], m["o_a"]

    qT = part(0, 4 * N, 4)
    kvT = part(4 * N, 6 * N, 6)
    cmpT = part(5200, 2 * CMPW, 2)
    w1 = [part(10384, 32 * P, 32), blocks_of(m["mixed"][:, 4 * N:4 * N + 32 * P], 32)]
    hs = part(14480, 4 * NBLK).rearrange("p (k g n) -> p k g n", k=2, g=2)
    sqr = part(15120, 2 * N, 2)
    ckT = part(16160, NBLK)
    peb = part(16320, 2)
    nm = part(16322, 64)
    rs = part(16386, 64)
    fac = part(16450, 64)
    winK = part(16640, B * PAST, B)
    winV = part(18688, B * PAST, 2 * B)
    slcP = part(20736, 2 * B * PAST, 2 * B)
    ssb = part(5200, 3 * 512, 3)
    prb = part(6736, 3 * 512, 3)
    ptb = part(8272, 3 * 512, 3)
    oacc = part(9808, 4 * 512, 4)
    tmp = part(11856, 512)
    vrow = part(12368, 10 * P).rearrange("p (b t n) -> p b t n", b=2, t=5)
    scb = part(6736, QT * 8 * NPB)
    pcb = part(8272, QT * 8 * NPB)
    cvp = part(14144, P)
    cvs = part(14272, P)
    ptc = (part(24832, 1024), part(5200, 1024))
    qm = part(25856, 64)
    g64 = part(25920, 3)
    g64w = part(25923, 24)
    snm = part(25947, 9, 3)
    stb = part(25956, P)
    qg = part(26084, 1)
    ssm = part(15088, PAST + B)
    spm = part(15352, PAST + B)
    spt = part(15616, 512)

    dsm, dcs, sel8, pos8 = const_of("dsm", 64), const_of("dcs", 64), const_of("sel8", 8), const_of("pos8", 64)
    dcmp = const_of("dcmp")
    cached = sem("kv_cache_loaded")
    cmp_in = sem("cmp_rows_loaded")
    padded = sem("cmp_rows_padded")
    kv_saved = sem("kv_rows_saved")
    norm6 = [qT[:, 0, :], qT[:, 1, :], qT[:, 2, :], qT[:, 3, :], kvT[:, 2, :], kvT[:, 4, :]]
    UNITS = QT * 2 * 8

    n_t, n_s, n_v = norm_steps("n", 6)
    T_ = Steps(sem("attn_tensor_step"),
               n_t + ["hs0", "hs1", "ckraw", "ckss", "cv", "vt", "g64"]
               + ["st0", "srow0", "spt0", "st1", "srow1", "spt1", "srow2", "cs", "spt2", "spv"]
               + ["cpt0"] + [n for t in range(1, QT) for n in (f"cpt{t}", f"cpv{t - 1}")] + [f"cpv{QT - 1}"])
    S_ = Steps(sem("attn_scalar_step"),
               ["kv"] + n_s + ["gates", "peb0", "hs00", "hs01", "peb1", "hs10", "hs11", "cksq", "ckstd", "cv", "vrow"]
               + ["st0", "sexp0", "spt0", "st1", "sexp1", "spt1", "sexp2", "spt2"]
               + ["ce"] + [f"cpt{t}" for t in range(QT)])
    V_ = Steps(sem("attn_vector_step"),
               n_v + ["ck", "qm", "g64", "sb0", "sn0", "sb1", "sn1", "sb2", "sn2", "so"]
               + ["cb", "cn"] + [f"co{t}" for t in range(QT)])
    s_ready, biased, negmax, probs, pt_ready, pt_copied, pv_done, comb, ot_ready, ot_copied = (
        sem(n) for n in ("scores_ready", "scores_biased", "row_max_ready", "probs_ready", "probs_transposed",
                         "probs_copied", "values_summed", "branch_added", "o_transposed", "o_copied"))

    def unit(a):
        return a // 16, a // 8 % 2, a % 8

    class Plan:
        def load(self, e, l):
            e.dma_start(winK, m["ins"]["win_k"][l].rearrange("p (b n) -> p b n", b=B)).then_inc(cached, 16)
            e.dma_start(winV, m["ins"]["win_v"][l].rearrange("p (b n) -> p b n", b=2 * B)).then_inc(cached, 16)
            e.dma_start(w1[1], m["ins"]["w1"][l, 1].rearrange("p (r n) -> p r n", r=32)).then_inc(cmp_in, 16)

        def load_page(self, e, l, i):
            page = e.value_load(m["pages"][0:1, bass.DynSlice(i, 1)], min_val=0, max_val=NPOOL - 1)
            e.dma_start(slcP[:, bass.DynSlice(i, 1), :], m["ins"]["slc_pages"][bass.DynSlice(l * NPOOL + page, 1)]
                        .rearrange("a p n -> p a n")).then_inc(cached, 16)

        def load_cmp(self, e, l):
            e.wait_ge(m["h_done"], 8 * (3 * l + 2))
            e.sem_inc(m["turns"], 1)
            e.dma_start(w1[0], m["ins"]["w1"][l, 0].rearrange("p (r n) -> p r n", r=32)).then_inc(cmp_in, 16)

        def load_cmp_pages(self, e, l, at):
            with e.Fori(at, at + PAGES) as i:
                page = e.value_load(m["pages"][0:1, bass.DynSlice(i, 1)], min_val=0, max_val=NPOOL - 1)
                e.dma_start(cmpT[:, :, bass.DynSlice(T + P * i, P)],
                            m["ins"]["cmp_pages"][bass.DynSlice(l * NPOOL + page, 1)]
                            .rearrange("a p (k n) -> p (a k) n", k=2)).then_inc(cmp_in, 16)

        def write_back(self, e, l):
            e.wait_ge(V_.sem, V_.at("nn5", l))
            e.sem_inc(m["turns"], 1)
            e.wait_ge(S_.sem, S_.at("kv", l))
            e.sem_inc(m["turns"], 1)
            e.dma_start(m["outs"]["kv"][l].rearrange("p (k n) -> p k n", k=6), kvT).then_inc(kv_saved, 16)

        def wait_left(self, e, l):
            e.wait_ge(ot_copied, QT * (l + 1))
            e.sem_inc(m["turns"], 1)
            e.wait_ge(kv_saved, 16 * (l + 1))
            e.sem_inc(m["turns"], 1)

        def tensor(self, pe, l):
            def s_(n):
                pe.wait_ge(S_.sem, S_.at(n, l))

            def v_(n):
                pe.wait_ge(V_.sem, V_.at(n, l))

            pe.wait_ge(m["const_in"], 16)
            norm_tensor(pe, l, m, T_, S_, V_, "n", 6, sqr, 2)
            pe.wait_ge(cmp_in, 16 * 18 * (l + 1))
            pe.wait_ge(padded, l + 1)
            s_("gates")
            v_("nn5")
            for k in range(2):
                for g in range(2):
                    for r in range(32):
                        o = slice(HD * g, HD * g + HD)
                        n = NBLK + (g == 0)
                        mm = pe.matmul(pair[2 + k][:, g, 0:n], w1[k][o, r, :],
                                       cmpT[o, k, r:r + 16 * (n - 1) + 1:16], start=(r == 0), stop=(r == 31))
                mm.then_inc(*T_.step(f"hs{k}"))
            w2 = [m["vec"][:, VEC["w2"][0] + HD * k:VEC["w2"][0] + HD * k + HD] for k in range(2)]
            s_("hs01")
            for g in range(2):
                mm = pe.matmul(bank(0)[HD * g:HD * g + HD, 0:NBLK], w2[0], hs[:, 0, g, :], start=True, stop=True)
            mm.then_inc(*T_.step("ckraw"))
            s_("cksq")
            pe.matmul(bank(1)[:, 0:NBLK], m["bones"], sqr[:, 0, 0:NBLK], start=True, stop=True).then_inc(*T_.step("ckss"))
            s_("hs11")
            for g in range(2):
                pe.matmul(bank(2)[0:NPB, 128 + HD * g:128 + HD * g + HD], hs[:, 1, g, 0:NPB], w2[1], start=True, stop=True)
                mm = pe.matmul(bank(3)[:, HD * g:HD * g + HD], hs[:, 1, g, 32:NBLK], w2[1], start=True, stop=True)
            mm.then_inc(*T_.step("cv"))
            v_("nn5")
            for b in range(2):
                for t in range(4):
                    pe.transpose(bank(4 + b)[:, P * t:P * t + P], kvT[:, 3 + 2 * b, P * t:P * t + P], ident)
                mm = pe.transpose(bank(6)[0:B, P * b:P * b + P], kvT[:, 3 + 2 * b, T:N], ident)
            mm.then_inc(*T_.step("vt"))
            s_("gates")
            s_("hs11")
            pe.matmul(bank(7)[0:64, 0:24], sel8, gate_tile(gate, 4)[0:B, 0:24], start=True, stop=True).then_inc(*T_.step("g64"))

            def compressed_scores(t):
                for p in range(8):
                    c, g = p // 2, p % 2
                    o = slice(HD * g, HD * g + HD)
                    at = NPB * (4 * t + c)
                    mm = pe.matmul(bank(4 + g)[:, at:at + NPB], qT[o, c, P * t:P * t + P], ckT[o, 0:NPB],
                                   start=True, stop=True)
                return mm

            v_("ck")
            v_("qm")
            s_("vrow")
            pe.wait_ge(cached, 16 * 18 * (l + 1))
            for b in range(3):
                if b < 2:
                    if b:
                        s_("st0")
                    for k in range(2):
                        for s in range(B):
                            kk = slcP[:, 2 * s + k, 0:P] if b == 0 else winK[:, s, P * k:P * k + P]
                            mm = pe.matmul(bank(0)[:, 64 * k + 8 * s:64 * k + 8 * s + 8], kk, qm[:, 8 * s:8 * s + 8],
                                           start=True, stop=True)
                    mm.then_inc(*T_.step(f"st{b}"))
                    s_(f"st{b}")
                    if b:
                        v_("sb0")
                    pe.matmul(bank(1)[0:64, PAST:PAST + B], qm, kvT[:, 2 + 2 * b, T:N], start=True, stop=True)
                    for k in range(2):
                        mm = pe.transpose(bank(1)[0:64, P * k:P * k + P], stb[:, 64 * k:64 * k + 64], ident)
                    mm.then_inc(*T_.step(f"srow{b}"))
                else:
                    v_("sb1")
                    pe.matmul(bank(1)[0:64, 0:P], qm, ckT[:, 32:NBLK], start=True, stop=True).then_inc(*T_.step("srow2"))
                for t in ((0,), (1, 2), (3,))[b]:
                    mm = compressed_scores(t)
                if b == 2:
                    mm.then_inc(*T_.step("cs"))
                v_(f"sn{b}")
                if b:
                    s_(f"spt{b - 1}")
                for k in range(2 if b < 2 else 1):
                    mm = pe.matmul(bank(2)[:, 64 * k:64 * k + 64], spm[0:64, P * k:P * k + P], ident[0:64, 0:64],
                                   start=True, stop=True)
                if b < 2:
                    mm = pe.matmul(bank(2)[0:B, 128:192], spm[0:64, PAST:PAST + B], ident[0:64, 0:64],
                                   start=True, stop=True)
                mm.then_inc(*T_.step(f"spt{b}"))
            s_("spt2")
            pe.matmul(bank(3)[:, 0:64], cvs, spt[:, 384:448], start=True, stop=False, skip_group_check=True)
            for b in range(2):
                pe.matmul(bank(3)[:, 0:64], vrow[0:B, b, 4, :], spt[0:B, 192 * b + 128:192 * b + 192],
                          start=False, stop=False, skip_group_check=True)
                for k in range(2):
                    for s in range(B):
                        vv = slcP[:, 2 * s + k, P:2 * P] if b == 0 else winV[:, 2 * s + k, :]
                        mm = pe.matmul(bank(3)[:, 8 * s:8 * s + 8], vv, spt[:, 192 * b + 64 * k + 8 * s:192 * b + 64 * k + 8 * s + 8],
                                       start=False, stop=(b == 1 and k == 1), skip_group_check=True)
            mm.then_inc(*T_.step("spv"))

            v_("so")
            v_("cn")
            for i in range(QT + 1):
                if i < QT:
                    if i >= 2:
                        s_(f"cpt{i - 2}")
                    for p in range(8):
                        at = NPB * (8 * i + p)
                        mm = pe.transpose(pair[1 - i % 2][0:NPB, p // 4, P * (p % 4):P * (p % 4) + P],
                                          pcb[:, at:at + NPB], ident)
                    mm.then_inc(*T_.step(f"cpt{i}"))
                if i:
                    t = i - 1
                    s_(f"cpt{t}")
                    for p in range(8):
                        mm = pe.matmul(bank(4 + t)[:, HD * p:HD * p + HD], ptc[t % 2][0:NPB, P * p:P * p + P],
                                       cvp[0:NPB, HD * (p % 2):HD * (p % 2) + HD], start=True, stop=True)
                    mm.then_inc(*T_.step(f"cpv{t}"))

            v_(f"co{QT - 1}")

            def scores(a):
                t, b, p = unit(a)
                if a >= 3:
                    pe.wait_ge(biased, UNITS * l + a - 2)
                w = P * (t + 1)
                o = slice(HD * (p % 2), HD * (p % 2) + HD)
                pe.matmul(bank(a % 3)[:, 0:w], qT[o, p // 2, P * t:P * t + P], kvT[o, 2 + 2 * b, 0:w],
                          start=True, stop=True).then_inc(s_ready, 1)

            def turn(a):
                t, _, _ = unit(a)
                pe.wait_ge(probs, UNITS * l + a + 1)
                if a >= 2:
                    pe.wait_ge(pt_copied, UNITS * l + a - 1)
                for k in range(t + 1):
                    mm = pe.transpose(bank(3 + a % 2)[:, P * k:P * k + P], prb[:, a % 3, P * k:P * k + P], ident)
                mm.then_inc(pt_ready, 1)

            def values(a):
                t, b, p = unit(a)
                c = a // 8
                pe.wait_ge(pt_copied, UNITS * l + a + 1)
                if p == 0 and c >= 2:
                    pe.wait_ge(comb, 8 * l + c - 1)
                for k in range(t + 1):
                    mm = pe.matmul(bank(5 + c % 2)[:, HD * p:HD * p + HD], ptb[:, a % 3, P * k:P * k + P],
                                   vrow[:, b, k, HD * (p % 2):HD * (p % 2) + HD], start=(k == 0), stop=(k == t))
                mm.then_inc(pv_done, 1)

            def o_turn(t):
                pe.wait_ge(comb, 8 * l + 2 * t + 2)
                if t:
                    pe.wait_ge(ot_copied, QT * l + t)
                for c in range(4):
                    mm = pe.transpose(bank(7)[:, P * c:P * c + P], oacc[:, t, P * c:P * c + P], ident)
                mm.then_inc(ot_ready, 1)

            for i in range(UNITS + 4):
                if i < UNITS:
                    scores(i)
                if 2 <= i < UNITS + 2:
                    turn(i - 2)
                if i >= 4:
                    values(i - 4)
                if i >= 28 and (i - 28) % 16 == 0:
                    o_turn((i - 28) // 16)
            o_turn(QT - 1)

        def scalar(self, e, l):
            def t_(n):
                e.wait_ge(T_.sem, T_.at(n, l))

            def v_(n):
                e.wait_ge(V_.sem, V_.at(n, l))

            for zi in range(10):
                e.wait_ge(m["z_ready"], ZT * l + zi + 1)
                if zi in (4, 5):
                    e.activation(cmpT[:, zi - 4, 0:HALF], pair[zi % 2][:, 0, 0:HALF], ACT.Copy)
                    e.activation(cmpT[:, zi - 4, HALF:T], pair[zi % 2][:, 1, 0:T - HALF], ACT.Copy)
                dst = qT[:, zi, :] if zi < 4 else kvT[:, zi - 4, :]
                e.activation(halves(dst), both(zi % 2), ACT.Copy).then_inc(m["z_used"], 1)
                m["split_hi"](e, l * TILES + m["z_tile"](zi), m["z_tile"](zi))
            e.drain().then_inc(*S_.step("kv"))

            norm_scalar(e, l, m, T_, S_, "n", norm6, sqr, 1.0 / HD, 2)
            e.wait_ge(m["small_ready"], l + 1)
            for at in (m["z_tile"](9) + 1, m["z_tile"](9) + 2):
                m["split_hi"](e, l * TILES + at, at)
            e.activation(m["small"][:, 0:128], bank(0)[:, 0:128], ACT.Copy)
            e.activation(m["small"][0:B, 128:160], bank(0)[0:B, 128:160], ACT.Copy)
            e.drain()
            e.activation(m["gate"][:, :].rearrange("p (t n) -> p t n", t=5),
                         m["small"][:, :].rearrange("p (t n) -> p t n", t=5)[:, :, 0:28], ACT.Sigmoid).then_inc(*S_.step("gates"))
            for k in range(2):
                t_(f"hs{k}")
                e.activation(peb[:, k:k + 1], pair[2 + k][:, 0, NBLK:NBLK + 1], ACT.Copy).then_inc(*S_.step(f"peb{k}"))
                e.drain()
                for g in range(2):
                    e.activation(hs[:, k, g, :], pair[2 + k][:, g, 0:NBLK], ACT.Silu,
                                 bias=peb[:, k:k + 1]).then_inc(*S_.step(f"hs{k}{g}"))
            t_("ckraw")
            e.activation(sqr[:, 0, 0:NBLK], bank(0)[:, 0:NBLK], ACT.Square).then_inc(*S_.step("cksq"))
            t_("ckss")
            e.activation(m["rstd"][:, 0:NBLK], bank(1)[:, 0:NBLK], ACT.Sqrt, bias=m["eps"][:, :],
                         scale=1.0 / HD).then_inc(*S_.step("ckstd"))
            t_("cv")
            e.activation(cvp[0:NPB, :], bank(2)[0:NPB, 128:256], ACT.Copy)
            e.activation(cvs, bank(3)[:, 0:P], ACT.Copy).then_inc(*S_.step("cv"))
            t_("vt")
            for b in range(2):
                e.activation(vrow[:, b, 0:4, :], bank(4 + b).rearrange("p (t n) -> p t n", t=4), ACT.Copy)
            e.activation(vrow[0:B, :, 4, :], bank(6)[0:B, 0:2 * P].rearrange("p (b n) -> p b n", b=2),
                         ACT.Copy).then_inc(*S_.step("vrow"))
            for b in range(3):
                if b < 2:
                    t_(f"st{b}")
                    if b:
                        t_("srow0")
                    e.activation(stb, bank(0)[:, 0:P], ACT.Copy).then_inc(*S_.step(f"st{b}"))
                v_(f"sb{b}")
                w = PAST + B if b < 2 else P
                e.activation(spm[0:64, 0:w], ssm[0:64, 0:w], ACT.Exp, bias=snm[0:64, b, 0:1],
                             accum_out=snm[0:64, b, 1:2]).then_inc(*S_.step(f"sexp{b}"))
                t_(f"spt{b}")
                e.activation(spt[:, 192 * b:192 * b + (128 if b < 2 else 64)], bank(2)[:, 0:(128 if b < 2 else 64)], ACT.Copy) \
                    .then_inc(*(S_.step("spt2") if b == 2 else (spare, 1)))
                if b < 2:
                    e.activation(spt[0:B, 192 * b + 128:192 * b + 192], bank(2)[0:B, 128:192],
                                 ACT.Copy).then_inc(*S_.step(f"spt{b}"))
            v_("cb")
            e.activation(pcb, scb, ACT.Exp).then_inc(*S_.step("ce"))
            for t in range(QT):
                t_(f"cpt{t}")
                if t >= 2:
                    t_(f"cpv{t - 2}")
                e.activation(ptc[t % 2][0:NPB, :].rearrange("p (a n) -> p a n", a=2), pair[1 - t % 2][0:NPB, :, :],
                             ACT.Copy).then_inc(*S_.step(f"cpt{t}"))

            def exp(a):
                w = P * (unit(a)[0] + 1)
                e.wait_ge(negmax, UNITS * l + a + 1)
                if a >= 3:
                    e.wait_ge(pt_ready, UNITS * l + a - 2)
                e.activation(prb[:, a % 3, 0:w], ssb[:, a % 3, 0:w], ACT.Exp, bias=nm[:, a:a + 1],
                             accum_out=rs[:, a:a + 1]).then_inc(probs, 1)

            def copy_pt(a):
                w = P * (unit(a)[0] + 1)
                e.wait_ge(pt_ready, UNITS * l + a + 1)
                if a >= 3:
                    e.wait_ge(pv_done, UNITS * l + a - 2)
                e.activation(ptb[:, a % 3, 0:w], bank(3 + a % 2)[:, 0:w], ACT.Copy).then_inc(pt_copied, 1)

            def o_copy(t):
                e.wait_ge(ot_ready, QT * l + t + 1)
                e.activation(o_a[:, :, P * t:P * t + P], bank(7).rearrange("p (c n) -> p c n", c=4),
                             ACT.Copy).then_inc(ot_copied, 1)

            for i in range(UNITS + 2):
                if i < UNITS:
                    exp(i)
                if i >= 2:
                    copy_pt(i - 2)
                if i >= 30 and (i - 30) % 16 == 0:
                    o_copy((i - 30) // 16)
            o_copy(QT - 1)

        def vector(self, e, l):
            def t_(n):
                e.wait_ge(T_.sem, T_.at(n, l))

            def s_(n):
                e.wait_ge(S_.sem, S_.at(n, l))

            e.wait_ge(m["const_in"], 16)
            e.memset(cmpT[:, :, T + B * PAST:CMPW], 0.0)
            e.drain()
            e.tensor_copy(cmpT[0:HD, :, T + B * PAST:CMPW],
                          m["vec_of"]("pe")[0:HD, :].rearrange("p (k r) -> p k r", k=2)).then_inc(padded, 1)
            e.tensor_scalar(qg, scalar_of("qg"), HD ** -0.5, None, ALU.mult)
            norm_vector(e, l, m, T_, S_, V_, "n", norm6, lambda i: qg if i < 4 else scalar_of("kg", i - 3),
                        lambda i: None, 2)
            s_("ckstd")
            e.reciprocal(m["rstd"][:, 0:NBLK], m["rstd"][:, 0:NBLK])
            e.drain()
            e.scalar_tensor_tensor(ckT, bank(0)[:, 0:NBLK], scalar_of("kg", 0), m["rstd"][:, 0:NBLK],
                                   ALU.mult, ALU.mult).then_inc(*V_.step("ck"))
            q4 = qm.rearrange("p (b c g) -> p b c g", c=4, g=2)
            e.memset(qm, 0.0)
            e.drain()
            for g in range(2):
                o = slice(HD * g, HD * g + HD)
                mm = e.tensor_copy(q4[o, :, :, g], qT[o, :, T:N].rearrange("p c b -> p b c"))
            e.drain().then_inc(*V_.step("qm"))
            t_("g64")
            gw = g64w[0:64, :].rearrange("p (b n) -> p b n", b=3)
            e.tensor_tensor(gw, bank(7)[0:64, 0:24].rearrange("p (b n) -> p b n", b=3),
                            pos8.unsqueeze(1).to_broadcast([64, 3, 8]), ALU.mult)
            e.drain()
            e.tensor_reduce(g64[0:64, :], gw, AX_X, ALU.add).then_inc(*V_.step("g64"))
            for b in range(3):
                w = PAST + B if b < 2 else P
                t_(f"srow{b}")
                e.tensor_tensor(ssm[0:64, 0:w], bank(1)[0:64, 0:w], dsm if b < 2 else dcs, ALU.add)
                e.drain()
                e.tensor_reduce(snm[0:64, b, 0:1], ssm[0:64, 0:w], AX_X, ALU.max, negate=True).then_inc(*V_.step(f"sb{b}"))
                s_(f"sexp{b}")
                e.reciprocal(snm[0:64, b, 2:3], snm[0:64, b, 1:2])
                e.drain()
                gi = (1, 2, 0)[b]
                e.tensor_scalar(spm[0:64, 0:w], spm[0:64, 0:w], snm[0:64, b, 2:3], g64[0:64, gi:gi + 1],
                                ALU.mult, ALU.mult).then_inc(*V_.step(f"sn{b}"))
            t_("spv")
            for g in range(2):
                o = slice(HD * g, HD * g + HD)
                e.tensor_copy(o_a[o, :, T:N].rearrange("p c b -> p b c"),
                              bank(3)[o, 0:64].rearrange("p (b c g) -> p b c g", c=4, g=2)[:, :, :, g])
            e.drain().then_inc(*V_.step("so"))
            s32 = scb.rearrange("p (h n) -> p h n", n=NPB)
            p32 = pcb.rearrange("p (h n) -> p h n", n=NPB)
            t_("cs")
            for g in range(2):
                e.tensor_tensor(scb.rearrange("p (c g n) -> p g c n", g=2, n=NPB)[:, g],
                                bank(4 + g)[:, 0:4 * QT * NPB].rearrange("p (c n) -> p c n", n=NPB),
                                dcmp.rearrange("p (c g n) -> p g c n", g=2, n=NPB)[:, g], ALU.add)
            e.drain()
            e.tensor_reduce(nm[:, 0:32], s32, AX_X, ALU.max, negate=True)
            e.drain()
            e.tensor_scalar(nm[:, 32:64], nm[:, 0:32], 1e20, None, ALU.min)
            e.drain()
            e.tensor_tensor(s32, s32, nm[:, 32:64].unsqueeze(2).to_broadcast([P, 32, NPB]), ALU.add).then_inc(*V_.step("cb"))
            s_("ce")
            e.tensor_reduce(rs[:, 0:32], p32, AX_X, ALU.add)
            e.drain()
            e.tensor_scalar(rs[:, 32:64], rs[:, 0:32], 1e-30, None, ALU.max)
            e.drain()
            e.reciprocal(fac[:, 0:32], rs[:, 32:64])
            e.drain()
            e.tensor_tensor(fac[:, 32:64].rearrange("p (t n) -> p t n", t=QT), fac[:, 0:32].rearrange("p (t n) -> p t n", t=QT),
                            gate[:, 0:28 * QT].rearrange("p (t n) -> p t n", t=QT)[:, :, 0:8], ALU.mult)
            e.drain()
            e.tensor_tensor(p32, p32, fac[:, 32:64].unsqueeze(2).to_broadcast([P, 32, NPB]), ALU.mult).then_inc(*V_.step("cn"))
            for t in range(QT):
                t_(f"cpv{t}")
                e.tensor_copy(oacc[:, t, :], bank(4 + t)).then_inc(*V_.step(f"co{t}"))
            e.drain()

            def bias(a):
                t, b, p = unit(a)
                w = P * (t + 1)
                e.wait_ge(s_ready, UNITS * l + a + 1)
                if a >= 3:
                    e.wait_ge(probs, UNITS * l + a - 2)
                e.scalar_tensor_tensor(ssb[:, a % 3, 0:w], m["dist"][:, T - w:T], slope(p), bank(a % 3)[:, 0:w],
                                       ALU.mult, ALU.add).then_inc(biased, 1)

            def rowmax(a):
                w = P * (unit(a)[0] + 1)
                e.wait_ge(biased, UNITS * l + a + 1)
                e.tensor_reduce(nm[:, a:a + 1], ssb[:, a % 3, 0:w], AX_X, ALU.max, negate=True).then_inc(negmax, 1)

            def combine(c):
                t, b = c // 2, c % 2
                e.wait_ge(pv_done, UNITS * l + 8 * c + 8)
                e.reciprocal(fac[:, 0:8], rs[:, 8 * c:8 * c + 8])
                e.drain()
                e.tensor_tensor(fac[:, 8:16], fac[:, 0:8], gate_tile(gate, t)[:, 8 + 8 * b:16 + 8 * b], ALU.mult)
                e.drain()
                e.tensor_tensor(tmp.rearrange("p (h n) -> p h n", h=8), bank(5 + c % 2).rearrange("p (h n) -> p h n", h=8),
                                fac[:, 8:16].unsqueeze(2).to_broadcast([P, 8, HD]), ALU.mult)
                e.drain()
                e.tensor_tensor(oacc[:, t, :], oacc[:, t, :], tmp, ALU.add).then_inc(comb, 1)

            for i in range(UNITS + 6):
                if i < UNITS:
                    bias(i)
                if 1 <= i <= UNITS:
                    rowmax(i - 1)
                if i >= 13 and (i - 13) % 8 == 0:
                    combine((i - 13) // 8)
            e.drain()

    spare = sem("sample_probs_copied")
    p = Plan()
    p.kv_saved = kv_saved
    p.ot_copied = ot_copied
    return p


def state_steps(kind):
    vb = [f"vb{i}" for i in range(8)]
    return vb + ["so"], ["so"], ["sdec"] + [f"sa{i}" for i in range(8)]


def state_tensor(pe, l, m, T_, V_, S_, ss, vcol, q, banks):
    for i in range(8):
        pe.wait_ge(V_.sem, V_.at("sdec" if i < 2 else f"sa{i - 2}", l))
        for j in range(4):
            mm = pe.matmul(m["bank"](banks[i % 2])[:, P * j:P * j + P], vcol(4 * i + j).to_broadcast([P, P]), m["ident"],
                           start=True, stop=True)
        mm.then_inc(*T_.step(f"vb{i}"))
    pe.wait_ge(V_.sem, V_.at("sa7", l))
    for i in range(32):
        mm = pe.matmul(m["bank"](banks[2])[:, i:i + 1], ss[:, i, :], q[:, i // 8, T + i % 8:T + i % 8 + 1],
                       start=True, stop=True)
    mm.then_inc(*T_.step("so"))


def state_vector(e, l, m, T_, V_, ss, decay, k, tmp, banks):
    e.tensor_tensor(ss, ss, decay.unsqueeze(2).to_broadcast([P, 32, P]), ALU.mult).then_inc(*V_.step("sdec"))
    for i in range(8):
        e.wait_ge(T_.sem, T_.at(f"vb{i}", l))
        kc = k[:, i // 2, T + 4 * (i % 2):T + 4 * (i % 2) + 4]
        e.tensor_tensor(tmp[:, i % 2, :].rearrange("p (i n) -> p i n", i=4),
                        m["bank"](banks[i % 2]).rearrange("p (i n) -> p i n", i=4),
                        kc.unsqueeze(2).to_broadcast([P, 4, P]), ALU.mult)
        e.drain()
        e.tensor_tensor(ss[:, 4 * i:4 * i + 4, :], ss[:, 4 * i:4 * i + 4, :],
                        tmp[:, i % 2, :].rearrange("p (i n) -> p i n", i=4), ALU.add).then_inc(*V_.step(f"sa{i}"))


def state_scalar(e, l, m, T_, S_, o, banks):
    e.wait_ge(T_.sem, T_.at("so", l))
    e.activation(o[:, :, T:N], m["bank"](banks[2])[:, 0:32].rearrange("p (h b) -> p h b", h=4),
                 ACT.Copy).then_inc(*S_.step("so"))


def norm_steps(name, n):
    return ([f"{name}s{i}" for i in range(n)] + [f"{name}b{i}" for i in range(n)],
            [f"{name}q{i}" for i in range(n)] + [f"{name}d"], [f"{name}r"] + [f"{name}n{i}" for i in range(n)])


def norm_tensor(pe, l, m, T_, S_, V_, name, n, sqr, groups=1):
    at = lambda i, j: groups * (len(SUMS) * i + j)
    src = m["ones"][:, 0:1] if groups == 1 else m["bones"][:, 0:P:P // groups]
    for i in range(n):
        pe.wait_ge(S_.sem, S_.at(f"{name}q{i}", l))
        for j, c in enumerate(SUMS):
            mm = pe.matmul(m["bank"](7)[:, at(i, j):at(i, j) + groups], sqr[:, i % 2, c:c + P], src, start=True, stop=True)
        mm.then_inc(*T_.step(f"{name}s{i}"))
    for i in range(n):
        pe.wait_ge(V_.sem, V_.at(f"{name}r" if i < 2 else f"{name}n{i - 2}", l))
        spread(pe, m["pair"][2 + i % 2], m["ident"], m["rstd"][:, at(i, 0):at(i + 1, 0)],
               groups).then_inc(*T_.step(f"{name}b{i}"))


def norm_scalar(e, l, m, T_, S_, name, bufs, sqr, scale, groups=1):
    for i, b in enumerate(bufs):
        if i >= 2:
            e.wait_ge(T_.sem, T_.at(f"{name}s{i - 2}", l))
        e.activation(sqr[:, i % 2, :], b, ACT.Square).then_inc(*S_.step(f"{name}q{i}"))
    e.wait_ge(T_.sem, T_.at(f"{name}s{len(bufs) - 1}", l))
    w = groups * len(SUMS) * len(bufs)
    e.activation(m["rstd"][:, 0:w], m["bank"](7)[:, 0:w], ACT.Sqrt, bias=m["eps"][:, :],
                 scale=scale).then_inc(*S_.step(f"{name}d"))


def norm_vector(e, l, m, T_, S_, V_, name, bufs, gain, after, groups=1):
    e.wait_ge(S_.sem, S_.at(f"{name}d", l))
    w = groups * len(SUMS) * len(bufs)
    e.reciprocal(m["rstd"][:, 0:w], m["rstd"][:, 0:w]).then_inc(*V_.step(f"{name}r"))
    for i, b in enumerate(bufs):
        e.wait_ge(T_.sem, T_.at(f"{name}b{i}", l))
        h = m["halves"](b)
        e.scalar_tensor_tensor(h, h, gain(i), m["both"](2 + i % 2), ALU.mult, ALU.mult)
        if after(i) is None:
            e.drain().then_inc(*V_.step(f"{name}n{i}"))
        else:
            e.drain()
            e.tensor_tensor(b, b, after(i), ALU.mult).then_inc(*V_.step(f"{name}n{i}"))


def delta_plan(m):
    part, sem, bank, pair, both, halves = m["part"], m["sem"], m["bank"], m["pair"], m["both"], m["halves"]
    scalar_of, vec_of, gate, ident, ones, upper, level, o_d = (
        m["scalar_of"], m["vec_of"], m["gate"], m["ident"], m["ones"], m["upper"], m["level"], m["o_d"])

    cx = part(0, 12 * 515, 12)
    xs = part(6180, 12 * B * 4).rearrange("p (c b j) -> p c b j", c=12, b=B)
    cy = part(6564, 12 * N, 12)
    dz = part(12804, 4 * N, 4)
    ss = part(14884, 32 * P, 32)
    sqr = part(18980, 2 * N, 2)

    def four(at):
        return part(at, 512, 4)

    S, dec, at_0, lt0, ta0, tb0, yb0, ls0, ls1, rb, vn, eg = (four(20020 + 512 * i) for i in range(12))
    ktl, vr, qt = (four(0), four(1536)), (four(512), four(2048)), (four(1024), four(3024))
    at_, lt, ta, tb = (at_0, four(3536)), (lt0, four(4048)), (ta0, four(4560)), (tb0, four(5072))
    ls = ((ls0, ls1), (four(5584), four(18980)))
    yb = (yb0, dec)
    tmp = part(1536, 1024, 2)
    cin = part(21044, 288)
    cout = part(2700, 36 + 288)
    xw = part(21400, 128).rearrange("p (c b j) -> p c b j", c=4, b=B)
    gx, ga, gl, gd = (part(26164 + 20 * i, 20) for i in range(4))
    gc, egc, ktf, neg0, ea = (part(26244 + 4 * i, 4) for i in range(5))
    neg = (neg0, part(26328, 4))
    egl = (part(26332, 4), part(26336, 4))
    egs = part(26264, 32)
    vns = part(26296, 32)

    n_t, n_s, n_v = norm_steps("l", 8)
    o_t, o_s, o_v = norm_steps("o", 4)
    st_t, st_s, st_v = state_steps("d")
    lv = range(1, 7)

    def of_tiles(before, levels, after):
        return [f"{n}.{t}" for u in range(0, QT, 2) for names in [before] + levels + [after]
                for t, n in ([(t, n) for n in names for t in (u, u + 1)] if names in levels else
                             [(t, n) for t in (u, u + 1) for n in names])]

    tile_t = of_tiles(["gb", "kk", "rows", "y0"], [[f"y{i}", f"ty{i}"] for i in lv], ["ks", "vn", "o", "s"])
    tile_s = of_tiles(["exp", "vr"], [[f"y{i}"] for i in lv], ["vn", "o"])
    tile_v = of_tiles(["dec", "lt", "qt", "kt", "t0"], [[f"t{i}"] for i in lv], ["r", "s"])
    T_ = Steps(sem("delta_tensor_step"), n_t + tile_t + ["sk"] + st_t + o_t)
    S_ = Steps(sem("delta_scalar_step"), ["ge", "gl"] + ["silu0", "silu1", "silu2"] + n_s
               + tile_s + ["seg"] + st_s + o_s)
    V_ = Steps(sem("delta_vector_step"), ["pad", "ga", "cin", "conv0", "conv1", "conv2", "g"] + n_v
               + tile_v + ["svn"] + st_v + o_v)
    P_ = Steps(sem("delta_pool_step"), [f"ls{i}.{t + j}" for t in range(0, QT, 2) for i in range(7) for j in range(2)])
    conv_in, states_in, saved = sem("conv_state_loaded"), sem("delta_states_loaded"), sem("delta_outputs_saved")

    def each_head(ap):
        return ap.unsqueeze(1).to_broadcast([P, 4, P])

    def cols(ap):
        return ap.unsqueeze(2).to_broadcast([P, 4, P])

    def heads(i):
        return bank(i).rearrange("p (h n) -> p h n", h=4)

    class Plan:
        def load(self, e, l):
            m["A"].wait_left(e, l)
            e.dma_start(cin, m["ins"]["conv_in"][l]).then_inc(conv_in, 16)
            e.dma_start(ss, m["ins"]["dn_in"][l].rearrange("p (i n) -> p i n", i=32)).then_inc(states_in, 16)

        def write_back(self, e, l):
            e.wait_ge(S_.sem, S_.at("so", l))
            e.sem_inc(m["turns"], 1)
            e.dma_start(m["outs"]["conv_p"][l], cout[:, 0:36]).then_inc(saved, 16)
            e.dma_start(m["outs"]["conv_s"][l], cout[:, 36:324]).then_inc(saved, 16)
            e.dma_start(m["outs"]["dn_p"][l].rearrange("p (h n) -> p h n", h=4), S).then_inc(saved, 16)
            e.dma_start(m["outs"]["dn_s"][l].rearrange("p (i n) -> p i n", i=32), ss).then_inc(saved, 16)

        def pool(self, e, l):
            for u in range(0, QT, 2):
                for i in range(7):
                    for t in (u, u + 1):
                        if i == 0:
                            e.wait_ge(V_.sem, V_.at(f"lt.{t}", l))
                        if i >= 2:
                            e.wait_ge(T_.sem, T_.at(f"y{i - 2}.{t}", l))
                        if i == 2:
                            e.wait_ge(V_.sem, V_.at(f"t0.{t}", l))
                        e.tensor_tensor(ls[t % 2][i % 2], lt[t % 2], each_head(level[:, i, :]),
                                        ALU.mult).then_inc(*P_.step(f"ls{i}.{t}"))

        def tensor(self, pe, l):
            def w(steps, n):
                pe.wait_ge(steps.sem, steps.at(n, l))

            norm_tensor(pe, l, m, T_, S_, V_, "l", 8, sqr)
            w(V_, "g")
            w(V_, "ln7")

            def k_of(t):
                return [cy[:, 4 + h, P * t:P * t + P] for h in range(4)]

            def prepare(t):
                k, z = k_of(t), t % 2
                q = [cy[:, h, P * t:P * t + P] for h in range(4)]
                v = [cy[:, 8 + h, P * t:P * t + P] for h in range(4)]
                if z:
                    w(V_, f"lt.{t - 1}")
                    w(S_, f"exp.{t - 1}")
                elif t:
                    w(V_, f"t6.{t - 1}")
                    w(S_, f"o.{t - 1}")
                pe.matmul(bank(7)[:, 0:4], upper, gd[:, 4 * t:4 * t + 4], start=True, stop=True)
                for h in range(4):
                    pe.matmul(heads(6)[:, h, :], gd[:, 4 * t + h:4 * t + h + 1].to_broadcast([P, P]), upper,
                              start=True, stop=True)
                    b = gate_tile(gate, t)[:, 24 + h:25 + h]
                    mm = pe.matmul(heads(5)[:, h, :], b.to_broadcast([P, P]), ident, start=True, stop=True)
                mm.then_inc(*T_.step(f"gb.{t}"))
                if t and not z:
                    w(V_, f"s.{t - 1}")
                for h in range(4):
                    pe.matmul(heads(4)[:, h, :], k[h], k[h], start=True, stop=True)
                    mm = pe.matmul(heads(3)[:, h, :], k[h], q[h], start=True, stop=True)
                mm.then_inc(*T_.step(f"kk.{t}"))
                if z:
                    w(V_, f"kt.{t - 1}")
                    w(S_, f"vr.{t - 1}")
                for h in range(4):
                    pe.transpose(heads(2)[:, h, :], k[h], ident)
                    mm = pe.transpose(heads(1)[:, h, :], v[h], ident)
                mm.then_inc(*T_.step(f"rows.{t}"))
                w(P_, f"ls0.{t}")
                if z:
                    w(V_, f"t0.{t - 1}")
                for h in range(4):
                    mm = pe.matmul(heads(0)[:, h, :], ls[z][0][:, h, :], ident, start=True, stop=True)
                mm.then_inc(*T_.step(f"y0.{t}"))

            def samples_sk(first):
                for i in range(first, first + 8):
                    pe.matmul(bank(7)[:, 64 + i:65 + i], ss[:, i, :], cy[:, 4 + i // 8, T + i % 8:T + i % 8 + 1],
                              start=True, stop=True)

            def output(t):
                k, z = k_of(t), t % 2
                if t == QT - 2:
                    w(V_, f"t6.{QT - 1}")
                    pe.wait_ge(states_in, 16 * (l + 1))
                if t:
                    w(V_, f"s.{t - 1}")
                for h in range(4):
                    mm = pe.matmul(heads(4)[:, h, :], k[h], S[:, h, :], start=True, stop=True)
                mm.then_inc(*T_.step(f"ks.{t}"))
                if t >= QT - 2:
                    samples_sk(16 * (t - QT + 2))
                w(V_, f"r.{t}")
                for h in range(4):
                    mm = pe.matmul(heads(3)[:, h, :], tb[z][:, h, :], rb[:, h, :], start=True, stop=True)
                mm.then_inc(*T_.step(f"vn.{t}"))
                if t >= QT - 2:
                    samples_sk(16 * (t - QT + 2) + 8)
                w(S_, f"vn.{t}")
                for h in range(4):
                    pe.matmul(heads(5)[:, h, :], S[:, h, :], qt[z][:, h, :], start=True, stop=False)
                    mm = pe.matmul(heads(5)[:, h, :], vn[:, h, :], at_[z][:, h, :], start=False, stop=True)
                mm.then_inc(*T_.step(f"o.{t}"))
                for h in range(4):
                    mm = pe.matmul(heads(4)[:, h, :], ktl[z][:, h, :], vn[:, h, :], start=True, stop=True)
                mm.then_inc(*T_.step(f"s.{t}"))

            yk, tak, tbk = (0, 1), (6, 2), (7, 5)
            for u in range(0, QT, 2):
                prepare(u)
                prepare(u + 1)
                w(V_, f"t0.{u + 1}")
                w(S_, f"vr.{u + 1}")
                for i in lv:
                    for t in (u, u + 1):
                        z = t % 2
                        if i > 1:
                            w(V_, f"t{i - 1}.{t}")
                        w(P_, f"ls{i}.{t}")
                        for h in range(4):
                            mm = pe.matmul(heads(yk[z])[:, h, :], ls[z][i % 2][:, h, :], ta[z][:, h, :],
                                           start=True, stop=True)
                        mm.then_inc(*T_.step(f"y{i}.{t}"))
                    for t in (u, u + 1):
                        z = t % 2
                        w(S_, f"y{i}.{t}")
                        for h in range(4):
                            if i < 6:
                                pe.matmul(heads(tak[z])[:, h, :], tb[z][:, h, :], yb[z][:, h, :], start=True, stop=True)
                            mm = pe.matmul(heads(tbk[z])[:, h, :], yb[z][:, h, :], tb[z][:, h, :], start=True, stop=True)
                        mm.then_inc(*T_.step(f"ty{i}.{t}"))
                output(u)
                output(u + 1)
            for h in range(4):
                pe.matmul(bank(7)[:, 8 * h:8 * h + 8], gd[0:B, 16 + h:17 + h].to_broadcast([B, P]), ident[0:B, 0:B],
                          start=True, stop=True)
                mm = pe.matmul(bank(7)[:, 32 + 8 * h:40 + 8 * h], gate_tile(gate, 4)[0:B, 24 + h:25 + h].to_broadcast([B, P]),
                          ident[0:B, 0:B], start=True, stop=True)
            mm.then_inc(*T_.step("sk"))
            w(S_, "o.3")
            state_tensor(pe, l, m, T_, V_, S_, ss, lambda i: vns[:, i:i + 1], cy, (5, 6, 0))
            norm_tensor(pe, l, m, T_, S_, V_, "o", 4, sqr)

        def scalar(self, e, l):
            def w(steps, n):
                e.wait_ge(steps.sem, steps.at(n, l))

            e.wait_ge(m["A"].kv_saved, 16 * (l + 1))
            w(V_, "ga")
            e.activation(ga, ga, ACT.Exp, scale=-1.0)
            e.activation(ea, vec_of("alog"), ACT.Exp).then_inc(*S_.step("ge"))
            e.drain()
            e.activation(gl, ga, ACT.Ln, bias=ones[:, 0:1]).then_inc(*S_.step("gl"))
            for zi in range(10, 26):
                e.wait_ge(m["z_ready"], ZT * l + zi + 1)
                c = zi - 10
                if c == 0:
                    w(V_, "pad")
                if c < 12:
                    e.activation(cx[:, c, 3:3 + HALF], pair[zi % 2][:, 0, 0:HALF], ACT.Copy)
                    e.activation(cx[:, c, 3 + HALF:3 + T], pair[zi % 2][:, 1, 0:T - HALF], ACT.Copy)
                    e.activation(xs[:, c, :, 3], pair[zi % 2][:, 1, T - HALF:HALF], ACT.Copy).then_inc(m["z_used"], 1)
                else:
                    e.activation(halves(dz[:, c - 12, :]), both(zi % 2), ACT.Silu).then_inc(m["z_used"], 1)
                m["split_hi"](e, l * TILES + m["z_tile"](zi), m["z_tile"](zi))
                if zi in (18, 22, 25):
                    g = (18, 22, 25).index(zi)
                    w(V_, f"conv{g}")
                    e.activation(cy[:, 4 * g:4 * g + 4, :], cy[:, 4 * g:4 * g + 4, :], ACT.Silu).then_inc(*S_.step(f"silu{g}"))
            e.drain()
            norm_scalar(e, l, m, T_, S_, "l", [cy[:, i, :] for i in range(8)], sqr, 1.0)
            for u in range(0, QT, 2):
                for t in (u, u + 1):
                    w(V_, f"dec.{t}")
                    if t == u and t:
                        w(T_, f"o.{t - 1}")
                    e.activation(dec, dec, ACT.Exp)
                    e.activation(eg, heads(6), ACT.Exp)
                    e.activation(egc, gc, ACT.Exp)
                    e.activation(ktf, ktf, ACT.Exp).then_inc(*S_.step(f"exp.{t}"))
                    w(T_, f"rows.{t}")
                    e.activation(vr[t % 2], heads(1), ACT.Copy).then_inc(*S_.step(f"vr.{t}"))
                for i in lv:
                    for t in (u, u + 1):
                        w(T_, f"y{i}.{t}")
                        e.activation(yb[t % 2], heads(t % 2), ACT.Copy).then_inc(*S_.step(f"y{i}.{t}"))
                for t in (u, u + 1):
                    w(T_, f"vn.{t}")
                    e.activation(vn, heads(3), ACT.Copy).then_inc(*S_.step(f"vn.{t}"))
                    w(T_, f"o.{t}")
                    e.activation(o_d[:, :, P * t:P * t + P], heads(5), ACT.Copy).then_inc(*S_.step(f"o.{t}"))
            w(T_, "sk")
            e.activation(egs, bank(7)[:, 0:32], ACT.Exp).then_inc(*S_.step("seg"))
            state_scalar(e, l, m, T_, S_, o_d, (5, 6, 0))
            e.drain()
            norm_scalar(e, l, m, T_, S_, "o", [o_d[:, i, :] for i in range(4)], sqr, 1.0 / P)

        def vector(self, e, l):
            def w(steps, n):
                e.wait_ge(steps.sem, steps.at(n, l))

            def v3(ap, n=5):
                return ap.rearrange("p (t h) -> p t h", t=n)

            e.wait_ge(m["A"].ot_copied, QT * (l + 1))
            e.wait_ge(m["A"].kv_saved, 16 * (l + 1))
            e.memset(cx[:, :, 0:3], 0.0).then_inc(*V_.step("pad"))
            e.tensor_tensor(v3(gx), m["small"][:, :].rearrange("p (t n) -> p t n", t=5)[:, :, 28:32],
                            vec_of("dtb").unsqueeze(1).to_broadcast([P, 5, 4]), ALU.add)
            e.drain()
            e.scalar_tensor_tensor(ga, gx, -1.0, gx, ALU.mult, ALU.max).then_inc(*V_.step("ga"))
            e.wait_ge(conv_in, 16 * (l + 1))
            e.tensor_copy(xs[:, :, :, 0:3], cin.rearrange("p (c b j) -> p c b j", c=12, b=B)).then_inc(*V_.step("cin"))
            e.drain()
            cw = vec_of("conv").rearrange("p (c j) -> p c j", j=4)
            for g in range(3):
                e.wait_ge(m["z_used"], ZT * l + 10 + 4 * g + 4)
                for j in range(4):
                    for c in range(4 * g, 4 * g + 4):
                        if j == 0:
                            e.tensor_scalar(cy[:, c, 0:T], cx[:, c, 0:T], cw[:, c, 0:1], None, ALU.mult)
                        else:
                            e.scalar_tensor_tensor(cy[:, c, 0:T], cx[:, c, j:j + T], cw[:, c, j:j + 1], cy[:, c, 0:T],
                                                   ALU.mult, ALU.add)
                    if j == 0:
                        e.tensor_tensor(xw, xs[:, 4 * g:4 * g + 4], cw[:, 4 * g:4 * g + 4, :].unsqueeze(2)
                                        .to_broadcast([P, 4, B, 4]), ALU.mult)
                    if j == 2:
                        e.tensor_reduce(cy[:, 4 * g:4 * g + 4, T:N], xw, AX_X, ALU.add)
                    e.drain() if j < 3 else e.drain().then_inc(*V_.step(f"conv{g}"))
            e.tensor_copy(cout[:, 36:324].rearrange("p (c b j) -> p c b j", c=12, b=B), xs[:, :, :, 1:4])
            e.tensor_copy(cout[:, 0:36].rearrange("p (c j) -> p c j", c=12), cx[:, :, T:T + 3])
            w(S_, "gl")
            e.tensor_scalar(gx, gx, 0.0, None, ALU.max)
            e.drain()
            e.tensor_tensor(gx, gx, gl, ALU.add)
            e.drain()
            e.scalar_tensor_tensor(v3(gd), v3(gx), -1.0, ea.unsqueeze(1).to_broadcast([P, 5, 4]),
                                   ALU.mult, ALU.mult).then_inc(*V_.step("g"))
            e.memset(S, 0.0)
            norm_vector(e, l, m, T_, S_, V_, "l", [cy[:, i, :] for i in range(8)],
                        lambda i: P ** -0.5 if i < 4 else 1.0, lambda i: None)

            def prepare(t):
                k4, z = slice(P * t, P * t + P), t % 2
                w(T_, f"gb.{t}")
                e.tensor_copy(gc, bank(7)[:, 0:4])
                e.drain()
                for h in range(4):
                    e.tensor_scalar(dec[:, h, :], heads(6)[:, h, :], gc[:, h:h + 1], 0.0, ALU.subtract, ALU.min)
                e.tensor_tensor(ktf, heads(6)[:, :, P - 1], gc, ALU.subtract)
                e.drain().then_inc(*V_.step(f"dec.{t}"))
                w(S_, f"exp.{t}")
                e.tensor_tensor(dec, dec, each_head(upper), ALU.mult)
                e.tensor_scalar(neg[z], egc, -1.0, None, ALU.mult)
                e.tensor_copy(egl[z], eg[:, :, P - 1])
                e.drain()
                w(T_, f"kk.{t}")
                e.tensor_tensor(lt[z], heads(4), dec, ALU.mult)
                e.tensor_tensor(at_[z], heads(3), dec, ALU.mult)
                e.drain()
                e.tensor_tensor(lt[z], lt[z], heads(5), ALU.mult).then_inc(*V_.step(f"lt.{t}"))
                e.tensor_tensor(qt[z], cy[:, 0:4, k4], eg, ALU.mult).then_inc(*V_.step(f"qt.{t}"))
                w(T_, f"rows.{t}")
                e.tensor_tensor(ktl[z], heads(2), cols(ktf), ALU.mult).then_inc(*V_.step(f"kt.{t}"))
                w(T_, f"y0.{t}")
                e.tensor_tensor(ta[z], each_head(ident), heads(0), ALU.subtract)
                e.tensor_tensor(tb[z], each_head(ident), ls[z][0], ALU.subtract)
                e.drain().then_inc(*V_.step(f"t0.{t}"))

            def output(t):
                z = t % 2
                w(T_, f"ks.{t}")
                w(S_, f"vr.{t}")
                for h in range(4):
                    e.scalar_tensor_tensor(rb[:, h, :], heads(4)[:, h, :], neg[z][:, h:h + 1], vr[z][:, h, :],
                                           ALU.mult, ALU.add)
                e.drain()
                e.tensor_tensor(rb, rb, cols(gate_tile(gate, t)[:, 24:28]), ALU.mult).then_inc(*V_.step(f"r.{t}"))
                w(T_, f"s.{t}")
                for h in range(4):
                    e.scalar_tensor_tensor(S[:, h, :], S[:, h, :], egl[z][:, h:h + 1], heads(4)[:, h, :],
                                           ALU.mult, ALU.add)
                e.drain().then_inc(*V_.step(f"s.{t}"))

            for u in range(0, QT, 2):
                prepare(u)
                prepare(u + 1)
                for i in lv:
                    for t in (u, u + 1):
                        w(T_, f"ty{i}.{t}")
                        if i < 6:
                            e.tensor_tensor(ta[t % 2], ta[t % 2], heads((6, 2)[t % 2]), ALU.subtract)
                        e.tensor_tensor(tb[t % 2], tb[t % 2], heads((7, 5)[t % 2]), ALU.subtract)
                        e.drain().then_inc(*V_.step(f"t{i}.{t}"))
                output(u)
                output(u + 1)
            w(S_, "seg")
            v32 = vns.rearrange("p (h b) -> p h b", h=4)
            e.tensor_tensor(vns, bank(7)[:, 64:96], egs, ALU.mult)
            e.drain()
            e.tensor_tensor(v32, cy[:, 8:12, T:N], v32, ALU.subtract)
            e.drain()
            e.tensor_tensor(vns, vns, bank(7)[:, 32:64], ALU.mult).then_inc(*V_.step("svn"))
            state_vector(e, l, m, T_, V_, ss, egs, cy[:, 4:8], tmp, (5, 6, 0))
            norm_vector(e, l, m, T_, S_, V_, "o", [o_d[:, i, :] for i in range(4)],
                        lambda i: scalar_of("dng"), lambda i: dz[:, i, :])

    p = Plan()
    p.saved, p.T_, p.S_, p.V_ = saved, T_, S_, V_
    return p


def hgrn_plan(m):
    part, sem, bank, pair, both, halves = m["part"], m["sem"], m["bank"], m["pair"], m["both"], m["halves"]
    scalar_of, ident, ones, level, o_h = m["scalar_of"], m["ident"], m["ones"], m["level"], m["o_h"]

    lf, kin, q, vT, og, gc, ex0, qk0 = (part(4 * N * i, 4 * N, 4) for i in range(8))
    ex, qk = (ex0, o_h), (qk0, part(20736, 4 * N, 4))
    am = part(0, 2048).rearrange("p (t h n) -> p t h n", t=QT, h=4)
    qt = vT
    ktr = part(16640, 2048).rearrange("p (t h n) -> p t h n", t=QT, h=4)
    vr = part(18688, 2048).rearrange("p (t h n) -> p t h n", t=QT, h=4)
    ss = part(20736, 32 * P, 32)
    S = part(24832, 512, 4)
    fs = part(25344, 32)
    egl = part(25376, 16, 4)
    lbc = part(25392, 4)
    oml = part(25396, 4)
    tmp = part(4 * N * 5, 1024, 2)
    sqr = part(4 * N * 6, 2 * N, 2)
    scan = m["const_of"]("scanmask")
    i32 = [level[:, i, :].bitcast(I32).unsqueeze(1).to_broadcast([P, 4, P]) for i in range(7)]

    st_t, st_s, st_v = state_steps("h")
    o_t, o_s, o_v = norm_steps("o", 4)
    T_ = Steps(sem("hgrn_tensor_step"), ["vrows", "ktr", "ad"] + [f"a{i}" for i in range(7)]
               + [n + str(t) for t in range(QT) for n in ("o", "s")] + st_t + o_t)
    S_ = Steps(sem("hgrn_scalar_step"), ["ln", "e0", "ke", "z", "vr", "ktr"] + [f"e{i}" for i in range(1, 8)]
               + [f"o{t}" for t in range(QT)] + st_s + o_s)
    V_ = Steps(sem("hgrn_vector_step"), ["f", "scan", "ka", "kt", "qt", "ad"]
               + [n for i in range(8) for n in ([f"qk{i}"] * (i < 7) + [f"a{i - 1}"] * (i > 0))]
               + [f"s{t}" for t in range(QT)] + st_v + o_v)
    P_ = Steps(sem("hgrn_pool_step"), [f"arg{i}" for i in range(7)])
    states_in, saved = sem("hgrn_states_loaded"), sem("hgrn_outputs_saved")

    def halves_of(ap, n):
        return ap[:, :, 0:T].rearrange("p h (b s n) -> p h b s n", s=2, n=n)

    class Plan:
        def load(self, e, l):
            e.wait_ge(T_.sem, T_.at("a6", l))
            e.sem_inc(m["turns"], 1)
            e.dma_start(ss, m["ins"]["hg_in"][l].rearrange("p (i n) -> p i n", i=32)).then_inc(states_in, 16)

        def write_back(self, e, l):
            e.wait_ge(S_.sem, S_.at("so", l))
            e.sem_inc(m["turns"], 1)
            e.dma_start(m["outs"]["hg_p"][l].rearrange("p (h n) -> p h n", h=4), S).then_inc(saved, 16)
            e.dma_start(m["outs"]["hg_s"][l].rearrange("p (i n) -> p i n", i=32), ss).then_inc(saved, 16)

        def pool(self, e, l):
            for i in range(7):
                e.wait_ge(V_.sem, V_.at(("scan", "qt")[i] if i < 2 else f"qk{i - 2}", l))
                n = 1 << i
                g5, e5 = halves_of(gc, n), halves_of(ex[1 - i % 2], n)
                for h in range(4):
                    r = g5[:, h, :, 0, n - 1:n].to_broadcast([P, T // (2 * n), n])
                    e.tensor_tensor(e5[:, h, :, 1, :], g5[:, h, :, 1, :], r, ALU.subtract)
                    d = e.tensor_tensor(e5[:, h, :, 0, :], r, g5[:, h, :, 0, :], ALU.subtract)
                d.then_inc(*P_.step(f"arg{i}"))

        def tensor(self, pe, l):
            def w(steps, n):
                pe.wait_ge(steps.sem, steps.at(n, l))

            def tile(ap, t, h):
                return ap[:, h, P * t:P * t + P]

            w(S_, "z")
            for t in range(QT):
                for h in range(4):
                    mm = pe.transpose(bank(t)[:, P * h:P * h + P], tile(vT, t, h), ident)
            mm.then_inc(*T_.step("vrows"))
            w(V_, "kt")
            for t in range(QT):
                for h in range(4):
                    mm = pe.transpose(bank(4 + t)[:, P * h:P * h + P], tile(qk[0], t, h), ident)
            mm.then_inc(*T_.step("ktr"))
            w(S_, "vr")
            for t in range(QT):
                for h in range(4):
                    mm = pe.matmul(bank(t)[:, P * h:P * h + P], tile(kin, t, h), tile(q, t, h), start=True, stop=True)
            mm.then_inc(*T_.step("ad"))
            w(S_, "ktr")
            for i in range(7):
                w(V_, f"qk{i}")
                if i:
                    w(V_, f"a{i - 2}" if i >= 2 else "ad")
                for t in range(QT):
                    for h in range(4):
                        d = tile(qk[1 - i % 2], t, h)
                        mm = pe.matmul(bank(4 * (1 - i % 2) + t)[:, P * h:P * h + P], d, d, start=True, stop=True)
                mm.then_inc(*T_.step(f"a{i}"))
            w(V_, "a6")
            for t in range(QT):
                if t:
                    w(V_, f"s{t - 1}")
                    w(S_, f"o{t - 1}")
                for h in range(4):
                    pe.matmul(bank(4)[:, P * h:P * h + P], S[:, h, :], tile(qt, t, h), start=True, stop=False)
                    mm = pe.matmul(bank(4)[:, P * h:P * h + P], vr[:, t, h, :], am[:, t, h, :], start=False, stop=True)
                mm.then_inc(*T_.step(f"o{t}"))
                for h in range(4):
                    mm = pe.matmul(bank(5)[:, P * h:P * h + P], ktr[:, t, h, :], vr[:, t, h, :], start=True, stop=True)
                mm.then_inc(*T_.step(f"s{t}"))
            w(S_, "o3")
            state_tensor(pe, l, m, T_, V_, S_, ss, lambda i: vT[:, i // 8, T + i % 8:T + i % 8 + 1], q, (1, 2, 0))
            norm_tensor(pe, l, m, T_, S_, V_, "o", 4, sqr)

        def wait_mixed(self, pe, l):
            pe.wait_ge(V_.sem, V_.at("on3", l))

        def scalar(self, e, l):
            def w(steps, n):
                e.wait_ge(steps.sem, steps.at(n, l))

            for zi in range(26, 42):
                e.wait_ge(m["z_ready"], ZT * l + zi + 1)
                c, src = (zi - 26) % 4, both(zi % 2)
                if zi == 26:
                    e.wait_ge(D_saved, 64 * (l + 1))
                    w(m["D"].V_, "on3")
                if zi < 30:
                    e.activation(halves(lf[:, c, :]), src, ACT.Sigmoid)
                    e.activation(halves(kin[:, c, :]), src, ACT.Sigmoid, scale=-1.0).then_inc(m["z_used"], 1)
                else:
                    dst, f = ((vT, ACT.Copy), (q, ACT.Silu), (og, ACT.Sigmoid))[(zi - 30) // 4]
                    e.activation(halves(dst[:, c, :]), src, f).then_inc(m["z_used"], 1)
                m["split_hi"](e, l * TILES + m["z_tile"](zi), m["z_tile"](zi))
                if zi == 33:
                    w(V_, "f")
                    e.activation(lf, lf, ACT.Ln).then_inc(*S_.step("ln"))
                elif zi == 37:
                    w(V_, "scan")
                    e.activation(ex[0][:, :, 0:T], gc[:, :, 0:T], ACT.Exp).then_inc(*S_.step("e0"))
                    w(V_, "ka")
                    e.activation(qk[0][:, :, 0:T], qk[0][:, :, 0:T], ACT.Exp).then_inc(*S_.step("ke"))
            e.drain().then_inc(*S_.step("z"))
            w(T_, "vrows")
            for t in range(QT):
                a = e.activation(vr[:, t, :, :], bank(t).rearrange("p (h n) -> p h n", h=4), ACT.Copy)
            a.then_inc(*S_.step("vr"))
            w(T_, "ktr")
            for t in range(QT):
                a = e.activation(ktr[:, t, :, :], bank(4 + t).rearrange("p (h n) -> p h n", h=4), ACT.Copy)
            a.then_inc(*S_.step("ktr"))
            for i in range(7):
                w(P_, f"arg{i}")
                ei = ex[1 - i % 2][:, :, 0:T]
                e.activation(ei, ei, ACT.Exp).then_inc(*S_.step(f"e{i + 1}"))
            for t in range(QT):
                w(T_, f"o{t}")
                e.activation(o_h[:, :, P * t:P * t + P], bank(4).rearrange("p (h n) -> p h n", h=4),
                             ACT.Copy).then_inc(*S_.step(f"o{t}"))
            state_scalar(e, l, m, T_, S_, o_h, (1, 2, 0))
            e.drain()
            norm_scalar(e, l, m, T_, S_, "o", [o_h[:, i, :] for i in range(4)], sqr, 1.0 / P)

        def vector(self, e, l):
            def w(steps, n):
                e.wait_ge(steps.sem, steps.at(n, l))

            e.wait_ge(D_saved, 64 * (l + 1))
            e.tensor_copy(lbc, m["lb"][:, bass.DynSlice(4 * l, 4)])
            e.drain()
            e.tensor_scalar(oml, lbc, -1.0, 1.0, ALU.mult, ALU.add)
            e.drain()
            e.wait_ge(m["z_used"], ZT * l + 30)
            for c in range(4):
                e.tensor_scalar(lf[:, c, :], lf[:, c, :], oml[:, c:c + 1], lbc[:, c:c + 1], ALU.mult, ALU.add)
                e.tensor_scalar(kin[:, c, :], kin[:, c, :], oml[:, c:c + 1], None, ALU.mult)
            e.drain()
            e.tensor_scalar(lf, lf, 1e-18, None, ALU.max)
            e.drain()
            e.tensor_copy(fs.rearrange("p (h b) -> p h b", h=4), lf[:, :, T:N]).then_inc(*V_.step("f"))
            w(S_, "ln")
            for c in range(4):
                e.tensor_tensor_scan(gc[:, c, 0:T], scan, lf[:, c, 0:T], 0.0, ALU.mult, ALU.add)
            e.memset(S, 0.0)
            e.drain().then_inc(*V_.step("scan"))
            ends = gc[:, :, 0:T].rearrange("p h (t n) -> p h t n", t=QT)
            e.tensor_tensor(qk[0][:, :, 0:T].rearrange("p h (t n) -> p h t n", t=QT),
                            ends[:, :, :, P - 1:P].to_broadcast([P, 4, QT, P]), ends, ALU.subtract).then_inc(*V_.step("ka"))
            e.wait_ge(m["z_used"], ZT * l + 38)
            e.tensor_scalar(q, q, P ** -0.5, None, ALU.mult)
            w(S_, "e0")
            e.tensor_copy(egl, ex[0][:, :, P - 1:T:P])
            w(S_, "ke")
            e.tensor_tensor(qk[0][:, :, 0:T], qk[0][:, :, 0:T], kin[:, :, 0:T], ALU.mult).then_inc(*V_.step("kt"))
            e.drain()
            w(S_, "vr")
            e.tensor_tensor(qt[:, :, 0:T], q[:, :, 0:T], ex[0][:, :, 0:T], ALU.mult).then_inc(*V_.step("qt"))
            w(T_, "ad")
            for t in range(QT):
                d = e.tensor_tensor(am[:, t, :, :], bank(t).rearrange("p (h n) -> p h n", h=4),
                                    ident.unsqueeze(1).to_broadcast([P, 4, P]), ALU.mult)
            d.then_inc(*V_.step("ad"))
            for i in range(8):
                if i < 7:
                    n = 1 << i
                    w(S_, f"e{i + 1}")
                    if i:
                        w(T_, f"a{i - 2}" if i > 1 else "ktr")
                    e5, k5, q5, o5 = (halves_of(a, n) for a in (ex[1 - i % 2], kin, q, qk[1 - i % 2]))
                    e.tensor_tensor(o5[:, :, :, 1, :], q5[:, :, :, 1, :], e5[:, :, :, 1, :], ALU.mult)
                    e.tensor_tensor(o5[:, :, :, 0, :], k5[:, :, :, 0, :], e5[:, :, :, 0, :], ALU.mult)
                    e.drain().then_inc(*V_.step(f"qk{i}"))
                else:
                    e.drain()
                if i:
                    w(T_, f"a{i - 1}")
                    e.sem_inc(m["turns"], 1)
                    for t in range(QT):
                        d = e.copy_predicated(am[:, t, :, :], i32[i - 1],
                                              bank(4 * (i % 2) + t).rearrange("p (h n) -> p h n", h=4))
                    d.then_inc(*V_.step(f"a{i - 1}"))
            for t in range(QT):
                w(T_, f"s{t}")
                for h in range(4):
                    e.scalar_tensor_tensor(S[:, h, :], S[:, h, :], egl[:, h, t:t + 1], bank(5)[:, P * h:P * h + P],
                                           ALU.mult, ALU.add)
                e.drain().then_inc(*V_.step(f"s{t}"))
            e.wait_ge(states_in, 16 * (l + 1))
            state_vector(e, l, m, T_, V_, ss, fs, kin, tmp, (1, 2, 0))
            norm_vector(e, l, m, T_, S_, V_, "o", [o_h[:, i, :] for i in range(4)],
                        lambda i: scalar_of("hgg"), lambda i: og[:, i, :])

    D_saved = m["D"].saved
    p = Plan()
    p.saved = saved
    return p


def hybrid_step_kernel(nc, ins, outs):
    ctx = ExitStack()
    with ctx:
        def sb(name, width, parts=P, dtype=F32):
            return ctx.enter_context(nc.sbuf_tensor(name, [parts, width], dtype))

        def sem(name):
            return ctx.enter_context(nc.semaphore(name))

        def blocks(ap, n):
            return ap.rearrange("p (k n) -> p k n", k=n)

        def halves(ap):
            return ap.rearrange("p (a n) -> p a n", a=2)

        x = blocks(sb("x", KD * N)[:, :], KD)
        h_hi, h_lo = (blocks(sb(f"h_{n}", KD * N, dtype=F16)[:, :], KD) for n in ("hi", "lo"))
        raw = [blocks(sb(f"raw{i}", KD * P)[:, :], KD) for i in range(2)]
        w_hi = [blocks(sb(f"w_hi{i}", KD * P, dtype=F16)[:, :], KD) for i in range(4)]
        w_lo = [blocks(sb(f"w_lo{i}", KD * P, dtype=F16)[:, :], KD) for i in range(4)]
        const = sb("const", NCONST)
        vecs = sb("vecs", L * NVEC)
        vec = sb("vec", NVEC)
        lbl = sb("lbl", 8)
        lbw = sb("lbw", 24)
        lb = sb("lb", 8)
        eps = sb("eps", 1)
        rstd = sb("rstd", NBLK)
        mixed = sb("mixed", 12 * N)
        o_a, o_d, o_h = (blocks(mixed[:, i * 4 * N:(i + 1) * 4 * N], 4) for i in range(3))
        small = sb("small", 5 * 32)
        gate = sb("gate", 5 * 28)
        pages = ctx.enter_context(nc.sbuf_tensor("page_ids", [1, B * PAGES], I32))
        ARENA = 26340
        arena = sb("arena", ARENA)

        def part(at, width, n=None, parts=P):
            assert at + width <= ARENA
            ap = arena[0:parts, at:at + width]
            return ap if n is None else blocks(ap, n)

        def const_of(name, parts=P):
            o, w = CONST[name]
            return const[0:parts, o:o + w]

        ident, ones, bones, upper = (const_of(n) for n in ("ident", "ones", "bones", "upper"))
        level = blocks(const_of("level"), 7)
        dist = const_of("dist")

        def vec_of(name):
            o, w = VEC[name]
            return vec[:, o:o + w]

        def scalar_of(name, i=0, parts=P):
            o, _ = VEC[name]
            return vec[0:parts, o + i:o + i + 1]

        pair = [ctx.enter_context(nc.psum_tensor(f"pair{i}", [P, 2, 512], F32)) for i in range(4)]

        def bank(i):
            return pair[i // 2][:, i % 2, :]

        def both(i):
            return pair[i][:, :, 0:HALF]

        def two(at, n):
            w = part(at, n * N).bitcast(F16)
            return blocks(w[:, 0:n * N], n), blocks(w[:, n * N:2 * n * N], n)

        act_hi, act_lo = two(0, FC)
        sq_sum = part(FC * N, N)
        sq = part((FC + 1) * N, 2 * N, 2)
        sg = part(FC * N + KD * N, 4 * HALF, 4)
        merged = part(0, KD * N, KD)
        mgate = part(KD * N, 2 * N, 2)
        mprod = part((KD + 2) * N, 2 * N, 2)
        merged_hi, merged_lo = two((KD + 4) * N, KD)
        o_hi, o_lo = two((2 * KD + 4) * N, 12)
        hf = part(FC * N + KD * N, 2 * N, 2)

        loaded = sem("constants_loaded")
        const_in = sem("mixer_constants_loaded")
        x_loaded = sem("x_loaded")
        pages_in = sem("page_ids_loaded")
        setup = sem("setup_done")
        landed = [sem(f"raw{i}_landed") for i in range(2)]
        w_hi_done = sem("weight_hi_done")
        w_split = sem("weight_split")
        w_used = sem("weight_used")
        hf_done = sem("h_float_done")
        h_hi_done = sem("h_hi_done")
        act_hi_done = sem("act_hi_done")
        act_done = sem("act_done")
        o_hi_done = sem("o_hi_done")
        o_done = sem("o_split")
        merged_hi_done = sem("merged_hi_done")
        merged_done = sem("merged_split")
        gates_ready = sem("merge_gates_ready")
        x_done = sem("x_block_done")
        sq_done = sem("x_block_squared")
        sum_done = sem("square_added")
        ss_done = sem("norm_sum_done")
        std_done = sem("norm_std_done")
        inv_done = sem("norm_inverse_done")
        inv_spread = sem("norm_inverse_spread")
        h_done = sem("h_block_done")
        gu_ready = sem("gate_up_ready")
        silu_done = sem("silu_done")
        gu_free = sem("gate_up_used")
        proj_ready = sem("projection_ready")
        z_ready = sem("z_block_ready")
        z_used = sem("z_block_used")
        small_ready = sem("small_ready")
        mg_ready = sem("merge_product_ready")
        mg_gate = sem("merge_gate_done")
        mg_used = sem("merge_product_used")
        y_stored = sem("y_stored")
        turns = sem("waits_passed")
        lbx = sem("lower_bound_step")


        def fetch(sp, n, src, s, k=KD, w=P):
            sp.wait_ge(w_split, n + 1)
            sp.dma_start(raw[s % 2][:, 0:k, 0:w], src.rearrange("a p (k n) -> p (a k) n", k=k)).then_inc(landed[s % 2], 16)

        def split_hi(e, n, s):
            e.wait_ge(landed[s % 2], 8 * (n + 4 - s % 2) + 16)
            e.activation(w_hi[s % 4], raw[s % 2], ACT.Copy).then_inc(w_hi_done, 1)

        def split_lo(e, n, s):
            e.wait_ge(w_hi_done, n + 1)
            e.tensor_tensor(w_lo[s % 4], raw[s % 2], w_hi[s % 4], ALU.subtract).then_inc(w_split, 1)

        def products(pe, targets, ready):
            for k in range(KD):
                pe.wait_ge(h_done, ready + k + 1)
                last = []
                for out, s, a in targets:
                    for p, (w, xx) in enumerate(((w_hi, h_hi), (w_hi, h_lo), (w_lo, h_hi))):
                        mm = pe.matmul(out, w[s % 4][:, k, :], xx[:, k, a * HALF:(a + 1) * HALF],
                                       start=(k == 0 and p == 0), stop=(k == KD - 1 and p == 2))
                    last.append(mm)
            return last

        def product(pe, out, s, x_hi, x_lo, ks, first, last):
            for i, (kw, kx) in enumerate(ks):
                for p, (w, xx) in enumerate(((w_hi, x_hi), (w_hi, x_lo), (w_lo, x_hi))):
                    mm = pe.matmul(out, w[s % 4][:, kw, :], xx(kx), start=(first and i == 0 and p == 0),
                                   stop=(last and i == len(ks) - 1 and p == 2))
            return mm

        def columns(ap, a):
            return lambda k: ap[:, k, a * HALF:(a + 1) * HALF]

        AT_FFN = (0, 156)
        AT_Z, AT_MERGE, AT_OUT = 68, 112, 148

        def z_tile(zi):
            return AT_Z + (zi if zi < 10 else zi + 2)

        env = dict(const_in=const_in, split_hi=split_hi, split_lo=split_lo, z_tile=z_tile,
                   bank=bank, bones=bones, both=both, const_of=const_of, dist=dist, eps=eps, gate=gate,
                   h_done=h_done, halves=halves, ident=ident, ins=ins, lb=lb, level=level, mixed=mixed,
                   o_a=o_a, o_d=o_d, o_h=o_h, ones=ones, outs=outs, pages=pages, pair=pair, part=part,
                   rstd=rstd, scalar_of=scalar_of, sem=sem, small=small, small_ready=small_ready, turns=turns,
                   upper=upper, vec=vec, vec_of=vec_of, x_done=x_done, z_ready=z_ready, z_used=z_used)
        A = env["A"] = attention_plan(env)
        D = env["D"] = delta_plan(env)
        G = hgrn_plan(env)
        block = ctx.enter_context(nc.Block())

        @block.sync
        def _(sp):
            sp.dma_start(pages[:, :], ins["pages"]).then_inc(pages_in, 16)
            sp.dma_start(x, ins["x"]).then_inc(x_loaded, 16)
            sp.dma_start(const[:, 0:2 * P], ins["const"][:, 0:2 * P]).then_inc(loaded, 16)
            sp.dma_start(vecs[:, :].rearrange("p (l n) -> p l n", l=L),
                         ins["vec"].rearrange("l p n -> p l n")).then_inc(loaded, 16)
            sp.dma_start(lbl[:, :], ins["lb"]).then_inc(loaded, 16)
            sp.sem_inc(w_split, 2)
            sp.wait_ge(pages_in, 16)
            sp.sem_inc(turns, 1)

            with sp.Fori(0, L) as l:
                def ffn(f):
                    n = l * TILES + AT_FFN[f]
                    def up(r, pages):
                        for s in range(4):
                            fetch(sp, n + 4 * r + s, ins["w_up"][2 * l + f, bass.DynSlice(4 * r + s, 1)], s)
                            if pages and s % 2:
                                A.load_page(sp, l, 2 * r + s // 2)

                    if f == 0:
                        with sp.Fori(0, B * PAGES // 2) as r:
                            up(r, True)
                        A.load(sp, l)
                        with sp.Fori(B * PAGES // 2, FC // 2) as r:
                            up(r, False)
                    else:
                        with sp.Fori(0, FC // 2) as r:
                            up(r, False)

                    with sp.Fori(0, 2) as r:
                        for s in range(12):
                            j = s % 3
                            o = sum(DOWN[:j]) * P
                            src = ins["w_dn"][2 * l + f, bass.DynSlice(4 * r + s // 3, 1)]
                            fetch(sp, n + 44 + 12 * r + s, src[:, :, o:o + DOWN[j] * P], s, DOWN[j])

                ffn(0)
                for s in range(44):
                    n = l * TILES + AT_Z + s
                    if s in (10, 11):
                        fetch(sp, n, ins["w_sm"][bass.DynSlice(l, 1)], s, KD, 32)
                    else:
                        zi = s if s < 10 else s - 2
                        fetch(sp, n, ins["w_z"][l, zi:zi + 1], s)
                    if s == 5:
                        A.load_cmp(sp, l)
                    if 5 <= s < 5 + B:
                        A.load_cmp_pages(sp, l, PAGES * (s - 5))
                    if s == 16:
                        A.write_back(sp, l)
                    if s == 17:
                        D.load(sp, l)
                    if s == 33:
                        D.write_back(sp, l)
                def branch(i, first):
                    for s in range(12):
                        if first and s == 6:
                            G.load(sp, l)
                            G.write_back(sp, l)
                        d, j = s // 3, s % 3
                        src = (ins["w_wb"][l, bass.DynSlice(4 * i + d, 1)] if j == 1 else
                               ins["w_mg"][l, bass.DynSlice(8 * i + 2 * d + j // 2, 1)])
                        fetch(sp, l * TILES + AT_MERGE + 12 * i + s, src, s)

                branch(0, True)
                with sp.Fori(1, 3) as i:
                    branch(i, False)
                with sp.Fori(0, 2) as r:
                    for s in range(4):
                        fetch(sp, l * TILES + AT_OUT + 4 * r + s, ins["w_out"][l, bass.DynSlice(4 * r + s, 1)], s)
                sp.wait_ge(G.saved, 32 * (l + 1))
                sp.sem_inc(turns, 1)
                ffn(1)
            for s in range(4):
                fetch(sp, L * TILES + s, ins["w_up"][0, s:s + 1], s)
            for k in range(0, KD, 2):
                sp.wait_ge(x_done, 8 * (3 * L) + k + 2)
                sp.dma_start(outs["y"][:, k * N:(k + 2) * N].rearrange("p (k n) -> p k n", k=2),
                             x[:, k:k + 2, :]).then_inc(y_stored, 16)
            sp.wait_ge(y_stored, 16 * KD // 2)
            for s in range(2):
                sp.wait_ge(landed[s], 8 * (L * TILES + 4))

        @block.tensor
        def _(pe):
            pe.wait_ge(loaded, 48)

            def norm(l, s):
                pe.wait_ge(sum_done, 8 * (3 * l + s) + KD)
                for j, c in enumerate(SUMS):
                    mm = pe.matmul(bank(7)[:, j:j + 1], sq_sum[:, c:c + P], ones[:, 0:1], start=True, stop=True)
                mm.then_inc(ss_done, 1)
                pe.wait_ge(inv_done, 3 * l + s + 1)
                spread(pe, pair[3], ident, rstd[:, 0:5]).then_inc(inv_spread, 1)

            def ffn(l, f):
                n = l * TILES + AT_FFN[f]
                with pe.Fori(0, FC // 2) as r:
                    for j in range(2):
                        pe.wait_ge(w_split, n + 4 * r + 2 * j + 1 + 3)
                        t = 44 * (2 * l + f) + 4 * r + 2 * j
                        if j == 0:
                            pe.wait_ge(gu_free, t + 2)
                            done = products(pe, [(pair[a][:, gu, 0:HALF], gu, a) for a in range(2) for gu in range(2)],
                                            8 * (3 * l + 2 * f))
                            for a in range(2):
                                done[2 * a + 1].then_inc(gu_ready, 1)
                            continue
                        for a in range(2):
                            q = 2 * j + a
                            pe.wait_ge(gu_free, t + a + 1)
                            for gu in range(2):
                                mm = product(pe, pair[q][:, gu, 0:HALF], 2 * j + gu, columns(h_hi, a), columns(h_lo, a),
                                             [(k, k) for k in range(KD)], True, True)
                            mm.then_inc(gu_ready, 1)
                with pe.Fori(0, 2) as r:
                    pe.wait_ge(act_done, 44 * (2 * l + f + 1) + 4)
                    for b in range(4):
                        pe.wait_ge(x_done, 8 * (3 * l + 2 * f) + 4 * r + b + 7)
                        for a in range(2):
                            for j in range(3):
                                if a == 0:
                                    pe.wait_ge(w_split, n + 44 + 12 * r + 3 * b + j + 3)
                                mm = product(pe, pair[b % 2][:, a, 0:HALF], 3 * b + j, columns(act_hi, a), columns(act_lo, a),
                                             [(k, 8 * j + k) for k in range(DOWN[j])], j == 0, j == 2)
                                if a == 1 and j < 2:
                                    mm.then_inc(w_used, 1)
                        mm.then_inc(proj_ready, 1)

            def z_block(l, zi):
                pe.wait_ge(w_split, l * TILES + z_tile(zi) + 3)
                if zi >= 2:
                    pe.wait_ge(z_used, ZT * l + zi - 1)
                done = products(pe, [(pair[zi % 2][:, a, 0:HALF], z_tile(zi), a) for a in range(2)], 8 * (3 * l + 1))
                done[1].then_inc(z_ready, 1)

            def z_small(l):
                pe.wait_ge(w_split, l * TILES + AT_Z + 11 + 3)
                pe.wait_ge(z_used, ZT * l + 9)
                s = (AT_Z + 10) % 4
                for t in range(5):
                    w = P if t < 4 else B
                    for k in range(KD):
                        for p, (hh, ww) in enumerate(((h_hi, w_hi), (h_hi, w_lo), (h_lo, w_hi))):
                            mm = pe.matmul(bank(0)[0:w, 32 * t:32 * t + 32], hh[:, k, P * t:P * t + w],
                                           ww[s][:, k, 0:32], start=(k == 0 and p == 0), stop=(k == KD - 1 and p == 2))
                mm.then_inc(small_ready, 1)

            def merge(l):
                for i in range(3):
                    for b in range(KD):
                        d, odd = b // 2, b % 2
                        at = AT_MERGE + 12 * i + 3 * d
                        if i == 0 and b == 0:
                            G.wait_mixed(pe, l)
                        pe.wait_ge(w_split, l * TILES + at + 2 * odd + 3)
                        pe.wait_ge(mg_used, 24 * l + 8 * i + b + 1)
                        for a in range(2):
                            mm = product(pe, pair[2 * odd][:, a, 0:HALF], at + 2 * odd, columns(h_hi, a), columns(h_lo, a),
                                         [(k, k) for k in range(KD)], True, True)
                        mm.then_inc(gates_ready, 1)
                        if b == 0:
                            pe.wait_ge(o_done, 12 * l + 4 * i + 4)
                        pe.wait_ge(w_split, l * TILES + at + 1 + 3)
                        for a in range(2):
                            mm = product(pe, pair[2 * odd + 1][:, a, 0:HALF], at + 1, columns(o_hi, a), columns(o_lo, a),
                                         [(4 * odd + k, 4 * i + k) for k in range(4)], True, True)
                        mm.then_inc(mg_ready, 1)
                for b in range(KD):
                    pe.wait_ge(w_split, l * TILES + AT_OUT + b + 3)
                    pe.wait_ge(x_done, 8 * (3 * l + 1) + b + 7)
                    for a in range(2):
                        for k in range(KD):
                            if b == 0 and a == 0:
                                pe.wait_ge(merged_done, 8 * l + k + 1)
                            mm = product(pe, pair[b % 2][:, a, 0:HALF], AT_OUT + b, columns(merged_hi, a),
                                         columns(merged_lo, a), [(k, k)], k == 0, k == KD - 1)
                    mm.then_inc(proj_ready, 1)

            with pe.Fori(0, L) as l:
                norm(l, 0)
                ffn(l, 0)
                norm(l, 1)
                for zi in range(10):
                    z_block(l, zi)
                z_small(l)
                A.tensor(pe, l)
                for zi in range(10, 26):
                    z_block(l, zi)
                D.tensor(pe, l)
                for zi in range(26, 42):
                    z_block(l, zi)
                G.tensor(pe, l)
                merge(l)
                norm(l, 2)
                ffn(l, 1)

        @block.scalar
        def _(act_e):
            act_e.wait_ge(setup, 1)
            act_e.wait_ge(lbx, 1)
            act_e.activation(lbw[:, 4:12], lbw[:, 4:12], ACT.Exp).then_inc(lbx, 1)
            for s in range(2):
                split_hi(act_e, s - 4, s)
            for k in range(KD):
                act_e.wait_ge(x_done, k + 1)
                if k >= 2:
                    act_e.wait_ge(sum_done, k - 1)
                act_e.activation(sq[:, k % 2, :], x[:, k, :], ACT.Square).then_inc(sq_done, 1)

            for s in range(2, 4):
                split_hi(act_e, s - 4, s)
            act_e.dma_start(const[:, 2 * P:NCONST], ins["const"][:, 2 * P:NCONST]).then_inc(const_in, 16)

            def norm(l, s):
                act_e.wait_ge(ss_done, 3 * l + s + 1)
                act_e.activation(rstd[:, 0:5], bank(7)[:, 0:5], ACT.Sqrt, bias=eps[:, :],
                                 scale=1.0 / (KD * P)).then_inc(std_done, 1)
                for k in range(KD):
                    act_e.wait_ge(hf_done, 8 * (3 * l + s) + k + 1)
                    act_e.activation(h_hi[:, k, :], hf[:, k % 2, :], ACT.Copy).then_inc(h_hi_done, 1)

            def square(l, s, k, j):
                act_e.wait_ge(x_done, 8 * (3 * l + s) + k + 9)
                act_e.wait_ge(sum_done, 8 * (3 * l + s) + k + 7)
                act_e.activation(sq[:, j:j + 1, :], x[:, bass.DynSlice(k, 1), :],
                                 ACT.Square).then_inc(sq_done, 1)

            def ffn(l, f):
                n = l * TILES + AT_FFN[f]
                with act_e.Fori(0, FC // 2) as r:
                    for q in range(4):
                        t = 44 * (2 * l + f) + 4 * r + q
                        act_e.wait_ge(gu_ready, t + 1)
                        act_e.wait_ge(act_done, t + 1)
                        act_e.activation(sg[:, q, :], pair[q][:, 0, 0:HALF], ACT.Silu).then_inc(silu_done, 1)
                        if q % 2:
                            split_hi(act_e, n + 4 * r + q - 1, q - 1)
                            split_hi(act_e, n + 4 * r + q, q)
                        act_e.wait_ge(gu_free, t + 5)
                        act_e.activation(act_hi[:, bass.DynSlice(2 * r + q // 2, 1), (q % 2) * HALF:(q % 2 + 1) * HALF],
                                         sg[:, q:q + 1, :], ACT.Copy).then_inc(act_hi_done, 1)
                with act_e.Fori(0, 2) as r:
                    for b in range(4):
                        for j in range(2):
                            act_e.wait_ge(w_used, 16 * (2 * l + f) + 8 * r + 2 * b + j + 1)
                            split_hi(act_e, n + 44 + 12 * r + 3 * b + j, 3 * b + j)
                        act_e.wait_ge(proj_ready, 8 * (3 * l + 2 * f) + 4 * r + b + 1)
                        split_hi(act_e, n + 44 + 12 * r + 3 * b + 2, 3 * b + 2)
                        square(l, 2 * f, 4 * r + b, b % 2)

            def merge(l):
                for c in range(12):
                    if c == 0:
                        G.wait_mixed(act_e, l)
                    act_e.activation(o_hi[:, c, :], mixed[:, c * N:(c + 1) * N], ACT.Copy).then_inc(o_hi_done, 1)
                with act_e.Fori(0, 3) as i:
                    for b in range(KD):
                        d, odd = b // 2, b % 2
                        n = l * TILES + AT_MERGE + 12 * i + 3 * d
                        act_e.wait_ge(gates_ready, 24 * l + 8 * i + b + 1)
                        act_e.wait_ge(mg_used, 24 * l + 8 * i + b + 1)
                        act_e.activation(halves(mgate[:, odd, :]), both(2 * odd), ACT.Sigmoid).then_inc(mg_gate, 1)
                        if odd:
                            act_e.wait_ge(mg_ready, 24 * l + 8 * i + b + 1)
                            split_hi(act_e, n + 1, 3 * d + 1)
                            split_hi(act_e, n + 2, 3 * d + 2)
                        else:
                            split_hi(act_e, n, 3 * d)
                for b in range(KD):
                    act_e.wait_ge(mg_used, 24 * l + 16 + b + 3)
                    act_e.activation(merged_hi[:, b, :], merged[:, b, :], ACT.Copy).then_inc(merged_hi_done, 1)
                for b in range(KD):
                    act_e.wait_ge(proj_ready, 8 * (3 * l + 1) + b + 1)
                    split_hi(act_e, l * TILES + AT_OUT + b, b)
                    square(l, 1, b, b % 2)

            with act_e.Fori(0, L) as l:
                norm(l, 0)
                ffn(l, 0)
                norm(l, 1)
                A.scalar(act_e, l)
                D.scalar(act_e, l)
                G.scalar(act_e, l)
                merge(l)
                norm(l, 2)
                ffn(l, 1)

        @block.vector
        def _(dve):
            dve.memset(eps[:, :], EPS)
            dve.memset(small[:, :], 0.0).then_inc(setup, 1)
            dve.sem_inc(gu_free, 4)
            dve.sem_inc(act_done, 4)
            dve.sem_inc(mg_used, 2)
            dve.wait_ge(loaded, 48)
            a0, a1 = lbl[:, 0:4], lbl[:, 4:8]
            mx, e0, e1, r0 = (lbw[:, 4 * i:4 * i + 4] for i in range(4))
            dve.tensor_tensor(mx, a0, a1, ALU.max)
            dve.drain()
            dve.tensor_tensor(e0, a0, mx, ALU.subtract)
            dve.tensor_tensor(e1, a1, mx, ALU.subtract)
            dve.drain().then_inc(lbx, 1)
            dve.wait_ge(lbx, 2)
            dve.tensor_tensor(r0, e0, e1, ALU.add)
            dve.drain()
            dve.reciprocal(mx, r0)
            dve.drain()
            dve.tensor_tensor(e0, e0, mx, ALU.mult)
            dve.tensor_tensor(e1, e1, mx, ALU.mult)
            dve.drain()
            dve.tensor_tensor(lb[:, 0:4], e0, e0, ALU.subtract)
            dve.tensor_tensor(r0, e0, e1, ALU.add)
            dve.drain()
            dve.tensor_tensor(lb[:, 4:8], r0, e0, ALU.subtract)
            dve.wait_ge(x_loaded, 16)
            dve.sem_inc(x_done, 8)

            def add_square(count, j):
                dve.wait_ge(sq_done, count)
                dve.tensor_tensor(sq_sum, sq_sum, sq[:, j, :], ALU.add)
                dve.drain().then_inc(sum_done, 1)

            dve.memset(sq_sum, 0.0)
            dve.drain()
            for k in range(KD):
                add_square(k + 1, k % 2)

            def norm(l, s, gain):
                dve.wait_ge(std_done, 3 * l + s + 1)
                dve.reciprocal(rstd[:, 0:5], rstd[:, 0:5]).then_inc(inv_done, 1)
                dve.wait_ge(inv_spread, 3 * l + s + 1)
                for k in range(KD + 1):
                    if 2 <= k < KD:
                        dve.wait_ge(h_done, 8 * (3 * l + s) + k - 1)
                    if k < KD:
                        dve.scalar_tensor_tensor(halves(hf[:, k % 2, :]), halves(x[:, k, :]), scalar_of(gain, k),
                                                 both(3), ALU.mult, ALU.mult).then_inc(hf_done, 1)
                    if k:
                        dve.wait_ge(h_hi_done, 8 * (3 * l + s) + k)
                        dve.tensor_tensor(h_lo[:, k - 1, :], hf[:, (k - 1) % 2, :], h_hi[:, k - 1, :],
                                          ALU.subtract).then_inc(h_done, 1)

            def ffn(l, f):
                with dve.Fori(0, FC // 2) as r:
                    for q in range(4):
                        dve.wait_ge(silu_done, 44 * (2 * l + f) + 4 * r + q + 1)
                        dve.tensor_tensor(sg[:, q, :], sg[:, q, :], pair[q][:, 1, 0:HALF], ALU.mult).then_inc(gu_free, 1)
                        dve.wait_ge(act_hi_done, 44 * (2 * l + f) + 4 * r + q + 1)
                        c, cols = bass.DynSlice(2 * r + q // 2, 1), slice((q % 2) * HALF, (q % 2 + 1) * HALF)
                        dve.tensor_tensor(act_lo[:, c, cols], sg[:, q:q + 1, :], act_hi[:, c, cols],
                                          ALU.subtract).then_inc(act_done, 1)
                residual(l, 2 * f, 0.5)

            def residual(l, s, scale):
                dve.wait_ge(proj_ready, 8 * (3 * l + s) + 1)
                dve.memset(sq_sum, 0.0)
                dve.drain()
                with dve.Fori(0, KD // 2) as r:
                    for j in range(2):
                        dve.wait_ge(proj_ready, 8 * (3 * l + s) + 2 * r + j + 1)
                        xk = x[:, bass.DynSlice(2 * r + j, 1), :].rearrange("p k (a n) -> p (k a) n", a=2)
                        dve.scalar_tensor_tensor(xk, both(j), scale, xk, ALU.mult, ALU.add).then_inc(x_done, 1)
                        add_square(8 * (3 * l + s + 1) + 2 * r + j + 1, j)

            def merge(l):
                for c in range(12):
                    dve.wait_ge(o_hi_done, 12 * l + c + 1)
                    dve.tensor_tensor(o_lo[:, c, :], mixed[:, c * N:(c + 1) * N], o_hi[:, c, :],
                                      ALU.subtract).then_inc(o_done, 1)
                for i in range(3):
                    with dve.Fori(0, KD // 2) as r:
                        for j in range(2):
                            dve.wait_ge(mg_gate, 24 * l + 8 * i + 2 * r + j + 1)
                            dve.wait_ge(mg_ready, 24 * l + 8 * i + 2 * r + j + 1)
                            out = merged[:, bass.DynSlice(2 * r + j, 1), :].rearrange("p k (a n) -> p (k a) n", a=2)
                            g = halves(mgate[:, j, :])
                            if i == 0:
                                dve.tensor_tensor(out, g, both(2 * j + 1), ALU.mult).then_inc(mg_used, 1)
                            else:
                                t = halves(mprod[:, j, :])
                                dve.tensor_tensor(t, g, both(2 * j + 1), ALU.mult)
                                dve.drain()
                                dve.tensor_tensor(out, out, t, ALU.add).then_inc(mg_used, 1)

            with dve.Fori(0, L) as l:
                dve.tensor_copy(vec[:, :], vecs[:, bass.DynSlice(l * NVEC, NVEC)])
                dve.drain()
                norm(l, 0, "ffn1")
                ffn(l, 0)
                norm(l, 1, "mix")
                A.vector(dve, l)
                D.vector(dve, l)
                G.vector(dve, l)
                merge(l)
                for b in range(KD):
                    dve.wait_ge(merged_hi_done, 8 * l + b + 1)
                    dve.tensor_tensor(merged_lo[:, b, :], merged[:, b, :], merged_hi[:, b, :],
                                      ALU.subtract).then_inc(merged_done, 1)
                residual(l, 1, 1.0)
                norm(l, 2, "ffn2")
                ffn(l, 1)

        @block.gpsimd
        def _(pool):
            for s in range(4):
                split_lo(pool, s, s)

            def lo_tiles(n, count):
                with pool.Fori(0, count // 4) as r:
                    for s in range(4):
                        split_lo(pool, n + 4 * r + s, s)

            with pool.Fori(0, L) as l:
                lo_tiles(l * TILES + 4, AT_Z + 28)
                D.pool(pool, l)
                lo_tiles(l * TILES + 4 + AT_Z + 28, 16)
                G.pool(pool, l)
                lo_tiles(l * TILES + 4 + AT_MERGE, TILES - AT_MERGE)


def _constants():
    import numpy as np
    big = np.float32(-1e30)
    c = np.zeros((P, NCONST), np.float32)

    def put(name, a):
        o, w = CONST[name]
        a = np.asarray(a, np.float32).reshape(a.shape[0], -1)
        assert a.shape[1] == w, name
        c[:a.shape[0], o:o + w] = a

    p = np.arange(P)
    put("ident", np.eye(P))
    put("ones", np.ones((P, P)))
    put("bones", (p[:, None] // HD == p[None] // HD))
    put("upper", (p[:, None] <= p[None]))
    lev = []
    for s in (1, 2, 4, 8, 16, 32, 64):
        j, i = p[:, None], p[None]
        lev.append((j // (2 * s) == i // (2 * s)) & (j % (2 * s) < s) & (i % (2 * s) >= s))
    put("level", np.stack(lev, 1))
    d = np.arange(T)[None] - (T - P) - p[:, None]
    put("dist", np.where(d <= 0, d, big))
    t, pos, n = np.arange(QT), np.arange(8), np.arange(NPB)
    d = 16 * n + 31 - P * t[None, :, None, None] - p[:, None, None, None] + 0 * pos[None, None, :, None]
    sl = np.array([slope(x) for x in range(8)])
    put("dcmp", np.where(d <= 0, d * sl[None, None, :, None], big))
    m = np.arange(64)
    d = np.concatenate([np.broadcast_to(np.arange(PAST) - PAST, (64, PAST)),
                        np.where(np.arange(B)[None] == m[:, None] // 8, 0.0, big)], 1)
    put("dsm", d * sl[m % 8][:, None])
    k = np.arange(128)
    d = np.where((k[None] // 16 == m[:, None] // 8) & (k[None] % 16 <= 14), 16 * (k[None] % 16) + 31 - PAST, big)
    put("dcs", d * sl[m % 8][:, None])
    put("sel8", (np.arange(8)[:, None] == m[None] // 8))
    put("pos8", (m[:, None] % 8 == np.arange(8)[None]))
    put("scanmask", np.broadcast_to(np.arange(T) % P != 0, (P, T)))
    return c


def _layout(v):
    import numpy as np
    v = {k: np.asarray(a) for k, a in v.items()}
    f = np.ascontiguousarray
    out = {}
    x = np.concatenate([v["x_prompt"][0], v["x_sample"][:, 0]], 0)
    out["x"] = f(x.T.reshape(KD, P, N).transpose(1, 0, 2))
    out["const"] = _constants()
    ups, downs = [], []
    for l in range(L):
        for s in ("ffn1", "ffn2"):
            w = v[s + "_w_gu"][l].reshape(KD, P, 2, FC, P)
            ups.append(w.transpose(3, 2, 1, 0, 4).reshape(2 * FC, P, KD * P))
            w = v[s + "_w_down"][l].reshape(FC, P, KD, P)
            downs.append(w.transpose(2, 1, 0, 3).reshape(KD, P, FC * P))
    out["w_up"], out["w_dn"] = f(np.stack(ups)), f(np.stack(downs))
    w = v["w_in"]
    q = w[:, :, 0:512].reshape(L, 1024, 2, 4, HD).transpose(0, 1, 3, 2, 4).reshape(L, 1024, 512)
    z = np.concatenate([q, w[:, :, 512:1280], w[:, :, 1304:2840], w[:, :, 2848:5408]], 2)
    out["w_z"] = f(z.reshape(L, KD, P, ZT, P).transpose(0, 3, 2, 1, 4).reshape(L, ZT, P, KD * P))
    g = w[:, :, 1280:1304].reshape(L, 1024, 2, 4, 3).transpose(0, 1, 4, 3, 2).reshape(L, 1024, 24)
    sm = np.concatenate([g, w[:, :, 2840:2848]], 2)
    out["w_sm"] = f(sm.reshape(L, KD, P, 32).transpose(0, 2, 1, 3).reshape(L, P, KD * 32))
    mg = w[:, :, 5408:].reshape(L, KD, P, 24, P).transpose(0, 3, 2, 1, 4)
    wb = v["w_branch"].reshape(L, 3, 512, 1024)
    wa = wb[:, 0].reshape(L, 2, 4, HD, 1024).transpose(0, 2, 1, 3, 4).reshape(L, 1, 512, 1024)
    wb = np.concatenate([wa, wb[:, 1:]], 1).reshape(L, 3, 4, P, KD, P).transpose(0, 1, 4, 3, 2, 5)
    out["w_mg"] = f(mg.reshape(L, 24, P, KD * P))
    out["w_wb"] = f(wb.reshape(L, 3, 4, 2, P, 4, P).transpose(0, 1, 2, 4, 3, 5, 6).reshape(L, 12, P, KD * P))
    out["w_out"] = f(v["w_out"].reshape(L, KD, P, KD, P).transpose(0, 3, 2, 1, 4).reshape(L, KD, P, KD * P))
    w1 = v["nsa_cmp_w1"].transpose(0, 1, 3, 2, 4).reshape(L, 2, HD, 32 * P)
    out["w1"] = f(np.concatenate([w1, w1], 2))
    vec = np.zeros((L, P, NVEC), np.float32)

    def put(name, a):
        o, n = VEC[name]
        vec[:, :, o:o + n] = a.reshape(L, P, n)

    for s, k in (("ffn1", "ffn1_norm"), ("mix", "mix_norm"), ("ffn2", "ffn2_norm")):
        put(s, v[k].reshape(L, KD, P).transpose(0, 2, 1))
    put("conv", v["dn_conv_w"].reshape(L, 4, 12, P).transpose(0, 3, 2, 1))
    put("qg", np.concatenate([v["nsa_q_norm"]] * 2, 1))
    put("kg", np.concatenate([v["nsa_k_norm"].transpose(0, 2, 1)] * 2, 1))
    put("dng", v["dn_out_norm"])
    put("hgg", v["hg_out_norm"])
    put("alog", np.broadcast_to(v["dn_A_log"][:, None], (L, P, 4)))
    put("dtb", np.broadcast_to(v["dn_dt_bias"][:, None], (L, P, 4)))
    pe = v["nsa_cmp_pe"].transpose(0, 3, 1, 2).reshape(L, HD, 64)
    put("pe", np.concatenate([pe, pe], 1))
    put("w2", v["nsa_cmp_w2"].transpose(0, 2, 1, 3))
    out["vec"] = vec
    out["lb"] = f(v["hg_lb_logits"].reshape(L, 4, P).transpose(2, 0, 1).reshape(P, 8))
    out["pages"] = f(v["page_table"].reshape(1, B * PAGES))
    c = v["cache_cmp_kv"]
    out["cmp_pages"] = f(c.transpose(0, 1, 4, 5, 3, 2).reshape(L * NPOOL, P, 2 * P))
    c = v["cache_slc_kv"]
    sk = c[:, :, :, 0].transpose(0, 1, 3, 4, 2).reshape(L * NPOOL, P, P)
    sv = c[:, :, :, 1].reshape(L * NPOOL, P, P)
    out["slc_pages"] = f(np.stack([sk, sv], 2).reshape(L * NPOOL, P, 2 * P))
    c = v["cache_win_kv"]
    out["win_k"] = f(c[:, :, :, 0].transpose(0, 3, 4, 1, 2).reshape(L, P, B * PAST))
    out["win_v"] = f(c[:, :, :, 1].reshape(L, B, PAGES, P, P).transpose(0, 3, 1, 2, 4).reshape(L, P, B * PAST))
    out["conv_in"] = f(v["state_dn_conv"].reshape(L, B, 3, 12, P).transpose(0, 4, 3, 1, 2).reshape(L, P, 12 * B * 3))
    for k in ("dn", "hg"):
        out[k + "_in"] = f(v[f"state_{k}_S"].transpose(0, 3, 2, 1, 4).reshape(L, P, 32 * P))
    return out


_OUTS = [("y", (P, KD * N)), ("kv", (L, P, 6 * N)), ("conv_p", (L, P, 12 * 3)), ("conv_s", (L, P, 12 * B * 3)),
         ("dn_p", (L, P, 4 * P)), ("dn_s", (L, P, 32 * P)), ("hg_p", (L, P, 4 * P)), ("hg_s", (L, P, 32 * P))]


def kernel(**inputs):
    import numpy as np
    import concourse.bacc as _bacc
    from concourse.bass_utils import run_bass_kernel_spmd as _run

    nc = _bacc.Bacc("TRN2", target_bir_lowering=False, num_devices=1)
    arrays, ins, outs = {}, {}, {}
    for name, a in _layout(inputs).items():
        arrays["in_" + name] = a
        ins[name] = nc.dram_tensor("in_" + name, a.shape, mybir.dt.from_np(a.dtype), kind="ExternalInput").ap()
    for name, shape in _OUTS:
        outs[name] = nc.dram_tensor("out_" + name, shape, F32, kind="ExternalOutput").ap()
    hybrid_step_kernel(nc, ins, outs)
    r = _run(nc, [arrays], core_ids=[0]).results[0]
    g = {name: np.asarray(r["out_" + name]) for name, _ in _OUTS}

    y = g["y"].reshape(P, KD, N).transpose(2, 1, 0).reshape(N, KD * P)
    kv = g["kv"].reshape(L, 2, HD, 3, 2, N).transpose(0, 3, 5, 4, 1, 2)
    kvp = [kv[:, i, :T].reshape(L, 1, T, 2, 2, HD) for i in range(3)]
    kvs = [kv[:, i, T:].reshape(L, B, 1, 2, 2, HD) for i in range(3)]
    conv_p = g["conv_p"].reshape(L, P, 12, 3).transpose(0, 3, 2, 1).reshape(L, 1, 3, 12 * P)
    conv_s = g["conv_s"].reshape(L, P, 12, B, 3).transpose(0, 3, 4, 2, 1).reshape(L, B, 3, 12 * P)
    res = [y[:T].reshape(1, T, KD * P), y[T:].reshape(B, 1, KD * P)]
    for i in range(3):
        res += [kvp[i], kvs[i]]
    res += [conv_p, conv_s]
    for k in ("dn", "hg"):
        res.append(g[k + "_p"].reshape(L, P, 4, P).transpose(0, 2, 1, 3).reshape(L, 1, 4, P, P))
        res.append(g[k + "_s"].reshape(L, P, 4, B, P).transpose(0, 3, 2, 1, 4).reshape(L, B, 4, P, P))
    return tuple(np.ascontiguousarray(a) for a in res)
```
